# Optimizing a Trainium2 kernel written in Bass

```python
import math
import jax, jax.numpy as jnp
from jax import lax
import numpy as np

D_MODEL = 1024
BATCH = 1
SEQ = 1024
DEPTH = 2

CHUNK = 64
N_MIXERS = 2
EPS = 1e-6

A_HEADS = 16
A_HEAD_DIM = 64
A_Q_RANK = 256
A_KV_RANK = 128
IDX_HEADS = 8
IDX_DIM = 64
TOPK_MAX = 256
Q_BLOCK = 128
A_PROJ = A_Q_RANK + A_KV_RANK + IDX_DIM + IDX_HEADS

B_HEAD = 64
B_HEADS = D_MODEL // B_HEAD
DECAY_RANK = 64
AAA_RANK = 64
GATE_RANK = 128
GN_EPS = 64e-5

D_FF = 2816
CONV_W = 3

N_A = (DEPTH + 1) // 2
N_B = DEPTH // 2

kernel_name = 'hybrid_dsa_rwkv7_convffn_adaln'

def rms_norm(x, g, eps=EPS):
    xf = x.astype(jnp.float32)
    y = xf * lax.rsqrt(jnp.mean(xf * xf, axis=-1, keepdims=True) + eps)
    return (y * g.astype(jnp.float32)).astype(x.dtype)

def layer_norm(x, g, b, eps=EPS):
    xf = x.astype(jnp.float32)
    mu = jnp.mean(xf, axis=-1, keepdims=True)
    var = jnp.mean(jnp.square(xf - mu), axis=-1, keepdims=True)
    y = (xf - mu) * lax.rsqrt(var + eps)
    return (y * g.astype(jnp.float32) + b.astype(jnp.float32)).astype(x.dtype)

def alibi_slopes(n):
    return jnp.power(2.0, -8.0 * jnp.arange(1, n + 1, dtype=jnp.float32) / n)

def dsa_mixer(h, w_in, q_norm, kv_norm, kidx_g, kidx_b, w_uq, w_qi, w_uk, w_uv, w_o):
    B, S, _ = h.shape
    proj = h @ w_in
    s1, s2, s3 = A_Q_RANK, A_Q_RANK + A_KV_RANK, A_Q_RANK + A_KV_RANK + IDX_DIM
    q_lat, c_kv, k_idx, w_idx = proj[..., :s1], proj[..., s1:s2], proj[..., s2:s3], proj[..., s3:]
    q_lat = rms_norm(q_lat, q_norm)
    c_kv = rms_norm(c_kv, kv_norm)
    k_idx = layer_norm(k_idx, kidx_g, kidx_b)
    q = (q_lat @ w_uq).reshape(B, S, A_HEADS, A_HEAD_DIM)
    q_abs = jnp.einsum('bshd,hcd->bshc', q, w_uk) * (A_HEAD_DIM ** -0.5)
    q_idx = (q_lat @ w_qi).reshape(B, S, IDX_HEADS, IDX_DIM)
    w_idx = w_idx * (IDX_HEADS ** -0.5 * IDX_DIM ** -0.5)

    k_top = min(TOPK_MAX, S // 4)
    key_chunk = jnp.arange(S) // CHUNK
    slopes = alibi_slopes(A_HEADS)
    nb = S // Q_BLOCK

    def to_blocks(t):
        return t.reshape(B, nb, Q_BLOCK, *t.shape[2:]).swapaxes(0, 1)

    def block(args):
        qa, qi, wi, start = args
        qpos = start + jnp.arange(Q_BLOCK)
        qchunk = qpos // CHUNK
        rel = jax.nn.relu(jnp.einsum('bqhd,bsd->bqhs', qi, k_idx))
        score = jnp.einsum('bqh,bqhs->bqs', wi, rel).astype(jnp.float32)
        admissible = key_chunk[None, :] <= qchunk[:, None]
        score = jnp.where(admissible[None], score, -jnp.inf)
        _, idx = lax.top_k(score, k_top)
        ckv_sel = jax.vmap(lambda cb, ib: cb[ib])(c_kv, idx)
        valid = (idx // CHUNK) <= qchunk[None, :, None]
        dist = jnp.abs(qpos[None, :, None] - idx).astype(jnp.float32)
        logits = jnp.einsum('bqhc,bqkc->bqhk', qa, ckv_sel).astype(jnp.float32)
        logits = logits - slopes[None, None, :, None] * dist[:, :, None, :]
        logits = jnp.where(valid[:, :, None, :], logits, -jnp.inf)
        p = jax.nn.softmax(logits, axis=-1).astype(ckv_sel.dtype)
        return jnp.einsum('bqhk,bqkc->bqhc', p, ckv_sel)

    starts = jnp.arange(nb) * Q_BLOCK
    o_lat = lax.map(block, (to_blocks(q_abs), to_blocks(q_idx), to_blocks(w_idx), starts))
    o_lat = o_lat.swapaxes(0, 1).reshape(B, S, A_HEADS, A_KV_RANK)
    o = jnp.einsum('bshc,hcd->bshd', o_lat, w_uv).reshape(B, S, A_HEADS * A_HEAD_DIM)
    return o @ w_o

def rwkv7_mixer(h, mu, w_r, w_k, w_v, w_o, w0, w1, w2, a0, a1, a2, g1, g2,
                k_k, k_a, r_k, gn_g, gn_b):
    B, S, D = h.shape
    H, N = B_HEADS, B_HEAD
    f32 = jnp.float32
    h_prev = jnp.pad(h, ((0, 0), (1, 0), (0, 0)))[:, :-1]
    dx = h_prev - h
    xr, xw, xk, xv, xa, xg = h + dx * mu[:, None, None, :]
    r = xr @ w_r
    k = xk @ w_k
    v = xv @ w_v
    w_log = -jax.nn.softplus(-(w0 + jnp.tanh(xw @ w1) @ w2)) - 0.5
    decay = jnp.exp(-jnp.exp(w_log.astype(f32)))
    a = jax.nn.sigmoid(a0 + (xa @ a1) @ a2)
    g = jax.nn.sigmoid(xg @ g1) @ g2
    kk = (k * k_k).reshape(B, S, H, N).astype(f32)
    kk = kk / jnp.maximum(jnp.sqrt(jnp.sum(kk * kk, axis=-1, keepdims=True)), 1e-12)
    k = k * (1 + (a - 1) * k_a)

    def seq_major(t):
        return t.reshape(B, S, H, N).transpose(1, 0, 2, 3).astype(f32)

    xs = (seq_major(r), seq_major(decay), seq_major(k), seq_major(v),
          kk.transpose(1, 0, 2, 3), seq_major(a))

    def step(state, inp):
        r_t, w_t, k_t, v_t, kk_t, a_t = inp
        sa = jnp.einsum('bhvk,bhk->bhv', state, -kk_t)
        state = (state * w_t[:, :, None, :]
                 + sa[..., None] * (kk_t * a_t)[:, :, None, :]
                 + v_t[..., None] * k_t[:, :, None, :])
        y = jnp.einsum('bhvk,bhk->bhv', state, r_t)
        return state, y

    state0 = jnp.zeros((B, H, N, N), f32)
    _, y = lax.scan(step, state0, xs)
    y = y.transpose(1, 0, 2, 3)
    mu_y = jnp.mean(y, axis=-1, keepdims=True)
    var_y = jnp.mean(jnp.square(y - mu_y), axis=-1, keepdims=True)
    y = (y - mu_y) * lax.rsqrt(var_y + GN_EPS)
    y = y * gn_g.reshape(H, N).astype(f32) + gn_b.reshape(H, N).astype(f32)
    rh, kh, vh = (t.reshape(B, S, H, N).astype(f32) for t in (r, k, v))
    y = y + jnp.sum(rh * kh * r_k.astype(f32), axis=-1, keepdims=True) * vh
    y = y.reshape(B, S, D).astype(h.dtype) * g
    return y @ w_o

def conv_ffn(h, w_up, conv_w, conv_b, w_down):
    u = h @ w_up
    c2 = u.shape[-1]
    u = lax.conv_general_dilated(u, conv_w[:, None, :].astype(u.dtype), window_strides=(1,),
                                 padding=[(CONV_W - 1, 0)],
                                 dimension_numbers=('NWC', 'WIO', 'NWC'),
                                 feature_group_count=c2) + conv_b
    ug, uv = u[..., :D_FF], u[..., D_FF:]
    return (jax.nn.silu(ug) * uv) @ w_down

def setup_inputs(seed: int = 0) -> dict:
    key = jax.random.key(seed)
    ks = iter(jax.random.split(key, 48))
    f32 = jnp.float32
    D = D_MODEL
    H, dh, C = A_HEADS, A_HEAD_DIM, A_KV_RANK

    def nrm(shape, scale):
        return jax.random.normal(next(ks), shape, f32) * scale

    def gain(shape):
        return 1.0 + nrm(shape, 0.05)

    return {
        'x': nrm((BATCH, SEQ, D), 1.0),
        'c': nrm((BATCH, D), 1.0),
        'ada_w': nrm((DEPTH, D, 6 * D), 0.5 * D ** -0.5),
        'ada_b': nrm((DEPTH, 6 * D), 0.02),
        'norm_mix': gain((DEPTH, D)),
        'norm_ffn': gain((DEPTH, D)),
        'norm_final': gain((D,)),
        'a_w_in': nrm((N_A, D, A_PROJ), D ** -0.5),
        'a_q_norm': gain((N_A, A_Q_RANK)),
        'a_kv_norm': gain((N_A, C)),
        'a_kidx_g': gain((N_A, IDX_DIM)),
        'a_kidx_b': nrm((N_A, IDX_DIM), 0.02),
        'a_w_uq': nrm((N_A, A_Q_RANK, H * dh), A_Q_RANK ** -0.5),
        'a_w_qi': nrm((N_A, A_Q_RANK, IDX_HEADS * IDX_DIM), A_Q_RANK ** -0.5),
        'a_w_uk': nrm((N_A, H, C, dh), C ** -0.5),
        'a_w_uv': nrm((N_A, H, C, dh), C ** -0.5),
        'a_w_o': nrm((N_A, H * dh, D), (H * dh) ** -0.5),
        'b_mu': jax.random.uniform(next(ks), (N_B, 6, D), f32),
        'b_w_r': nrm((N_B, D, D), D ** -0.5),
        'b_w_k': nrm((N_B, D, D), D ** -0.5),
        'b_w_v': nrm((N_B, D, D), D ** -0.5),
        'b_w_o': nrm((N_B, D, D), D ** -0.5),
        'b_w0': nrm((N_B, D), 0.5),
        'b_w1': nrm((N_B, D, DECAY_RANK), D ** -0.5),
        'b_w2': nrm((N_B, DECAY_RANK, D), 0.5 * DECAY_RANK ** -0.5),
        'b_a0': nrm((N_B, D), 0.1),
        'b_a1': nrm((N_B, D, AAA_RANK), D ** -0.5),
        'b_a2': nrm((N_B, AAA_RANK, D), 0.5 * AAA_RANK ** -0.5),
        'b_g1': nrm((N_B, D, GATE_RANK), D ** -0.5),
        'b_g2': nrm((N_B, GATE_RANK, D), GATE_RANK ** -0.5),
        'b_k_k': 0.85 + nrm((N_B, D), 0.05),
        'b_k_a': gain((N_B, D)),
        'b_r_k': nrm((N_B, B_HEADS, B_HEAD), 0.1),
        'b_gn_g': gain((N_B, D)),
        'b_gn_b': nrm((N_B, D), 0.02),
        'f_w_up': nrm((DEPTH, D, 2 * D_FF), D ** -0.5),
        'f_conv_w': nrm((DEPTH, CONV_W, 2 * D_FF), 0.6),
        'f_conv_b': nrm((DEPTH, 2 * D_FF), 0.02),
        'f_w_down': nrm((DEPTH, D_FF, D), D_FF ** -0.5),
    }

def reference(x, c, ada_w, ada_b, norm_mix, norm_ffn, norm_final,
              a_w_in, a_q_norm, a_kv_norm, a_kidx_g, a_kidx_b, a_w_uq, a_w_qi, a_w_uk, a_w_uv, a_w_o,
              b_mu, b_w_r, b_w_k, b_w_v, b_w_o, b_w0, b_w1, b_w2, b_a0, b_a1, b_a2, b_g1, b_g2,
              b_k_k, b_k_a, b_r_k, b_gn_g, b_gn_b,
              f_w_up, f_conv_w, f_conv_b, f_w_down):
    h = x
    c_act = jax.nn.silu(c)
    for i in range(DEPTH):
        mod = (c_act @ ada_w[i] + ada_b[i])[:, None, :]
        sh_m, sc_m, g_m, sh_f, sc_f, g_f = jnp.split(mod, 6, axis=-1)
        hn = rms_norm(h, norm_mix[i]) * (1 + sc_m) + sh_m
        j = i // N_MIXERS
        if i % N_MIXERS == 0:
            y = dsa_mixer(hn, a_w_in[j], a_q_norm[j], a_kv_norm[j], a_kidx_g[j], a_kidx_b[j],
                          a_w_uq[j], a_w_qi[j], a_w_uk[j], a_w_uv[j], a_w_o[j])
        else:
            y = rwkv7_mixer(hn, b_mu[j], b_w_r[j], b_w_k[j], b_w_v[j], b_w_o[j],
                            b_w0[j], b_w1[j], b_w2[j], b_a0[j], b_a1[j], b_a2[j],
                            b_g1[j], b_g2[j], b_k_k[j], b_k_a[j], b_r_k[j], b_gn_g[j], b_gn_b[j])
        h = h + g_m * y
        hn = rms_norm(h, norm_ffn[i]) * (1 + sc_f) + sh_f
        h = h + g_f * conv_ffn(hn, f_w_up[i], f_conv_w[i], f_conv_b[i], f_w_down[i])
    return rms_norm(h, norm_final)


_drawn_inputs = setup_inputs


def setup_inputs(seed=0):
    import zlib

    import numpy as np

    out = dict(_drawn_inputs(seed))
    spreads = {}
    factors = {'a_q_norm': 2.908,
     'a_kv_norm': 6.264,
     'a_kidx_b': 5.265,
     'b_w1': 4.368,
     'b_w2': 4.084,
     'b_a0': 5.909,
     'b_k_k': 200.0,
     'b_k_a': 5.175,
     'b_gn_g': 27.645,
     'b_gn_b': 38.073,
     'f_conv_b': 6.689,
     'norm_ffn': 4.375}
    for name, (base, spread) in spreads.items():
        noise = np.random.default_rng([zlib.crc32(name.encode()), seed]).standard_normal(out[name].shape)
        drawn = base * np.exp(spread * noise) if base else spread * noise
        out[name] = __import__('jax').numpy.asarray(drawn.astype(out[name].dtype))
    for name, factor in factors.items():
        out[name] = (out[name] * factor).astype(out[name].dtype)
    return out
```

```python
from collections import namedtuple
from contextlib import ExitStack

import concourse.bass as bass
from concourse import mybir

F32 = mybir.dt.float32
F32R = mybir.dt.float32r
U8 = mybir.dt.uint8
ACT = mybir.ActivationFunctionType
ALU = mybir.AluOpType
AX_X = mybir.AxisListType.X

P = 128
S = 1024
D = 1024
KT = D // P
TT = S // P
HALF = 512
NH = S // HALF
CHUNK = 64
EPS = 1e-6
GN_EPS = 64e-5

A_HEADS, A_DH = 16, 64
Q_RANK, KV_RANK = 256, 128
IDX_HEADS, IDX_DIM = 8, 64
TOPK = 256
A_PROJ = Q_RANK + KV_RANK + IDX_DIM + IDX_HEADS

D_FF = 2816
FT = D_FF // P
CONV_W = 3
FF_PARTS = (6, 6, 6, 4)

UNSELECTED = 1e30
INADMISSIBLE = -2e38
TAKEN = -3e38

PARAM_ROWS = [
    [("c", KT), ("ada_b", 96), ("norm_mix", 16)],
    [("norm_ffn", 16), ("norm_final", 8), ("b_mu", 48), ("b_w0", 8), ("b_a0", 8), ("b_k_k", 8),
     ("b_k_a", 8), ("b_r_k", 8), ("b_gn_b", 8)],
    [("f_conv_b", 88), ("a_q_norm", 2), ("a_kv_norm", 1), ("kidx_g", 1), ("kidx_b", 1)],
    [("f_conv_w0", 128)],
    [("f_conv_w1", 128)],
    [("f_conv_w2", 8)],
]


def param_columns():
    col, at, rows = {}, 0, []
    for tile in PARAM_ROWS:
        here = 0
        for name, n in tile:
            col[name] = at + here
            here += n
        rows.append((at, here))
        at += here
    return col, rows, at


PCOL, PTILES, NPCOL = param_columns()


class Kern:
    pass


def alloc(k, stack):
    nc = k.nc
    k.sb = lambda name, shape, dt=F32: stack.enter_context(nc.sbuf_tensor(name, shape, dt))
    k.sem = lambda name: stack.enter_context(nc.semaphore(name))
    k.h = k.sb("h", [P, KT, S])
    k.ident = k.sb("ident", [P, P])
    k.ones = k.sb("ones", [P, 2])
    k.pc = k.sb("pc", [P, NPCOL])
    k.mod = k.sb("mod", [P, 96])
    k.scl = k.sb("scl", [P, 4 * KT])
    k.ps = [stack.enter_context(nc.psum_tensor(f"ps{i}", [P, S], F32)) for i in range(4)]
    k.w_raw = [k.sb(f"w_raw{i}", [P, KT, P]) for i in range(2)]
    k.w_hi = [k.sb(f"w_hi{i}", [P, KT, P], F32R) for i in range(2)]
    k.w_lo = [k.sb(f"w_lo{i}", [P, KT, P], F32R) for i in range(2)]
    k.w_landed = [k.sem(f"w_landed{i}") for i in range(2)]
    k.w_hi_done = k.sem("w_hi_done")
    k.w_split = k.sem("w_split")
    k.w_used = k.sem("w_used")
    k.stage_done = k.sem("stage_done")
    k.stages = 0
    k.blocks = 0
    k.landed = [0, 0]
    k.parts = {"pe": [], "act": [], "dve": [], "pool": [], "sp": []}
    k.norms = k.norm_lo = k.norm_hi = 0
    k.nm = {n: k.sem("nm_" + n) for n in
            ("scale", "sq", "sum", "ms", "root", "rinv", "bcast", "t", "hi", "lo")}


def mod_col(layer, which, t=0):
    return layer * 48 + which * KT + t


def stage_end(k):
    k.stages += 1
    n = 3 * k.stages
    for name in ("pe", "act", "dve"):
        def barrier(eng, n=n):
            eng.drain().then_inc(k.stage_done, 1)
            eng.wait_ge(k.stage_done, n)
        k.parts[name].append(barrier)
    return n


def passes3(pe, out, w_hi, w_lo, x_hi, x_lo, first, last):
    pe.matmul(out, w_hi, x_hi, start=first, stop=False)
    pe.matmul(out, w_hi, x_lo, start=False, stop=False)
    return pe.matmul(out, w_lo, x_hi, start=False, stop=last)


def stream_weights(k, count, source, kts=KT):
    b0, landed0 = k.blocks, list(k.landed)
    pairs = count // 2

    def load(sp, i):
        for s in range(2):
            sp.wait_ge(k.w_split, b0 + 2 * i + s + 1)
            sp.dma_start(k.w_raw[s][:, 0:kts, :], source(i, s)).then_inc(k.w_landed[s], 16)

    def split(pool, i):
        for s in range(2):
            b = b0 + 2 * i + s
            pool.wait_ge(k.w_landed[s], landed0[s] + 16 * i + 16)
            pool.wait_ge(k.w_used, b + 1)
            one = k.ones[:, 0:1].unsqueeze(2).to_broadcast([P, kts, P])
            pool.tensor_tensor(k.w_hi[s][:, 0:kts, :], k.w_raw[s][:, 0:kts, :], one, ALU.mult
                               ).then_inc(k.w_hi_done, 1)
            pool.wait_ge(k.w_hi_done, b + 1)
            pool.tensor_tensor(k.w_lo[s][:, 0:kts, :], k.w_raw[s][:, 0:kts, :],
                               k.w_hi[s][:, 0:kts, :].bitcast(F32), ALU.subtract).then_inc(k.w_split, 1)

    def sp_part(sp):
        with sp.Fori(0, pairs) as i:
            load(sp, i)

    def pool_part(pool):
        with pool.Fori(0, pairs) as i:
            split(pool, i)

    k.parts["sp"].append(sp_part)
    k.parts["pool"].append(pool_part)
    k.blocks += count
    for s in range(2):
        k.landed[s] += 16 * pairs
    return b0


def stream_pieces(k, blocks):
    b0, landed = k.blocks, list(k.landed)
    waits = []
    for n, pieces in enumerate(blocks):
        landed[n % 2] += 16 * len(pieces)
        waits.append(landed[n % 2])

    def sp_part(sp):
        for n, pieces in enumerate(blocks):
            sp.wait_ge(k.w_split, b0 + n + 1)
            for c0, c1, src in pieces:
                sp.dma_start(k.w_raw[n % 2][:, :, c0:c1], src).then_inc(k.w_landed[n % 2], 16)

    def pool_part(pool):
        for n in range(len(blocks)):
            pool.wait_ge(k.w_landed[n % 2], waits[n])
            pool.wait_ge(k.w_used, b0 + n + 1)
            raw = k.w_raw[n % 2][:, :, :]
            one = k.ones[:, 0:1].unsqueeze(2).to_broadcast([P, KT, P])
            pool.tensor_tensor(k.w_hi[n % 2][:, :, :], raw, one, ALU.mult).then_inc(k.w_hi_done, 1)
            pool.wait_ge(k.w_hi_done, b0 + n + 1)
            pool.tensor_tensor(k.w_lo[n % 2][:, :, :], raw, k.w_hi[n % 2][:, :, :].bitcast(F32), ALU.subtract
                               ).then_inc(k.w_split, 1)

    k.parts["sp"].append(sp_part)
    k.parts["pool"].append(pool_part)
    k.blocks += len(blocks)
    k.landed = landed
    return b0


def block_done(k, eng, b):
    eng.wait_ge(k.w_used, b + 3)


def wait_split(k, pe, b):
    pe.wait_ge(k.w_split, b + 3)


def setup_stage(k, a):
    nc = k.nc
    RING = 8
    with ExitStack() as st:
        sb = lambda name, shape, dt=F32: st.enter_context(nc.sbuf_tensor(name, shape, dt))
        xin = sb("xin", [P, TT, D])
        prow = sb("prow", [P, len(PTILES), P])
        cact = sb("cact", [P, KT])
        ada_w = [sb(f"ada_w{i}", [P, D]) for i in range(RING)]
        ada_acc = sb("ada_acc", [P, D])
    const_ready = k.sem("const_ready")
    prow_landed = k.sem("prow_landed")
    x_landed = [k.sem(f"x_landed{i}") for i in range(2)]
    par_t = k.sem("par_t")
    par_done = k.sem("par_done")
    x_t = k.sem("x_t")
    x_act = k.sem("x_act")
    x_dve = k.sem("x_dve")
    c_act = k.sem("c_act")
    ada_landed = [k.sem(f"ada_landed{i}") for i in range(RING)]
    ada_acc_done = k.sem("ada_acc_done")
    ada_pe = k.sem("ada_pe")
    ada_mod = k.sem("ada_mod")

    srcs = {
        "c": a.c.rearrange("b (t p) -> (b t) p", p=P),
        "ada_b": a.ada_b.rearrange("l (t p) -> (l t) p", p=P),
        "norm_mix": a.norm_mix.rearrange("l (t p) -> (l t) p", p=P),
        "norm_ffn": a.norm_ffn.rearrange("l (t p) -> (l t) p", p=P),
        "norm_final": a.norm_final.rearrange("(t p) -> t p", p=P),
        "b_mu": a.b_mu.rearrange("l m (t p) -> (l m t) p", p=P),
        "b_w0": a.b_w0.rearrange("l (t p) -> (l t) p", p=P),
        "b_a0": a.b_a0.rearrange("l (t p) -> (l t) p", p=P),
        "b_k_k": a.b_k_k.rearrange("l (t p) -> (l t) p", p=P),
        "b_k_a": a.b_k_a.rearrange("l (t p) -> (l t) p", p=P),
        "b_r_k": a.b_r_k.rearrange("l (t h) n -> (l t) (h n)", h=2),
        "b_gn_b": a.b_gn_b.rearrange("l (t p) -> (l t) p", p=P),
        "f_conv_b": a.f_conv_b.rearrange("l (t p) -> (l t) p", p=P),
        "a_q_norm": a.a_q_norm.rearrange("l (t p) -> (l t) p", p=P),
        "a_kv_norm": a.a_kv_norm.rearrange("l (t p) -> (l t) p", p=P),
    }
    conv_rows = a.f_conv_w.rearrange("l w (t p) -> (l w t) p", p=P)

    def sp_part(sp):
        n = 0
        for i, tile in enumerate(PARAM_ROWS):
            at = 0
            for name, rows in tile:
                if name.startswith("f_conv_w"):
                    r0 = P * int(name[-1])
                    sp.dma_start(prow[0:rows, i, :], conv_rows[r0:r0 + rows, :]).then_inc(prow_landed, 16)
                    n += 1
                elif name.startswith("kidx"):
                    src = a.a_kidx_g if name == "kidx_g" else a.a_kidx_b
                    for half in range(2):
                        sp.dma_start(prow[at:at + 1, i, half * 64:half * 64 + 64], src).then_inc(prow_landed, 16)
                        n += 1
                else:
                    sp.dma_start(prow[at:at + rows, i, :], srcs[name]).then_inc(prow_landed, 16)
                    n += 1
                at += rows
        assert n == k.n_param_dmas
        for t in range(TT):
            sp.dma_start(xin[:, t, :], a.x[0, t * P:(t + 1) * P, :]).then_inc(x_landed[t // 4], 16)
        for layer in range(2):
            with sp.Fori(0, 6) as w:
                for kt in range(KT):
                    sp.wait_ge(ada_acc_done, (layer * 6 + w) * KT + kt + 1)
                    sp.dma_start(ada_w[kt][:, :], a.ada_w[layer, kt * P:(kt + 1) * P, bass.ds(w * D, D)]
                                 ).then_inc(ada_landed[kt], 16)

    k.n_param_dmas = sum(2 if n.startswith("kidx") else 1 for tile in PARAM_ROWS for n, _ in tile)

    def pool_part(pool):
        pool.sem_inc(k.w_split, 2)
        pool.memset(k.ident[:, :], 0.0).then_inc(const_ready, 1)
        pool.memset(k.ones[:, :], 1.0).then_inc(const_ready, 1)
        pool.wait_ge(const_ready, 2)
        pool.affine_select(out=k.ident[:, :], in_=k.ident[:, :], compare_op=ALU.not_equal, fill=1.0, base=0,
                           pattern=[[-1, P]], channel_multiplier=1).then_inc(const_ready, 1)

    def pe_part(pe):
        pe.sem_inc(k.w_used, 2)
        pe.sem_inc(ada_pe, 1)
        pe.wait_ge(const_ready, 3)
        pe.wait_ge(prow_landed, 16 * k.n_param_dmas)
        for i, (at, rows) in enumerate(PTILES):
            last = pe.transpose(k.ps[0][:, i * P:i * P + rows], prow[0:rows, i, :], k.ident[0:rows, 0:rows])
        last.then_inc(par_t, 1)
        pe.wait_ge(x_landed[0], 64)
        pe.wait_ge(x_landed[1], 64)
        for g in range(2 * KT):
            kt, half, bank = g // 2, g % 2, g % 6
            if g >= 6:
                pe.wait_ge(x_act if g % 2 == 0 else x_dve, (g - 6) // 2 + 1)
            out = k.ps[1 + bank // 2][:, (bank % 2) * HALF:(bank % 2 + 1) * HALF]
            for q in range(4):
                t = 4 * half + q
                last = pe.transpose(out[:, q * P:(q + 1) * P], xin[:, t, kt * P:(kt + 1) * P], k.ident[:, :])
            last.then_inc(x_t, 1)
        pe.wait_ge(par_done, len(PTILES))
        with pe.Fori(0, 12) as job:
            pe.wait_ge(ada_acc_done, KT + KT * job + KT)
            for m in range(KT):
                last = pe.matmul(k.ps[0][:, m:m + 1], ada_acc[:, m * P:(m + 1) * P], k.ones[:, 0:1],
                                 start=True, stop=True)
            last.then_inc(ada_pe, 1)

    def act_part(act):
        act.wait_ge(par_done, 1)
        act.activation(cact[:, :], k.pc[:, PCOL["c"]:PCOL["c"] + KT], ACT.Silu).then_inc(c_act, 1)
        for g in range(0, 2 * KT, 2):
            bank = g % 6
            act.wait_ge(x_t, g + 1)
            act.activation(k.h[:, g // 2, 0:HALF], k.ps[1 + bank // 2][:, (bank % 2) * HALF:(bank % 2 + 1) * HALF],
                           ACT.Copy).then_inc(x_act, 1)

    def dve_part(dve):
        dve.wait_ge(par_t, 1)
        for i, (at, rows) in enumerate(PTILES):
            dve.tensor_copy(k.pc[:, at:at + rows], k.ps[0][:, i * P:i * P + rows]).then_inc(par_done, 1)
        for g in range(1, 2 * KT, 2):
            bank = g % 6
            dve.wait_ge(x_t, g + 1)
            dve.tensor_copy(k.h[:, g // 2, HALF:S], k.ps[1 + bank // 2][:, (bank % 2) * HALF:(bank % 2 + 1) * HALF]
                            ).then_inc(x_dve, 1)
        dve.wait_ge(par_done, len(PTILES))
        dve.sem_inc(ada_acc_done, KT)
        dve.wait_ge(c_act, 1)
        with dve.Fori(0, 12) as job:
            dve.wait_ge(ada_pe, job + 1)
            for kt in range(KT):
                dve.wait_ge(ada_landed[kt], 16 * job + 16)
                if kt == 0:
                    dve.tensor_scalar(ada_acc[:, :], ada_w[0][:, :], cact[:, 0:1], None, ALU.mult
                                      ).then_inc(ada_acc_done, 1)
                else:
                    dve.wait_ge(ada_acc_done, KT + KT * job + kt)
                    dve.scalar_tensor_tensor(out=ada_acc[:, :], in0=ada_w[kt][:, :], scalar=cact[:, kt:kt + 1],
                                             in1=ada_acc[:, :], op0=ALU.mult, op1=ALU.add
                                             ).then_inc(ada_acc_done, 1)
            dve.wait_ge(ada_pe, job + 2)
            dve.tensor_tensor(k.mod[:, bass.ds(job * KT, KT)], k.ps[0][:, 0:KT],
                              k.pc[:, bass.ds(job * KT + PCOL["ada_b"], KT)], ALU.add).then_inc(ada_mod, 1)

    for name, part in (("sp", sp_part), ("pool", pool_part), ("pe", pe_part), ("act", act_part), ("dve", dve_part)):
        k.parts[name].append(part)
    k.ada_mod = ada_mod
    k.const_ready = const_ready


def norm_stage(k, gain, layer=None, which=None, hi=None, lo=None, plain=None):
    n = k.norms
    k.norms += 1
    nm = k.nm
    lo0, hi0 = k.norm_lo, k.norm_hi
    k.norm_lo += KT if hi is not None else 0
    k.norm_hi += KT if layer is not None else 0
    with ExitStack() as st:
        sq = [st.enter_context(k.nc.sbuf_tensor(f"nm_sq{n}_{i}", [P, S], F32)) for i in range(2)]
        t = [st.enter_context(k.nc.sbuf_tensor(f"nm_t{n}_{i}", [P, S], F32)) for i in range(2)]
        small = st.enter_context(k.nc.sbuf_tensor(f"nm_small{n}", [P, 3, TT], F32))
    ms, root, rinv = small[:, 0, :], small[:, 1, :], small[:, 2, :]
    sums, bcast = k.ps[0], k.ps[1]
    modulated = layer is not None
    scale = k.scl[:, 8 * (n % 4):8 * (n % 4) + 8] if modulated else k.pc[:, gain:gain + KT]
    split = hi is not None

    def shift(kt):
        c = mod_col(layer, which, kt)
        return k.mod[:, c:c + 1]

    def act_part(act):
        for kt in range(KT):
            if kt >= 2:
                act.wait_ge(nm["sum"], 8 * n + kt - 1)
            act.activation(sq[kt % 2][:, :], k.h[:, kt, :], ACT.Square).then_inc(nm["sq"], 1)
        act.wait_ge(nm["ms"], n + 1)
        act.activation(root, ms, ACT.Sqrt).then_inc(nm["root"], 1)
        if modulated:
            for kt in range(KT):
                act.wait_ge(nm["t"], 8 * n + kt + 1)
                out = hi[:, kt, :] if split else plain(kt)
                act.activation(out, t[kt % 2][:, :], ACT.Identity, bias=shift(kt)).then_inc(nm["hi"], 1)

    def pe_part(pe):
        for kt in range(KT):
            pe.wait_ge(nm["sq"], 8 * n + kt + 1)
            for tt in range(TT):
                last = pe.matmul(sums[:, tt:tt + 1], sq[kt % 2][:, tt * P:(tt + 1) * P], k.ones[:, 0:1],
                                 start=(kt == 0 and tt == 0), stop=(kt == KT - 1), skip_group_check=True)
            last.then_inc(nm["sum"], 1)
        pe.wait_ge(nm["rinv"], n + 1)
        for tt in range(TT):
            last = pe.transpose(bcast[:, tt * P:(tt + 1) * P], rinv[:, tt:tt + 1].to_broadcast([P, P]), k.ident[:, :])
        last.then_inc(nm["bcast"], 1)

    def dve_part(dve):
        if modulated:
            c = mod_col(layer, which + 1)
            dve.tensor_scalar(scale, k.mod[:, c:c + KT], 1.0, None, ALU.add).then_inc(nm["scale"], 1)
            dve.wait_ge(nm["scale"], 2 * n + 1)
            dve.tensor_tensor(scale, scale, k.pc[:, gain:gain + KT], ALU.mult).then_inc(nm["scale"], 1)
        dve.wait_ge(nm["sum"], 8 * n + 8)
        dve.tensor_scalar(ms, sums[:, 0:TT], 1.0 / D, EPS, ALU.mult, ALU.add).then_inc(nm["ms"], 1)
        dve.wait_ge(nm["root"], n + 1)
        dve.reciprocal(rinv, root).then_inc(nm["rinv"], 1)
        dve.wait_ge(nm["bcast"], n + 1)
        if modulated:
            dve.wait_ge(nm["scale"], 2 * n + 2)

        def low(kt):
            dve.wait_ge(nm["hi"], hi0 + kt + 1)
            dve.scalar_tensor_tensor(out=lo[:, kt, :], in0=t[kt % 2][:, :], scalar=shift(kt),
                                     in1=hi[:, kt, :].bitcast(F32), op0=ALU.add, op1=ALU.subtract
                                     ).then_inc(nm["lo"], 1)

        for kt in range(KT):
            if modulated and not split and kt >= 2:
                dve.wait_ge(nm["hi"], hi0 + kt - 1)
            if split and kt >= 2:
                dve.wait_ge(nm["lo"], lo0 + kt - 1)
            out = t[kt % 2][:, :] if modulated else plain(kt)
            dve.scalar_tensor_tensor(out=out, in0=k.h[:, kt, :], scalar=scale[:, kt:kt + 1], in1=bcast[:, :],
                                     op0=ALU.mult, op1=ALU.mult).then_inc(nm["t"], 1)
            if split and kt >= 1:
                low(kt - 1)
        if split:
            low(KT - 1)

    for name, part in (("pe", pe_part), ("act", act_part), ("dve", dve_part)):
        k.parts[name].append(part)
    return lo0


def ffn_stage(k, a, layer):
    nc = k.nc
    if layer == 0:
        k.ffn = {n: k.sem("ffn_" + n) for n in
                 ("zero", "u_copy", "u_lin", "tap", "silu", "gated", "g_hi", "g_free", "resid")}
    f = k.ffn
    with ExitStack() as st:
        sb = lambda name, shape, dt=F32: st.enter_context(nc.sbuf_tensor(f"{name}_{layer}", shape, dt))
        hn_hi, hn_lo = sb("hn_hi", [P, KT, S], F32R), sb("hn_lo", [P, KT, S], F32R)
        norm0 = norm_stage(k, PCOL["norm_ffn"] + layer * KT, layer, 3, hn_hi, hn_lo)
        g_hi = sb("g_hi", [P, FF_PARTS[0], S], F32R)
        g_lo = sb("g_lo", [P, FF_PARTS[0], S], F32R)
        u = [sb(f"u{i}", [P, S + 2]) for i in range(2)]
        c = [sb(f"uc{i}", [P, S]) for i in range(2)]
        sg = sb("sg", [P, S])
    w_up = a.f_w_up[layer].rearrange("(k p) n -> p k n", p=P)
    w_down = a.f_w_down[layer].rearrange("(k p) n -> p k n", p=P)
    bcol = PCOL["f_conv_b"] + 2 * FT * layer
    wcol = PCOL["f_conv_w0"] + CONV_W * 2 * FT * layer

    def dve_start(dve):
        dve.wait_ge(k.nm["lo"], norm0 + KT)
        for i in range(2):
            dve.memset(u[i][:, 0:2], 0.0).then_inc(f["zero"], 1)
        if layer == 0:
            dve.sem_inc(f["resid"], 2)
            dve.sem_inc(f["g_free"], 1)

    def act_start(act):
        if layer == 0:
            act.sem_inc(f["u_lin"], 4)
        act.wait_ge(f["zero"], 2 * layer + 2)
    k.parts["dve"].append(dve_start)
    k.parts["act"].append(act_start)
    k.parts["pe"].append(lambda pe: pe.wait_ge(k.nm["lo"], norm0 + KT))

    t0 = 0
    for part, nt in enumerate(FF_PARTS):
        b_up = stream_weights(k, 2 * nt, lambda i, s, t0=t0: w_up[:, :, bass.ds(i * P + (t0 * P + s * D_FF), P)])
        b_down = stream_weights(k, KT, lambda i, s, t0=t0, nt=nt: w_down[:, t0:t0 + nt, bass.ds(i * (2 * P) + s * P, P)],
                                kts=nt)
        ffn_part(k, f, layer, t0, nt, b_up, b_down, FT * layer + t0, KT * (len(FF_PARTS) * layer + part),
                 hn_hi, hn_lo, g_hi, g_lo, u, c, sg, bcol, wcol)
        t0 += nt
    stage_end(k)


def ffn_part(k, f, layer, t0, nt, b_up, b_down, g0, o0, hn_hi, hn_lo, g_hi, g_lo, u, c, sg, bcol, wcol):

    def pe_part(pe):
        pe.wait_ge(f["resid"], 2 + o0)
        with pe.Fori(0, nt // 2) as i:
            for s in range(2):
                for wi in range(2):
                    pe.wait_ge(f["u_lin"], i * 4 + (2 * g0 + 2 * s + wi + 1))
                    wait_split(k, pe, i * 4 + (b_up + 2 * s + wi))
                    for n in range(NH):
                        cols = slice(n * HALF, (n + 1) * HALF)
                        for kt in range(KT):
                            last = passes3(pe, k.ps[2 * s + wi][:, cols], k.w_hi[wi][:, kt, :], k.w_lo[wi][:, kt, :],
                                           hn_hi[:, kt, cols], hn_lo[:, kt, cols], kt == 0, kt == KT - 1)
                    last.then_inc(k.w_used, 1)
        pe.wait_ge(f["u_lin"], 4 + 2 * (g0 + nt - 1))
        pe.wait_ge(f["g_free"], g0 + nt + 1)
        with pe.Fori(0, KT // 2) as i:
            for s in range(2):
                pe.wait_ge(f["resid"], i * 2 + (o0 + s + 1))
                wait_split(k, pe, i * 2 + (b_down + s))
                for n in range(NH):
                    cols = slice(n * HALF, (n + 1) * HALF)
                    for kt in range(nt):
                        last = passes3(pe, k.ps[s][:, cols], k.w_hi[s][:, kt, :], k.w_lo[s][:, kt, :],
                                       g_hi[:, kt, cols], g_lo[:, kt, cols], kt == 0, kt == nt - 1)
                last.then_inc(k.w_used, 1)

    def act_part(act):
        with act.Fori(0, nt // 2) as i:
            for s in range(2):
                for wi in range(2):
                    block_done(k, act, i * 4 + (b_up + 2 * s + wi))
                    act.wait_ge(f["g_free"], i * 2 + (g0 + s + 1))
                    act.activation(u[wi][:, 2:S + 2], k.ps[2 * s + wi][:, :], ACT.Copy).then_inc(f["u_copy"], 1)
                    act.activation(c[wi][:, :], k.ps[2 * s + wi][:, :], ACT.Identity,
                                   bias=k.pc[:, bass.ds(i * 2 + (t0 + s + bcol + wi * FT), 1)],
                                   scale=k.pc[:, bass.ds(i * 2 + (t0 + s + wcol + 4 * FT + wi * FT), 1)]
                                   ).then_inc(f["u_lin"], 1)
                act.wait_ge(f["tap"], i * 8 + (4 * (g0 + s) + 2))
                act.activation(sg[:, :], c[0][:, :], ACT.Silu).then_inc(f["silu"], 1)
                act.wait_ge(f["gated"], i * 2 + (g0 + s + 1))
                act.activation(g_hi[:, bass.ds(i * 2 + s, 1), :], c[1][:, :].unsqueeze(1), ACT.Copy
                               ).then_inc(f["g_hi"], 1)

    def dve_part(dve):
        with dve.Fori(0, nt // 2) as i:
            for s in range(2):
                for wi in range(2):
                    dve.wait_ge(f["u_lin"], i * 4 + (4 + 2 * (g0 + s) + wi + 1))
                    for tap in (1, 0):
                        if tap == 0:
                            dve.wait_ge(f["tap"], i * 8 + (4 * (g0 + s) + 2 * wi + 1))
                        dve.scalar_tensor_tensor(
                            out=c[wi][:, :], in0=u[wi][:, tap:tap + S],
                            scalar=k.pc[:, bass.ds(i * 2 + (t0 + s + wcol + 2 * FT * tap + wi * FT), 1)],
                            in1=c[wi][:, :], op0=ALU.mult, op1=ALU.add).then_inc(f["tap"], 1)
                dve.wait_ge(f["silu"], i * 2 + (g0 + s + 1))
                dve.wait_ge(f["tap"], i * 8 + (4 * (g0 + s) + 4))
                dve.tensor_tensor(c[1][:, :], c[1][:, :], sg[:, :], ALU.mult).then_inc(f["gated"], 1)
                dve.wait_ge(f["g_hi"], i * 2 + (g0 + s + 1))
                dve.tensor_tensor(g_lo[:, bass.ds(i * 2 + s, 1), :], c[1][:, :].unsqueeze(1),
                                  g_hi[:, bass.ds(i * 2 + s, 1), :].bitcast(F32), ALU.subtract
                                  ).then_inc(f["g_free"], 1)
        with dve.Fori(0, KT // 2) as i:
            for s in range(2):
                block_done(k, dve, i * 2 + (b_down + s))
                hm = k.h[:, bass.ds(i * 2 + s, 1), :]
                gate = k.mod[:, bass.ds(i * 2 + (s + mod_col(layer, 5)), 1)]
                dve.scalar_tensor_tensor(out=hm, in0=k.ps[s][:, :].unsqueeze(1), scalar=gate, in1=hm,
                                         op0=ALU.mult, op1=ALU.add).then_inc(f["resid"], 1)

    k.parts["pe"].append(pe_part)
    k.parts["act"].append(act_part)
    k.parts["dve"].append(dve_part)


def split_tiles(k, name, src, hi, lo):
    hi_done, lo_done = k.sem(name + "_hi_done"), k.sem(name + "_lo_done")

    def act_part(act):
        for kt in range(KT):
            act.activation(hi[:, kt, :], src[:, kt, :], ACT.Copy).then_inc(hi_done, 1)

    def dve_part(dve):
        for kt in range(KT):
            dve.wait_ge(hi_done, kt + 1)
            dve.tensor_tensor(lo[:, kt, :], src[:, kt, :], hi[:, kt, :].bitcast(F32), ALU.subtract
                              ).then_inc(lo_done, 1)

    k.parts["act"].append(act_part)
    k.parts["dve"].append(dve_part)
    return lo_done


def project_residual(k, name, w, x_hi, x_lo, x_ready, gate_col):
    b0 = stream_weights(k, KT, lambda i, s: w[:, :, bass.ds(i * (2 * P) + s * P, P)])
    resid = k.sem(name + "_resid")

    def pe_part(pe):
        pe.wait_ge(x_ready, KT)
        with pe.Fori(0, KT // 2) as i:
            for s in range(2):
                pe.wait_ge(resid, i * 2 + (s + 1))
                wait_split(k, pe, i * 2 + (b0 + s))
                for n in range(NH):
                    cols = slice(n * HALF, (n + 1) * HALF)
                    for kt in range(KT):
                        last = passes3(pe, k.ps[s][:, cols], k.w_hi[s][:, kt, :], k.w_lo[s][:, kt, :],
                                       x_hi[:, kt, cols], x_lo[:, kt, cols], kt == 0, kt == KT - 1)
                last.then_inc(k.w_used, 1)

    def dve_part(dve):
        dve.sem_inc(resid, 2)
        with dve.Fori(0, KT // 2) as i:
            for s in range(2):
                block_done(k, dve, i * 2 + (b0 + s))
                hm = k.h[:, bass.ds(i * 2 + s, 1), :]
                dve.scalar_tensor_tensor(out=hm, in0=k.ps[s][:, :].unsqueeze(1),
                                         scalar=k.mod[:, bass.ds(i * 2 + (s + gate_col), 1)], in1=hm,
                                         op0=ALU.mult, op1=ALU.add).then_inc(resid, 1)

    k.parts["pe"].append(pe_part)
    k.parts["dve"].append(dve_part)


def dsa_stage(k, a):
    nc = k.nc
    perm, early, scratch = ExitStack(), ExitStack(), ExitStack()
    sb = lambda st, name, shape, dt=F32: st.enter_context(nc.sbuf_tensor("d_" + name, shape, dt))
    before = 3 * k.stages
    q_lat = sb(perm, "q_lat", [P, 2, S])
    ckv_t = sb(perm, "ckv_t", [P, S])
    ckv_n = sb(perm, "ckv_n", [P, TT, P])
    kidx = sb(perm, "kidx", [P, S])
    w_uq = sb(perm, "w_uq", [P, 2, A_HEADS * A_DH])
    w_qi = sb(perm, "w_qi", [P, 2, IDX_HEADS * IDX_DIM])
    w_uk_t = sb(perm, "w_uk_t", [P, A_HEADS // 2, P])
    w_uv = sb(perm, "w_uv", [P, A_HEADS, A_DH])
    w_ix = sb(perm, "w_ix", [P, KT, IDX_HEADS])
    w_ix_hi = sb(perm, "w_ix_hi", [P, KT, IDX_HEADS], F32R)
    w_ix_lo = sb(perm, "w_ix_lo", [P, KT, IDX_HEADS], F32R)
    wi = sb(perm, "wi", [P, TT, IDX_HEADS])
    stat = sb(perm, "stat", [P, 4, 4 * TT])
    small = sb(perm, "small", [P, 4, A_HEADS])
    top8 = sb(perm, "top8", [P, 8])
    hn_hi, hn_lo = sb(early, "hn_hi", [P, KT, S], F32R), sb(early, "hn_lo", [P, KT, S], F32R)
    norm0 = norm_stage(k, PCOL["norm_mix"], 0, 0, hn_hi, hn_lo)
    w_in = a.a_w_in[0].rearrange("(k p) n -> p k n", p=P)
    c2 = Q_RANK + KV_RANK
    b0 = stream_pieces(k, [[(0, P, w_in[:, :, 0:P])], [(0, P, w_in[:, :, P:2 * P])],
                           [(0, P, w_in[:, :, Q_RANK:c2])],
                           [(0, 64, w_in[:, :, c2:c2 + IDX_DIM]), (64, P, w_in[:, :, c2:c2 + IDX_DIM])]])
    early.close()
    sq = sb(early, "sq", [P, 3, S])
    w_uk = sb(early, "w_uk", [P, A_HEADS, A_DH])
    early.close()
    o_t = sb(perm, "o_t", [P, KT, S])
    q_t = sb(scratch, "q_t", [P, A_HEADS // 2, P])
    qi_t = sb(scratch, "qi_t", [P, IDX_HEADS // 2, P])
    q_abs = sb(scratch, "q_abs", [P, 2, A_HEADS // 2, P])
    work = [sb(scratch, f"work{i}", [P, S]) for i in range(2)]
    dist = [sb(scratch, f"dist{i}", [P, S]) for i in range(2)]
    rel = [sb(scratch, f"rel{i}", [P, S]) for i in range(2)]
    x = [sb(scratch, f"x{i}", [P, S]) for i in range(3)]
    p_t = [sb(scratch, f"p_t{i}", [P, TT, P]) for i in range(2)]
    o_lat = [sb(scratch, f"o_lat{i}", [P, P]) for i in range(2)]
    scratch.close()
    o_hi, o_lo = sb(scratch, "o_hi", [P, KT, S], F32R), sb(scratch, "o_lo", [P, KT, S], F32R)
    scratch.close()
    perm.close()

    sems = ExitStack()
    sem = {n: sems.enter_context(nc.semaphore("d_" + n)) for n in (
        "w_landed",
        "evac",
        "wi_split",
        "wi_ps",
        "wi_done",
        "sq",
        "sum", "ms", "root", "rinv", "bcast", "cent",
        "sq2", "sum2", "ms2", "root2", "rinv2", "bcast2", "kidx",
        "lat",
        "ckv_ps", "uk_ps", "ckv_n", "uk_t",
        "qT_ps", "qT_sb", "qi_ps", "qi_sb", "qa_ps", "qa_sb",
        "sc_ps", "relu", "acc", "iota", "dist", "mask", "top", "take",
        "qk_ps", "x_max", "nbias", "x_exp", "rinv_h", "x_norm", "p_ps", "p_sb", "ol_ps", "ol_sb", "o_ps", "o_sb",
        "mask_d", "unsel")}

    def slope(h):
        return 2.0 ** (-8.0 * (h + 1) / A_HEADS)

    def keys(s):
        return (s + 1) * P

    INDEXED = range(TOPK // P, TT)

    def sp_part(sp):
        sp.wait_ge(k.stage_done, before)
        for dst, src in ((w_uq[:, :, :], a.a_w_uq[0].rearrange("(t p) n -> p t n", p=P)),
                         (w_qi[:, :, :], a.a_w_qi[0].rearrange("(t p) n -> p t n", p=P)),
                         (w_uv[:, :, :], a.a_w_uv[0].rearrange("h c d -> c h d")),
                         (w_ix[:, :, :], w_in[:, :, c2 + IDX_DIM:A_PROJ])):
            sp.dma_start(dst, src).then_inc(sem["w_landed"], 16)
        sp.wait_ge(sem["wi_ps"], 1)
        sp.dma_start(w_uk[:, :, :], a.a_w_uk[0].rearrange("h c d -> c h d")).then_inc(sem["w_landed"], 16)

    def pe_prep(pe):
        pe.wait_ge(k.nm["lo"], norm0 + KT)
        for m in range(4):
            wait_split(k, pe, b0 + m)
            for n in range(NH):
                cols = slice(n * HALF, (n + 1) * HALF)
                for kt in range(KT):
                    last = passes3(pe, k.ps[m][:, cols], k.w_hi[m % 2][:, kt, :], k.w_lo[m % 2][:, kt, :],
                                   hn_hi[:, kt, cols], hn_lo[:, kt, cols], kt == 0, kt == KT - 1)
            last.then_inc(k.w_used, 1)
        pe.wait_ge(sem["wi_split"], 2)
        pe.wait_ge(sem["evac"], 1)
        for tt in range(TT):
            toks = slice(tt * P, (tt + 1) * P)
            for kt in range(KT):
                last = passes3(pe, k.ps[0][:, tt * 8:tt * 8 + 8], hn_hi[:, kt, toks], hn_lo[:, kt, toks],
                               w_ix_hi[:, kt, :], w_ix_lo[:, kt, :], kt == 0, kt == KT - 1)
        last.then_inc(sem["wi_ps"], 1)
        pe.wait_ge(sem["sq"], 3)
        pe.wait_ge(sem["evac"], 4)
        for tt in range(TT):
            toks = slice(tt * P, (tt + 1) * P)
            for m in range(2):
                pe.matmul(k.ps[1][:, tt:tt + 1], sq[:, m, toks], k.ones[:, 0:1], start=m == 0, stop=m == 1)
            pe.matmul(k.ps[1][:, TT + tt:TT + tt + 1], sq[:, 2, toks], k.ones[:, 0:1], start=True, stop=True)
            last = pe.matmul(k.ps[1][:, 2 * TT + tt:2 * TT + tt + 1], kidx[:, toks], k.ones[:, 0:1],
                             start=True, stop=True)
        last.then_inc(sem["sum"], 1)
        pe.wait_ge(sem["rinv"], 1)
        pe.wait_ge(sem["wi_done"], 1)
        for j, dst in ((2, k.ps[0]), (0, k.ps[2]), (1, k.ps[3])):
            for tt in range(TT):
                last = pe.transpose(dst[:, tt * P:(tt + 1) * P],
                                    stat[:, 2, j * TT + tt:j * TT + tt + 1].to_broadcast([P, P]), k.ident[:, :])
            last.then_inc(sem["bcast"], 1)
        pe.wait_ge(sem["sq2"], 1)
        for tt in range(TT):
            last = pe.matmul(k.ps[1][:, tt:tt + 1], sq[:, 0, tt * P:(tt + 1) * P], k.ones[:, 0:1],
                             start=True, stop=True)
        last.then_inc(sem["sum2"], 1)
        pe.wait_ge(sem["rinv2"], 1)
        for tt in range(TT):
            last = pe.transpose(k.ps[1][:, tt * P:(tt + 1) * P],
                                stat[:, 2, 3 * TT + tt:3 * TT + tt + 1].to_broadcast([P, P]), k.ident[:, :])
        last.then_inc(sem["bcast2"], 1)
        pe.wait_ge(sem["lat"], 3)
        for tt in range(TT):
            last = pe.transpose(k.ps[2][:, tt * P:(tt + 1) * P], ckv_t[:, tt * P:(tt + 1) * P], k.ident[:, :])
        last.then_inc(sem["ckv_ps"], 1)
        pe.wait_ge(sem["w_landed"], 16 * 5)
        for m in range(A_HEADS // 2):
            last = pe.transpose(k.ps[3][:, m * P:(m + 1) * P],
                                w_uk[:, 2 * m:2 * m + 2, :].rearrange("p h d -> p (h d)"), k.ident[:, :])
        last.then_inc(sem["uk_ps"], 1)

    def act_prep(act):
        for m, dst in enumerate((q_lat[:, 0, :], q_lat[:, 1, :], ckv_t[:, :], kidx[:, :])):
            block_done(k, act, b0 + m)
            act.activation(dst, k.ps[m][:, :], ACT.Copy).then_inc(sem["evac"], 1)
        act.wait_ge(sem["wi_ps"], 1)
        act.wait_ge(sem["evac"], 3)
        for m, src in enumerate((q_lat[:, 0, :], q_lat[:, 1, :], ckv_t[:, :])):
            act.activation(sq[:, m, :], src, ACT.Square).then_inc(sem["sq"], 1)
        act.wait_ge(sem["ms"], 3)
        act.activation(stat[:, 1, 0:2 * TT], stat[:, 0, 0:2 * TT], ACT.Sqrt).then_inc(sem["root"], 1)
        act.wait_ge(sem["cent"], 1)
        act.wait_ge(sem["sum"], 1)
        act.activation(sq[:, 0, :], kidx[:, :], ACT.Square).then_inc(sem["sq2"], 1)
        act.wait_ge(sem["ms2"], 1)
        act.activation(stat[:, 1, 3 * TT:4 * TT], stat[:, 0, 3 * TT:4 * TT], ACT.Sqrt).then_inc(sem["root2"], 1)
        act.wait_ge(sem["ckv_ps"], 1)
        act.activation(ckv_n[:, :, :].rearrange("p t c -> p (t c)"), k.ps[2][:, :], ACT.Copy).then_inc(sem["ckv_n"], 1)
        act.wait_ge(sem["uk_ps"], 1)
        for h in range(A_HEADS):
            m, half = h // 2, slice(64 * (h % 2), 64 * (h % 2) + 64)
            act.activation(w_uk_t[half, m, :], k.ps[3][half, m * P:(m + 1) * P], ACT.Copy,
                           scale=A_DH ** -0.5 / slope(h)).then_inc(sem["uk_t"], 1)

    def dve_prep(dve):
        dve.wait_ge(sem["w_landed"], 16 * 4)
        dve.tensor_copy(w_ix_hi[:, :, :], w_ix[:, :, :]).then_inc(sem["wi_split"], 1)
        dve.wait_ge(sem["wi_split"], 1)
        dve.tensor_tensor(w_ix_lo[:, :, :], w_ix[:, :, :], w_ix_hi[:, :, :].bitcast(F32), ALU.subtract
                          ).then_inc(sem["wi_split"], 1)
        dve.wait_ge(sem["wi_ps"], 1)
        dve.tensor_scalar(wi[:, :, :].rearrange("p t h -> p (t h)"), k.ps[0][:, 0:64],
                          IDX_HEADS ** -0.5 * IDX_DIM ** -0.5, None, ALU.mult).then_inc(sem["wi_done"], 1)
        dve.wait_ge(sem["sum"], 1)
        dve.tensor_scalar(stat[:, 0, 0:TT], k.ps[1][:, 0:TT], 1.0 / Q_RANK, EPS, ALU.mult, ALU.add
                          ).then_inc(sem["ms"], 1)
        dve.tensor_scalar(stat[:, 0, TT:2 * TT], k.ps[1][:, TT:2 * TT], 1.0 / KV_RANK, EPS, ALU.mult, ALU.add
                          ).then_inc(sem["ms"], 1)
        dve.tensor_scalar(stat[:, 2, 2 * TT:3 * TT], k.ps[1][:, 2 * TT:3 * TT], 1.0 / (2 * IDX_DIM), None, ALU.mult
                          ).then_inc(sem["ms"], 1)
        dve.wait_ge(sem["root"], 1)
        dve.reciprocal(stat[:, 2, 0:2 * TT], stat[:, 1, 0:2 * TT]).then_inc(sem["rinv"], 1)
        dve.wait_ge(sem["bcast"], 1)
        dve.tensor_tensor(kidx[:, :], kidx[:, :], k.ps[0][:, :], ALU.subtract).then_inc(sem["cent"], 1)
        for m, (dst, gain) in enumerate(((q_lat[:, 0, :], PCOL["a_q_norm"]), (q_lat[:, 1, :], PCOL["a_q_norm"] + 1),
                                         (ckv_t[:, :], PCOL["a_kv_norm"]))):
            dve.wait_ge(sem["bcast"], 2 if m < 2 else 3)
            dve.scalar_tensor_tensor(out=dst, in0=dst, scalar=k.pc[:, gain:gain + 1],
                                     in1=k.ps[2 if m < 2 else 3][:, :], op0=ALU.mult, op1=ALU.mult
                                     ).then_inc(sem["lat"], 1)
        dve.wait_ge(sem["sum2"], 1)
        dve.tensor_scalar(stat[:, 0, 3 * TT:4 * TT], k.ps[1][:, 0:TT], 1.0 / (2 * IDX_DIM), EPS, ALU.mult, ALU.add
                          ).then_inc(sem["ms2"], 1)
        dve.wait_ge(sem["root2"], 1)
        dve.reciprocal(stat[:, 2, 3 * TT:4 * TT], stat[:, 1, 3 * TT:4 * TT]).then_inc(sem["rinv2"], 1)
        dve.wait_ge(sem["bcast2"], 1)
        dve.scalar_tensor_tensor(out=kidx[:, :], in0=kidx[:, :], scalar=k.pc[:, PCOL["kidx_g"]:PCOL["kidx_g"] + 1],
                                 in1=k.ps[1][:, :], op0=ALU.mult, op1=ALU.mult).then_inc(sem["kidx"], 1)
        dve.wait_ge(sem["kidx"], 1)
        dve.tensor_scalar(kidx[:, :], kidx[:, :], k.pc[:, PCOL["kidx_b"]:PCOL["kidx_b"] + 1], None, ALU.add
                          ).then_inc(sem["kidx"], 1)

    k.parts["sp"].append(sp_part)
    k.parts["pe"].append(pe_prep)
    k.parts["act"].append(act_prep)
    k.parts["dve"].append(dve_prep)
    stage_end(k)
    prep_done = 3 * k.stages

    def pe_step(pe, s):
        n, qs = keys(s), slice(s * P, (s + 1) * P)
        if s:
            pe.wait_ge(sem["x_max"], 16 * s)
            pe.wait_ge(sem["p_sb"], 16 * s)
            pe.wait_ge(sem["ol_sb"], 16 * s)
            pe.wait_ge(sem["o_sb"], 8 * s)
        for m in range(A_HEADS // 2):
            for t in range(2):
                last = pe.matmul(k.ps[0][:, m * P:(m + 1) * P], w_uq[:, t, m * P:(m + 1) * P], q_lat[:, t, qs],
                                 start=t == 0, stop=t == 1)
        last.then_inc(sem["qT_ps"], 1)
        indexed = s + 2 in INDEXED
        if indexed:
            qs2 = slice((s + 2) * P, (s + 3) * P)
            for m in range(IDX_HEADS // 2):
                for t in range(2):
                    last = pe.matmul(k.ps[1][:, m * P:(m + 1) * P], w_qi[:, t, m * P:(m + 1) * P],
                                     q_lat[:, t, qs2], start=t == 0, stop=t == 1)
            last.then_inc(sem["qi_ps"], 1)
        pe.wait_ge(sem["qT_sb"], s + 1)
        for parity in range(2):
            half = slice(64 * parity, 64 * parity + 64)
            for m in range(A_HEADS // 2):
                last = pe.matmul(k.ps[2 + parity][:, m * P:(m + 1) * P], w_uk_t[half, m, :], q_t[half, m, :],
                                 start=True, stop=True)
            last.then_inc(sem["qa_ps"], 1)
        if indexed:
            pe.wait_ge(sem["qi_sb"], s + 1)
            n2 = keys(s + 2)
            for j in range(IDX_HEADS):
                if j >= 2:
                    pe.wait_ge(sem["relu"], 8 * s + j - 1)
                half = slice(64 * (j % 2), 64 * (j % 2) + 64)
                for c in range(0, n2, HALF):
                    e = min(c + HALF, n2)
                    last = pe.matmul(k.ps[j % 2][:, c:e], qi_t[half, j // 2, :], kidx[half, c:e],
                                     start=True, stop=True)
                last.then_inc(sem["sc_ps"], 1)
            pe.wait_ge(sem["relu"], 8 * s + 8)
        for i in range(A_HEADS + 4):
            if i < A_HEADS:
                A = 16 * s + i
                if i >= 2:
                    pe.wait_ge(sem["x_max"], A - 1)
                pe.wait_ge(sem["qa_sb"], 2 * s + (1 if i == 0 else 2))
                for c in range(0, n, HALF):
                    e = min(c + HALF, n)
                    last = pe.matmul(k.ps[i % 2][:, c:e], q_abs[:, i % 2, i // 2, :], ckv_t[:, c:e], start=True, stop=True)
                last.then_inc(sem["qk_ps"], 1)
            if 0 <= i - 3 < A_HEADS:
                A = 16 * s + i - 3
                pe.wait_ge(sem["p_sb"], A + 1)
                if A:
                    pe.wait_ge(sem["ol_sb"], A)
                else:
                    pe.wait_ge(sem["qa_sb"], 2)
                for kt in range(s + 1):
                    last = pe.matmul(k.ps[3][:, 0:P], ckv_n[:, kt, :], p_t[A % 2][:, kt, :],
                                     start=kt == 0, stop=kt == s)
                last.then_inc(sem["ol_ps"], 1)
            if 0 <= i - 2 < A_HEADS:
                A = 16 * s + i - 2
                pe.wait_ge(sem["x_norm"], A + 1)
                pe.wait_ge(sem["qa_sb"], 2 * s + 2)
                if A:
                    pe.wait_ge(sem["p_sb"], A)
                for kt in range(s + 1):
                    last = pe.transpose(k.ps[2][:, kt * P:(kt + 1) * P], x[A % 3][:, kt * P:(kt + 1) * P],
                                        k.ident[:, :])
                last.then_inc(sem["p_ps"], 1)
            if 0 <= i - 4 < A_HEADS:
                h = i - 4
                A = 16 * s + h
                pe.wait_ge(sem["ol_sb"], A + 1)
                if h % 2 == 0 and A:
                    pe.wait_ge(sem["o_sb"], A // 2)
                pe.matmul(k.ps[3][64 * (h % 2):64 * (h % 2) + 64, HALF:HALF + P], w_uv[:, h, :],
                          o_lat[A % 2][:, :], start=True, stop=True).then_inc(sem["o_ps"], 1)

    def act_step(act, s):
        n = keys(s)
        act.wait_ge(sem["qT_ps"], s + 1)
        act.activation(q_t[:, :, :].rearrange("p m q -> p (m q)"), k.ps[0][:, :], ACT.Copy).then_inc(sem["qT_sb"], 1)
        indexed = s + 2 in INDEXED
        if indexed:
            act.wait_ge(sem["qi_ps"], s + 1)
            act.activation(qi_t[:, :, :].rearrange("p m q -> p (m q)"), k.ps[1][:, 0:HALF], ACT.Copy
                           ).then_inc(sem["qi_sb"], 1)
        for half in range(2):
            act.wait_ge(sem["qa_ps"], 2 * s + 1 + half)
            act.activation(q_abs[:, half, :, :].rearrange("p h q -> p (h q)"), k.ps[2 + half][:, :],
                           ACT.Copy).then_inc(sem["qa_sb"], 1)
        if s + 1 < TT:
            act.wait_ge(sem["iota"], s + 2)
            act.activation(dist[(s + 1) % 2][:, 0:keys(s + 1)], dist[(s + 1) % 2][:, 0:keys(s + 1)], ACT.Abs
                           ).then_inc(sem["dist"], 1)
        if indexed:
            n2 = keys(s + 2)
            for j in range(IDX_HEADS):
                act.wait_ge(sem["sc_ps"], 8 * s + j + 1)
                if 8 * s + j >= 2:
                    act.wait_ge(sem["acc"], 8 * s + j - 1)
                act.activation(rel[j % 2][:, 0:n2], k.ps[j % 2][:, 0:n2], ACT.Relu).then_inc(sem["relu"], 1)
        for i in range(A_HEADS + 4):
            if i < A_HEADS:
                A = 16 * s + i
                act.wait_ge(sem["x_max"], A + 1)
                act.activation(small[:, 1, i:i + 1], small[:, 0, i:i + 1], ACT.Copy, scale=-slope(i)
                               ).then_inc(sem["nbias"], 1)
                act.wait_ge(sem["nbias"], A + 1)
                act.activation(x[A % 3][:, 0:n], x[A % 3][:, 0:n], ACT.Exp, bias=small[:, 1, i:i + 1], scale=slope(i),
                               accum_out=small[:, 2, i:i + 1]).then_inc(sem["x_exp"], 1)
            if 0 <= i - 2 < A_HEADS:
                A = 16 * s + i - 2
                act.wait_ge(sem["p_ps"], A + 1)
                if A >= 2:
                    act.wait_ge(sem["ol_ps"], A - 1)
                act.activation(p_t[A % 2][:, 0:s + 1, :].rearrange("p t q -> p (t q)"), k.ps[2][:, 0:n], ACT.Copy
                               ).then_inc(sem["p_sb"], 1)
            if 0 <= i - 3 < A_HEADS:
                A = 16 * s + i - 3
                act.wait_ge(sem["ol_ps"], A + 1)
                if A >= 2:
                    act.wait_ge(sem["o_ps"], A - 1)
                act.activation(o_lat[A % 2][:, :], k.ps[3][:, 0:P], ACT.Copy).then_inc(sem["ol_sb"], 1)
            if 0 <= i - 4 < A_HEADS and i % 2 == 1:
                h = i - 4
                act.wait_ge(sem["o_ps"], 16 * s + h + 1)
                act.activation(o_t[:, h // 2, s * P:(s + 1) * P], k.ps[3][:, HALF:HALF + P], ACT.Copy
                               ).then_inc(sem["o_sb"], 1)

    def dve_step(dve, s):
        n, n1 = keys(s), keys(s + 1)
        if s + 2 in INDEXED:
            n2 = keys(s + 2)
            w = work[s % 2][:, 0:n2]
            dve.wait_ge(sem["mask_d"], s + 1)
            for j in range(IDX_HEADS):
                dve.wait_ge(sem["relu"], 8 * s + j + 1)
                col = wi[:, s + 2, j:j + 1]
                if j == 0:
                    dve.tensor_scalar(w, rel[0][:, 0:n2], col, None, ALU.mult).then_inc(sem["acc"], 1)
                else:
                    dve.wait_ge(sem["acc"], 8 * s + j)
                    dve.scalar_tensor_tensor(out=w, in0=rel[j % 2][:, 0:n2], scalar=col, in1=w,
                                             op0=ALU.mult, op1=ALU.add).then_inc(sem["acc"], 1)
            dve.wait_ge(sem["acc"], 8 * s + 8)
            dve.memset(work[s % 2][0:CHUNK, n2 - CHUNK:n2], INADMISSIBLE).then_inc(sem["mask"], 1)
        searching = s + 1 in INDEXED
        w1 = work[(s + 1) % 2][:, 0:n1] if searching else None
        if searching:
            dve.wait_ge(sem["mask"], s)
            t0 = (TOPK // 8) * (s + 1 - TOPK // P)
        for i in range(A_HEADS):
            A = 16 * s + i
            dve.wait_ge(sem["qk_ps"], A + 1)
            if A >= 3:
                dve.wait_ge(sem["p_ps"], A - 2)
            if i == 0:
                dve.wait_ge(sem["dist"], s + 1)
                dve.wait_ge(sem["mask_d"], s + 1)
            dve.tensor_tensor_reduce(x[A % 3][:, 0:n], k.ps[i % 2][:, 0:n], dist[s % 2][:, 0:n], 1.0, TAKEN,
                                     ALU.subtract, ALU.max, small[:, 0, i:i + 1]).then_inc(sem["x_max"], 1)
            if searching:
                for r in range(2 * i, 2 * i + 2):
                    if t0 + r:
                        dve.wait_ge(sem["take"], t0 + r)
                    dve.max(top8[:, :], w1).then_inc(sem["top"], 1)
                    dve.wait_ge(sem["top"], t0 + r + 1)
                    dve.match_replace(w1, top8[:, :], w1, TAKEN).then_inc(sem["take"], 1)
            if i >= 1:
                dve.wait_ge(sem["x_exp"], A)
                dve.reciprocal(small[:, 3, i - 1:i], small[:, 2, i - 1:i]).then_inc(sem["rinv_h"], 1)
        dve.wait_ge(sem["x_exp"], 16 * s + 16)
        dve.reciprocal(small[:, 3, 15:16], small[:, 2, 15:16]).then_inc(sem["rinv_h"], 1)
        if s + 1 < TT:
            finish_dist(dve, s + 1)

    def finish_dist(dve, s):
        n, d = keys(s), dist[s % 2]
        dve.wait_ge(sem["dist"], s + 1)
        if s in INDEXED:
            w = work[s % 2][:, 0:n]
            dve.wait_ge(sem["take"], (TOPK // 8) * (s + 1 - TOPK // P))
            dve.tensor_scalar(w, w, (INADMISSIBLE + TAKEN) / 2, UNSELECTED, ALU.is_gt, ALU.mult
                              ).then_inc(sem["unsel"], 1)
            dve.wait_ge(sem["unsel"], s + 1 - TOPK // P)
            dve.tensor_tensor(d[:, 0:n], d[:, 0:n], w, ALU.add).then_inc(sem["mask_d"], 1)
        else:
            dve.memset(d[0:CHUNK, n - CHUNK:n], UNSELECTED).then_inc(sem["mask_d"], 1)


    def pool_step(pool, s):
        if s + 1 < TT:
            if s:
                pool.wait_ge(sem["x_max"], 16 * s)
            pool.iota(dist[(s + 1) % 2][:, 0:keys(s + 1)], [[-1, keys(s + 1)]], base=(s + 1) * P,
                      channel_multiplier=1, allow_small_or_imprecise_dtypes=True).then_inc(sem["iota"], 1)
        for i in range(A_HEADS):
            A = 16 * s + i
            pool.wait_ge(sem["rinv_h"], A + 1)
            pool.tensor_scalar(x[A % 3][:, 0:keys(s)], x[A % 3][:, 0:keys(s)], small[:, 3, i:i + 1], None, ALU.mult
                               ).then_inc(sem["x_norm"], 1)

    def pool_attention(pool):
        pool.wait_ge(k.stage_done, prep_done)
        pool.iota(dist[0][:, 0:P], [[-1, P]], base=0, channel_multiplier=1,
                  allow_small_or_imprecise_dtypes=True).then_inc(sem["iota"], 1)
        for s in range(TT):
            pool_step(pool, s)

    def act_attention(act):
        act.wait_ge(sem["iota"], 1)
        act.activation(dist[0][:, 0:P], dist[0][:, 0:P], ACT.Abs).then_inc(sem["dist"], 1)
        for s in range(TT):
            act_step(act, s)

    def dve_attention(dve):
        finish_dist(dve, 0)
        for s in range(TT):
            dve_step(dve, s)

    def pe_attention(pe):
        for s in range(TT):
            pe_step(pe, s)

    k.parts["pool"].append(pool_attention)
    k.parts["pe"].append(pe_attention)
    k.parts["act"].append(act_attention)
    k.parts["dve"].append(dve_attention)
    stage_end(k)

    def clear(dve):
        for s in sem.values():
            dve.sem_clear(s)

    k.parts["dve"].append(clear)
    lo_done = split_tiles(k, "d_o", o_t, o_hi, o_lo)
    project_residual(k, "d", a.a_w_o[0].rearrange("(k p) n -> p k n", p=P), o_hi, o_lo, lo_done, mod_col(0, 2))
    stage_end(k)
    sems.close()


DECAY_C = 0.6065306597126334
PAIRS = KT
R_, K_, V_, W_, A_, G_ = range(6)


def rwkv_project(k, a, scr):
    nc = k.nc
    st = ExitStack()
    sb = lambda name, shape, dt=F32: st.enter_context(nc.sbuf_tensor("rp_" + name, shape, dt))
    sem = {n: k.sem("rp_" + n) for n in ("zero", "omu", "t", "x", "hi", "lo", "hid", "gh_lo", "ev", "w2", "sec")}
    stored = [k.sem(f"rp_stored{i}") for i in range(2)]
    before = 3 * k.stages
    hn = sb("hn", [P, KT, S + 1])
    omu = sb("omu", [P, 48])
    wa2 = sb("wa2", [P, D])
    wa_h = sb("wa_h", [P, S])
    stage = [sb(f"stage{i}", [P, S]) for i in range(2)]
    norm_stage(k, PCOL["norm_mix"] + KT, 1, 0, plain=lambda kt: hn[:, kt, 1:S + 1])
    hi0 = k.norm_hi
    x_hi, x_lo = sb("x_hi", [P, KT, S], F32R), sb("x_lo", [P, KT, S], F32R)
    t = sb("t", [P, S])
    x = sb("x", [P, S])
    g_hi, g_lo = sb("g_hi", [P, S], F32R), sb("g_lo", [P, S], F32R)
    st.close()

    def sp_part(sp):
        sp.wait_ge(k.stage_done, before)
        sp.dma_start(wa2[0:64, :], a.b_w2[0]).then_inc(sem["w2"], 16)
        sp.dma_start(wa2[64:P, :], a.b_a2[0]).then_inc(sem["w2"], 16)

    k.parts["sp"].append(sp_part)
    v = lambda w: w[0].rearrange("(k p) n -> p k n", p=P)
    b0 = stream_pieces(k, [[(0, 64, v(a.b_w1)), (64, P, v(a.b_w1))], [(0, 64, v(a.b_a1)), (64, P, v(a.b_a1))],
                           [(0, P, v(a.b_g1))], [(0, P, a.b_g2[0].rearrange("p (m n) -> p m n", n=P))]])
    big = []
    for w in (a.b_w_r, a.b_w_k, a.b_w_v):
        big.append(stream_weights(k, KT, lambda i, s, w=w: v(w)[:, :, bass.ds(i * (2 * P) + s * P, P)]))
    mixes = [(1, None), (4, b0), (5, b0 + 1), (0, b0 + 2), (2, big[0] + KT - 1), (3, big[1] + KT - 1)]

    def x_act(act, j):
        mu, prev = mixes[j]
        for kt in range(KT):
            n = KT * j + kt
            if n:
                act.wait_ge(sem["x"], n)
            act.activation(t[:, :], hn[:, kt, 1:S + 1], ACT.Copy, scale=omu[:, mu * 8 + kt:mu * 8 + kt + 1]
                           ).then_inc(sem["t"], 1)
            act.wait_ge(sem["x"], n + 1)
            if kt == 0 and prev is not None:
                block_done(k, act, prev)
            act.activation(x_hi[:, kt, :], x[:, :], ACT.Copy).then_inc(sem["hi"], 1)

    def x_dve(dve, j):
        mu, _ = mixes[j]
        for kt in range(KT):
            n = KT * j + kt
            dve.wait_ge(sem["t"], n + 1)
            if n:
                dve.wait_ge(sem["lo"], n)
            col = PCOL["b_mu"] + mu * 8 + kt
            dve.scalar_tensor_tensor(out=x[:, :], in0=hn[:, kt, 0:S], scalar=k.pc[:, col:col + 1], in1=t[:, :],
                                     op0=ALU.mult, op1=ALU.add).then_inc(sem["x"], 1)
            dve.wait_ge(sem["hi"], n + 1)
            dve.tensor_tensor(x_lo[:, kt, :], x[:, :], x_hi[:, kt, :].bitcast(F32), ALU.subtract
                              ).then_inc(sem["lo"], 1)

    def product(pe, out, slot, j):
        for n in range(NH):
            cols = slice(n * HALF, (n + 1) * HALF)
            for kt in range(KT):
                pe.wait_ge(sem["lo"], KT * j + kt + 1)
                last = passes3(pe, out[:, cols], k.w_hi[slot][:, kt, :], k.w_lo[slot][:, kt, :],
                               x_hi[:, kt, cols], x_lo[:, kt, cols], kt == 0, kt == KT - 1)
        return last

    def pe_part(pe):
        for j in range(3):
            wait_split(k, pe, b0 + j)
            if j == 2:
                pe.wait_ge(sem["hid"], 1)
            product(pe, k.ps[2 + j % 2], j % 2, j).then_inc(k.w_used, 1)
        for o in range(2 * KT):
            half, m = slice(64 * (o // KT), 64 * (o // KT) + 64), o % KT
            if o == 0:
                pe.wait_ge(sem["hid"], 2)
                pe.wait_ge(sem["w2"], 32)
            pe.wait_ge(sem["ev"], o + 1)
            for n in range(NH):
                cols = slice(n * HALF, (n + 1) * HALF)
                last = pe.matmul(k.ps[o % 2][:, cols], wa2[half, m * P:(m + 1) * P], wa_h[half, cols],
                                 start=True, stop=True)
            last.then_inc(sem["sec"], 1)
        pe.wait_ge(sem["gh_lo"], 1)
        wait_split(k, pe, b0 + 3)
        for m in range(KT):
            o = 2 * KT + m
            pe.wait_ge(sem["ev"], o + 1)
            for n in range(NH):
                cols = slice(n * HALF, (n + 1) * HALF)
                last = passes3(pe, k.ps[o % 2][:, cols], k.w_hi[1][:, m, :], k.w_lo[1][:, m, :],
                               g_hi[:, cols], g_lo[:, cols], True, True)
            last.then_inc(sem["sec"], 1)
        pe.wait_ge(sem["ev"], 3 * KT + 2)
        pe.sem_inc(k.w_used, 1)
        for j, bb in enumerate(big):
            with pe.Fori(0, KT // 2) as i:
                for s in range(2):
                    pe.wait_ge(sem["ev"], i * 2 + (3 * KT + KT * j + s + 1))
                    wait_split(k, pe, i * 2 + (bb + s))
                    product(pe, k.ps[s], s, 3 + j).then_inc(k.w_used, 1)

    def act_part(act):
        act.sem_inc(sem["ev"], 2)
        for i in range(2):
            act.sem_inc(stored[i], 16)
        act.wait_ge(k.nm["hi"], hi0)
        act.wait_ge(sem["zero"], 1)
        act.wait_ge(sem["omu"], 1)
        for j in range(3):
            x_act(act, j)
            block_done(k, act, b0 + j)
            if j == 0:
                act.activation(wa_h[0:64, :], k.ps[2][0:64, :], ACT.Tanh).then_inc(sem["hid"], 1)
            elif j == 1:
                act.activation(wa_h[64:P, :], k.ps[3][64:P, :], ACT.Copy).then_inc(sem["hid"], 1)
            else:
                act.activation(t[:, :], k.ps[2][:, :], ACT.Sigmoid).then_inc(sem["hid"], 1)
                act.wait_ge(sem["hid"], 3)
                act.activation(g_hi[:, :], t[:, :], ACT.Copy).then_inc(sem["hid"], 1)
        for o in range(3 * KT):
            row, m, slot = (W_, A_, G_)[o // KT], o % KT, o % 2
            act.wait_ge(sem["sec"], o + 1)
            act.wait_ge(stored[slot], 16 * (o // 2) + 16)
            if row == G_:
                act.activation(stage[slot][:, :], k.ps[slot][:, :], ACT.Copy).then_inc(sem["ev"], 1)
            else:
                c = PCOL["b_w0" if row == W_ else "b_a0"] + m
                act.activation(stage[slot][:, :], k.ps[slot][:, :], ACT.Sigmoid, bias=k.pc[:, c:c + 1]
                               ).then_inc(sem["ev"], 1)
            act.wait_ge(sem["ev"], o + 3)
            act.dma_start(scr[row, m, :, :], stage[slot][:, :]).then_inc(stored[slot], 16)
        for j, row in enumerate((R_, K_, V_)):
            x_act(act, 3 + j)
            with act.Fori(0, KT // 2) as i:
                for s in range(2):
                    block_done(k, act, i * 2 + (big[j] + s))
                    act.wait_ge(stored[s], i * 16 + (16 * (3 + j) * KT // 2 + 16))
                    act.activation(stage[s][:, :], k.ps[s][:, :], ACT.Copy).then_inc(sem["ev"], 1)
                    act.wait_ge(sem["ev"], i * 2 + (3 * KT + KT * j + s + 3))
                    act.dma_start(scr[row, bass.ds(i * 2 + s, 1), :, :].rearrange("m p t -> (m p) t"),
                                  stage[s][:, :]).then_inc(stored[s], 16)
        for i in range(2):
            act.wait_ge(stored[i], 16 * 3 * KT + 16)

    def dve_part(dve):
        dve.memset(hn[:, :, 0:1], 0.0).then_inc(sem["zero"], 1)
        c = PCOL["b_mu"]
        dve.tensor_scalar(omu[:, :], k.pc[:, c:c + 48], -1.0, 1.0, ALU.mult, ALU.add).then_inc(sem["omu"], 1)
        for j in range(3):
            x_dve(dve, j)
        dve.wait_ge(sem["hid"], 4)
        dve.tensor_tensor(g_lo[:, :], t[:, :], g_hi[:, :].bitcast(F32), ALU.subtract).then_inc(sem["gh_lo"], 1)
        for j in range(3, 6):
            x_dve(dve, j)

    k.parts["pe"].append(pe_part)
    k.parts["act"].append(act_part)
    k.parts["dve"].append(dve_part)
    stage_end(k)


def rwkv_stage(k, a):
    nc = k.nc
    scr = nc.dram_tensor("rwkv_scratch", (6, PAIRS, P, S), F32, kind="Internal").ap()
    yscr = nc.dram_tensor("rwkv_y", (PAIRS, P, S), F32, kind="Internal").ap()
    rwkv_project(k, a, scr)
    before = 3 * k.stages
    st = ExitStack()
    sb = lambda name, shape, dt=F32: st.enter_context(nc.sbuf_tensor("rc_" + name, shape, dt))
    BLK = S // P
    upper = sb("upper", [P, 2, P])
    diag = sb("diag", [P, P])
    level = sb("level", [P, 6, 2 * P], U8)
    carry = sb("carry", [P, S], mybir.dt.bfloat16)
    heads2 = sb("heads2", [P, 2])
    omka = sb("omka", [P, PAIRS])
    raw = sb("raw", [P, 4, S])
    r_in, k_in, w_in, a_in = (raw[:, i, :] for i in range(4))
    v_t = [sb(f"v_t{i}", [P, S]) for i in range(2)]
    ar = [sb(f"ar{i}", [P, BLK, 2, P]) for i in range(2)]
    b_t = [sb(f"b_t{i}", [P, S]) for i in range(2)]
    k_t = [sb(f"k_t{i}", [P, S]) for i in range(2)]
    b_e = [sb(f"b_e{i}", [P, S]) for i in range(2)]
    k_e = [sb(f"k_e{i}", [P, S]) for i in range(2)]
    p_end = [sb(f"p_end{i}", [P, 2 * BLK]) for i in range(2)]
    bonus = [sb(f"bonus{i}", [P, 2 * BLK]) for i in range(2)]
    gng = [sb(f"gng{i}", [P, P]) for i in range(2)]
    dec = sb("dec", [P, S])
    kk = sb("kk", [P, S])
    km = sb("km", [P, S])
    cum = sb("cum", [P, S])
    sm = sb("sm", [P, 8, 2 * BLK])
    rkw = sb("rkw", [P, 2])
    v_n = [sb(f"v_n{i}", [P, BLK, P]) for i in range(2)]
    y_n = [sb(f"y_n{i}", [P, BLK, P]) for i in range(2)]
    g_in = sb("g_in", [P, S])
    tmp = sb("tmp", [P, S])
    au = [sb(f"au{x}", [P, 2, P]) for x in range(2)]
    bk = [sb(f"bk{x}", [P, 2, P]) for x in range(2)]
    gm = [sb(f"gm{x}", [P, 2, 4, P]) for x in range(2)]
    n_t = [sb(f"n_t{x}", [P, 2, P]) for x in range(2)]
    xx = [sb(f"xx{x}", [P, 2, 2, P]) for x in range(2)]
    z = [sb(f"z{x}", [P, 2, P]) for x in range(2)]
    wu = [sb(f"wu{x}", [P, 2, P]) for x in range(2)]
    q_t = [sb(f"q_t{x}", [P, P]) for x in range(2)]
    mg = [[sb(f"mg{x}_{c}", [P, 2, P]) for c in range(2)] for x in range(2)]
    gp = sb("gp", [P, P])
    state = [sb(f"state{i}", [P, P]) for i in range(2)]
    st.close()
    y_t = st.enter_context(nc.sbuf_tensor("rc_y_t", [P, KT, S], F32))
    y_hi = st.enter_context(nc.sbuf_tensor("rc_y_hi", [P, KT, S], F32R))
    y_lo = st.enter_context(nc.sbuf_tensor("rc_y_lo", [P, KT, S], F32R))
    st.close()

    def bank(i):
        return k.ps[i // 2][:, (i % 2) * HALF:(i % 2 + 1) * HALF]

    sem = {n: k.sem("rc_" + n) for n in (
        "const", "masks", "raw", "g", "store", "omka",
        "sq", "scan", "km1", "km", "cump", "sum", "nmax", "nrec", "nroot", "exp", "bc", "kk", "b", "pend", "out",
        "rkw", "bon_ps", "bon",
        "s1", "mean", "yc", "ysq", "s2", "var", "vroot", "vrec", "yn", "gn", "bv", "z", "tp", "y",
        "seen", "zero", "s_ps", "gp", "s_new")}
    for n in ("t_ps", "t_sb", "g_ps", "g_sb", "n_sb", "x_up", "z_ps", "z_sb", "x_ps", "up_ps", "up_sb",
              "wu_ps", "wu_sb", "q_ps", "q_sb", "mg_ps", "mg_sb", "y_ps", "y_sb"):
        sem[n] = [k.sem(f"rc_{n}{x}") for x in range(2)]
    v_ld = [k.sem(f"rc_v_ld{i}") for i in range(2)]
    gn_ld = [k.sem(f"rc_gn_ld{i}") for i in range(2)]

    def pool_const(pool):
        pool.wait_ge(k.stage_done, before)
        n = [0]

        def done(ins):
            n[0] += 1
            ins.then_inc(sem["const"], 1)
            pool.wait_ge(sem["const"], n[0])
        done(pool.memset(upper[:, :, :], 1.0))
        for i in range(2):
            done(pool.affine_select(out=upper[:, i, :], in_=upper[:, i, :], compare_op=ALU.is_ge if i else ALU.is_gt, fill=0.0, base=0, pattern=[[1, P]], channel_multiplier=-1))
        done(pool.memset(upper[0:CHUNK, :, CHUNK:P], 0.0))
        done(pool.memset(diag[:, :], 0.0))
        done(pool.memset(heads2[:, :], 0.0))
        for h in range(2):
            half = slice(64 * h, 64 * h + 64)
            done(pool.memset(diag[half, half], 1.0))
            done(pool.memset(heads2[half, h:h + 1], 1.0))
        done(pool.memset(carry[:, :], 1.0))
        done(pool.memset(carry[:, :].rearrange("p (c t) -> p c t", t=CHUNK)[:, :, 0:1], 0.0))
        for lv in range(6):
            half, full = 1 << lv, 2 << lv
            nb = P // full
            f = tmp[:, 0:2 * P]
            done(pool.memset(f, 0.0))
            for part in range(2):
                view = f[:, part * P:(part + 1) * P].rearrange("p (b s w) -> p b s w", s=2, w=half)[:, :, 1 - part, :]
                done(pool.memset(view, 1.0))
                lo = part * half
                done(pool.affine_select(out=view, in_=view, compare_op=ALU.is_ge, fill=0.0, base=-lo,
                                        pattern=[[-full, nb], [0, half]], channel_multiplier=1))
                done(pool.affine_select(out=view, in_=view, compare_op=ALU.is_ge, fill=0.0, base=lo + half - 1,
                                        pattern=[[full, nb], [0, half]], channel_multiplier=-1))
            done(pool.tensor_copy(level[:, lv, :], f))
        pool.sem_inc(sem["masks"], 1)

    def dve_const(dve):
        c = PCOL["b_k_a"]
        dve.tensor_scalar(omka[:, :], k.pc[:, c:c + PAIRS], -1.0, 1.0, ALU.mult, ALU.add).then_inc(sem["omka"], 1)

    def sp_part(sp):
        sp.wait_ge(k.stage_done, before)
        for p in range(PAIRS):
            if p:
                sp.wait_ge(sem["out"], 7 * p)
                sp.wait_ge(sem["bon_ps"], p)
            for i, row in enumerate((R_, K_, W_, A_)):
                sp.dma_start(raw[:, i, :], scr[row, p, :, :]).then_inc(sem["raw"], 16)
            if p >= 2:
                for x in range(2):
                    sp.wait_ge(sem["t_ps"][x], 4 * (p - 1))
                sp.wait_ge(sem["gn"], p - 1)
            sp.dma_start(v_t[p % 2][:, :], scr[V_, p, :, :]).then_inc(v_ld[p % 2], 16)
            sp.dma_start(gng[p % 2][:, :], a.b_gn_g[0:1, p * P:(p + 1) * P].to_broadcast([P, P])
                         ).then_inc(gn_ld[p % 2], 16)
            if p >= 2:
                store(sp, p - 2)
            if p >= 1:
                sp.dma_start(g_in[:, :], scr[G_, p - 1, :, :]).then_inc(sem["g"], 16)
        store(sp, PAIRS - 2)
        sp.dma_start(g_in[:, :], scr[G_, PAIRS - 1, :, :]).then_inc(sem["g"], 16)
        store(sp, PAIRS - 1)

    def store(sp, p):
        sp.wait_ge(sem["y"], p + 1)
        sp.dma_start(yscr[p, :, :], g_in[:, :]).then_inc(sem["store"], 16)
        sp.wait_ge(sem["store"], 16 * (p + 1))

    def first(q, n=1):
        return isinstance(q, int) and q < n

    def col(name, q):
        return k.pc[:, bass.ds(q + PCOL[name], 1)]

    def prep_act(act, q, u, piece):
        if piece == 0:
            act.wait_ge(sem["raw"], q * 64 + 64)
            if not first(q):
                act.wait_ge(sem["pend"], q)
            act.activation(dec[:, :], k_in, ACT.Square, scale=col("b_k_k", q)).then_inc(sem["sq"], 1)
        elif piece == 1:
            act.wait_ge(sem["nrec"], q + 1)
            act.activation(sm[:, 2, :], sm[:, 1, :], ACT.Sqrt).then_inc(sem["nroot"], 1)
            act.wait_ge(sem["sum"], q + 1)
            act.wait_ge(sem["cump"], q + 1)
            act.activation(dec[:, :], cum[:, :], ACT.Exp, scale=-DECAY_C).then_inc(sem["exp"], 1)
            act.activation(w_in, w_in, ACT.Exp, scale=-DECAY_C).then_inc(sem["exp"], 1)
            act.wait_ge(sem["exp"], q * 3 + 2)
            act.activation(cum[:, :], cum[:, :], ACT.Exp, scale=DECAY_C).then_inc(sem["exp"], 1)
        elif piece == 2:
            if not first(q, 2):
                act.wait_ge(sem["s_new"], q * 16 - 16)
            act.activation(p_end[u][:, :].unsqueeze(2),
                           dec[:, :].rearrange("p (c t) -> p c t", t=CHUNK)[:, :, CHUNK - 1:CHUNK], ACT.Copy
                           ).then_inc(sem["pend"], 1)

    def prep_dve(dve, q, u, piece):
        if piece == 0:
            dve.wait_ge(sem["raw"], q * 64 + 64)
            dve.tensor_tensor_scan(cum[:, :], carry[:, :], w_in, 0.0, ALU.mult, ALU.add).then_inc(sem["scan"], 1)
            dve.tensor_scalar(km[:, :], a_in, col("b_k_a", q), omka[:, bass.ds(q, 1)], ALU.mult, ALU.add
                              ).then_inc(sem["km1"], 1)
            dve.tensor_scalar(rkw[:, :], heads2[:, :], col("b_r_k", q), None, ALU.mult).then_inc(sem["rkw"], 1)
        elif piece == 1:
            dve.wait_ge(sem["sum"], q + 1)
            dve.tensor_scalar(sm[:, 0, :], k.ps[3][:, 0:2 * BLK], 1e-24, None, ALU.max).then_inc(sem["nmax"], 1)
            dve.wait_ge(sem["nmax"], q + 1)
            dve.reciprocal(sm[:, 1, :], sm[:, 0, :]).then_inc(sem["nrec"], 1)
        elif piece == 2:
            dve.wait_ge(sem["bc"], q + 1)
            dve.scalar_tensor_tensor(out=kk[:, :], in0=k_in, scalar=col("b_k_k", q), in1=k.ps[3][:, :],
                                     op0=ALU.mult, op1=ALU.mult).then_inc(sem["kk"], 1)
            dve.wait_ge(sem["kk"], q + 1)
            dve.scalar_tensor_tensor(out=a_in, in0=kk[:, :], scalar=-1.0, in1=a_in, op0=ALU.mult, op1=ALU.mult
                                     ).then_inc(sem["b"], 1)
        elif piece == 3:
            dve.wait_ge(sem["bon_ps"], q + 1)
            if not first(q, 2):
                dve.wait_ge(sem["bv"], q - 1)
            dve.tensor_copy(bonus[u][:, :], k.ps[3][:, 0:2 * BLK]).then_inc(sem["bon"], 1)

    def prep_pool(pool, q, u, piece):
        if piece == 0:
            pool.wait_ge(sem["km1"], q + 1)
            pool.tensor_tensor(km[:, :], km[:, :], k_in, ALU.mult).then_inc(sem["km"], 1)
            pool.wait_ge(sem["scan"], q + 1)
            pool.tensor_tensor(w_in, cum[:, :], w_in, ALU.subtract).then_inc(sem["cump"], 1)
        elif piece == 2:
            pool.wait_ge(sem["exp"], q * 3 + 3)
            pool.wait_ge(sem["km"], q + 1)
            blocks = lambda t: t.rearrange("p (b t) -> p b t", t=P)
            ops = [(ar[u][:, :, 1, :], blocks(r_in), blocks(dec[:, :])),
                   (k_t[u][:, :], km[:, :], cum[:, :]),
                   (r_in, r_in, km[:, :]),
                   (ar[u][:, :, 0, :], blocks(kk[:, :]), blocks(w_in)),
                   (b_t[u][:, :], a_in, cum[:, :])]
            chunks = lambda t: t.rearrange("p (c t) -> p c t", t=CHUNK)
            end = chunks(dec[:, :])[:, :, CHUNK - 1:CHUNK].to_broadcast([P, 2 * BLK, CHUNK])
            ops += [(chunks(b_e[u][:, :]), chunks(b_t[u][:, :]), end), (chunks(k_e[u][:, :]), chunks(k_t[u][:, :]), end)]
            for n, (out, x0, x1) in enumerate(ops):
                if n == 2:
                    pool.wait_ge(sem["out"], q * 7 + 1)
                if n == 3:
                    pool.wait_ge(sem["b"], q + 1)
                if n == 5:
                    pool.wait_ge(sem["out"], q * 7 + 5)
                pool.tensor_tensor(out, x0, x1, ALU.mult).then_inc(sem["out"], 1)

    def prep_pe(pe, q, u, piece):
        if piece == 1:
            pe.wait_ge(sem["sq"], q + 1)
            if not first(q):
                pe.wait_ge(sem["bon"], q)
            for tt in range(BLK):
                last = pe.matmul(k.ps[3][:, 2 * tt:2 * tt + 2], dec[:, tt * P:(tt + 1) * P], heads2[:, :],
                                 start=True, stop=True)
            last.then_inc(sem["sum"], 1)
        elif piece == 2:
            pe.wait_ge(sem["masks"], 1)
            pe.wait_ge(sem["nroot"], q + 1)
            for tt in range(BLK):
                for h in range(2):
                    last = pe.matmul(k.ps[3][hs(h), tt * P:(tt + 1) * P],
                                     sm[:, 2, 2 * tt + h:2 * tt + h + 1].to_broadcast([P, 64]), k.ident[:, :],
                                     start=True, stop=True)
            last.then_inc(sem["bc"], 1)
        elif piece == 3:
            pe.wait_ge(sem["out"], q * 7 + 3)
            pe.wait_ge(sem["rkw"], q + 1)
            pe.wait_ge(sem["kk"], q + 1)
            for tt in range(BLK):
                last = pe.matmul(k.ps[3][:, 2 * tt:2 * tt + 2], r_in[:, tt * P:(tt + 1) * P], rkw[:, :],
                                 start=True, stop=True)
            last.then_inc(sem["bon_ps"], 1)


    def heads(t):
        return t.rearrange("p (g n) -> p g n", n=64)

    def flat(t):
        return t[:, :, :].rearrange("p b c -> p (b c)")

    def post_dve(dve, q, u, piece):
        if piece == 0:
            for x in range(2):
                dve.wait_ge(sem["y_sb"][x], q * 4 + 4)
            dve.tensor_reduce(sm[:, 3, :], heads(flat(y_n[u])), AX_X, ALU.add).then_inc(sem["s1"], 1)
            dve.wait_ge(sem["s1"], q + 1)
            dve.tensor_scalar(sm[:, 4, :], sm[:, 3, :], 1.0 / 64, None, ALU.mult).then_inc(sem["mean"], 1)
        elif piece == 1:
            dve.wait_ge(sem["ysq"], q + 1)
            dve.tensor_reduce(sm[:, 5, :], heads(tmp[:, :]), AX_X, ALU.add).then_inc(sem["s2"], 1)
            dve.wait_ge(sem["s2"], q + 1)
            dve.tensor_scalar(sm[:, 6, :], sm[:, 5, :], 1.0 / 64, GN_EPS, ALU.mult, ALU.add).then_inc(sem["var"], 1)
            dve.wait_ge(sem["vroot"], q + 1)
            dve.reciprocal(sm[:, 5, :], sm[:, 7, :]).then_inc(sem["vrec"], 1)
        elif piece == 3:
            dve.wait_ge(sem["tp"], q + 2)
            dve.wait_ge(sem["g"], q * 16 + 16)
            dve.scalar_tensor_tensor(out=g_in[:, :], in0=k.ps[3][:, :], scalar=col("b_gn_b", q), in1=g_in[:, :],
                                     op0=ALU.add, op1=ALU.mult).then_inc(sem["y"], 1)

    def post_act(act, q, u, piece):
        if piece == 1:
            act.wait_ge(sem["var"], q + 1)
            act.activation(sm[:, 7, :], sm[:, 6, :], ACT.Sqrt).then_inc(sem["vroot"], 1)

    def post_pool(pool, q, u, piece):
        wide = [P, 2 * BLK, 64]
        if piece == 0:
            pool.wait_ge(sem["mean"], q + 1)
            pool.tensor_tensor(heads(flat(y_n[u])), heads(flat(y_n[u])), sm[:, 4, :].unsqueeze(2).to_broadcast(wide),
                               ALU.subtract).then_inc(sem["yc"], 1)
            pool.wait_ge(sem["yc"], q + 1)
            pool.tensor_tensor(tmp[:, :], flat(y_n[u]), flat(y_n[u]), ALU.mult).then_inc(sem["ysq"], 1)
        elif piece == 1:
            pool.wait_ge(sem["vrec"], q + 1)
            pool.tensor_tensor(heads(flat(y_n[u])), heads(flat(y_n[u])), sm[:, 5, :].unsqueeze(2).to_broadcast(wide),
                               ALU.mult).then_inc(sem["yn"], 1)
            pool.wait_ge(sem["bon"], q + 1)
            pool.tensor_tensor(heads(tmp[:, :]), heads(flat(v_n[u])), bonus[u][:, :].unsqueeze(2).to_broadcast(wide),
                               ALU.mult).then_inc(sem["bv"], 1)
            pool.wait_ge(sem["yn"], q + 1)
            pool.wait_ge(gn_ld[u], (q - u) * 8 + 16)
            pool.tensor_tensor(y_n[u][:, :, :], y_n[u][:, :, :], gng[u][:, :].unsqueeze(1).to_broadcast([P, BLK, P]),
                               ALU.mult).then_inc(sem["gn"], 1)
            pool.wait_ge(sem["gn"], q + 1)
            pool.wait_ge(sem["bv"], q + 1)
            pool.tensor_tensor(flat(y_n[u]), flat(y_n[u]), tmp[:, :], ALU.add).then_inc(sem["z"], 1)

    def post_pe(pe, q, u, piece):
        if piece == 3:
            pe.wait_ge(sem["z"], q + 1)
            pe.wait_ge(sem["bon"], min(q + 3, PAIRS) if isinstance(q, int) else q + 3)
            for tt in range(BLK):
                last = pe.transpose(k.ps[3][:, tt * P:(tt + 1) * P], y_n[u][:, tt, :], k.ident[:, :])
            last.then_inc(sem["tp"], 1)

    def hs(h):
        return slice(64 * h, 64 * h + 64)

    LV = range(1, 6)

    def group_pe(pe, p, u, g):
        n = p * 4 + g
        for x in range(2):
            blk = 2 * g + x
            toks = slice(blk * P, (blk + 1) * P)
            if x == 0:
                if g or not first(p):
                    for y in range(2):
                        pe.wait_ge(sem["y_sb"][y], n)
                        pe.wait_ge(sem["mg_sb"][y], n * 2)
                    pe.wait_ge(sem["s_new"], n * 4)
                if g == 0:
                    pe.wait_ge(v_ld[u], (p - u) * 8 + 16)
                    pe.wait_ge(sem["out"], p * 7 + 7)
            else:
                pe.wait_ge(sem["t_sb"][0], n * 3 + 3)
            for i, src in enumerate((ar[u][:, blk, 0, :], b_e[u][:, toks], k_e[u][:, toks], v_t[u][:, toks])):
                last = pe.transpose(bank(0)[:, i * P:(i + 1) * P], src, k.ident[:, :])
            last.then_inc(sem["t_ps"][x], 1)
            if x == 1:
                pe.wait_ge(sem["g_sb"][0], n * 2 + 2)
                pe.wait_ge(sem["n_sb"][0], n * 2 + 2)
            for h in range(2):
                out = bank(4 + h)
                rhs = ar[u][hs(h), blk, :, :].rearrange("p a t -> p (a t)")
                pe.matmul(out[:, 0:2 * P], b_t[u][hs(h), toks], rhs, start=True, stop=True)
                pe.matmul(out[:, 2 * P:4 * P], k_t[u][hs(h), toks], rhs, start=True, stop=True
                          ).then_inc(sem["g_ps"][x], 1)
            for h in range(2):
                pe.matmul(bank(1 + h)[:, 0:P], ar[u][hs(h), blk, 0, :], b_t[u][hs(h), toks],
                          start=True, stop=True).then_inc(sem["g_ps"][x], 1)
        for x in range(2):
            if x == 0:
                for y in range(2):
                    pe.wait_ge(sem["g_sb"][y], n * 2 + 2)
                    pe.wait_ge(sem["t_sb"][y], n * 3 + 3)
            for h in range(2):
                last = pe.matmul(bank(4 + x)[:, hs(h)], gm[x][:, h, 2, :], v_n[u][:, 2 * g + x, hs(h)],
                                 start=True, stop=True)
            last.then_inc(sem["up_ps"][x], 1)
        for lv in LV:
            for x in range(2):
                if lv == 1:
                    pe.wait_ge(sem["n_sb"][1], n * 2 + 2)
                pe.wait_ge(sem["x_up"][x], n * 8 + (lv + 2))
                for h in range(2):
                    last = pe.matmul(bank(x)[:, h * P:(h + 1) * P], n_t[x][:, h, :], xx[x][:, h, 0, :],
                                     start=True, stop=True)
                last.then_inc(sem["z_ps"][x], 1)
            for x in range(2):
                pe.wait_ge(sem["z_sb"][x], n * 5 + lv)
                for h in range(2):
                    out = bank(2 + x)[:, h * 2 * P:(h + 1) * 2 * P]
                    pe.matmul(out[:, 0:P], xx[x][:, h, 1, :], z[x][:, h, :], start=True, stop=True)
                    last = pe.matmul(out[:, P:2 * P], z[x][:, h, :], xx[x][:, h, 1, :], start=True, stop=True)
                last.then_inc(sem["x_ps"][x], 1)
        for x in range(2):
            pe.wait_ge(sem["up_sb"][x], n + 1)
            pe.wait_ge(sem["x_up"][x], n * 8 + 8)
            for h in range(2):
                last = pe.matmul(bank(4 + x)[:, h * P:(h + 1) * P], xx[x][:, h, 0, :], au[x][:, h, :],
                                 start=True, stop=True)
            last.then_inc(sem["wu_ps"][x], 1)
        for x in range(2):
            pe.wait_ge(sem["wu_sb"][x], n + 1)
            for h in range(2):
                last = pe.matmul(bank(4 + x)[hs(h), 0:P], wu[x][:, 0, hs(h)], gm[x][:, h, 1, :], start=True, stop=True)
            last.then_inc(sem["q_ps"][x], 1)
            for c in range(2):
                if x == 0:
                    out = bank(c)
                else:
                    out = bank(3 + c)
                    if c == 1:
                        pe.wait_ge(sem["q_sb"][0], n + 1)
                rows = hs(c)
                pe.matmul(out[:, 0:P], wu[x][rows, 0, :], bk[x][rows, 0, :], start=True, stop=True)
                pe.matmul(out[:, P:2 * P], bk[x][rows, 0, :], wu[x][rows, 1, :], start=True, stop=False,
                          skip_group_check=True)
                pe.matmul(out[:, P:2 * P], bk[x][rows, 1, :], v_n[u][rows, 2 * g + x, :], start=False, stop=True,
                          skip_group_check=True).then_inc(sem["mg_ps"][x], 1)
            if x == 1:
                pe.wait_ge(sem["q_sb"][1], n + 1)
            y = bank(2) if x == 0 else bank(5)
            for h in range(2):
                pe.matmul(y[:, hs(h)], gm[x][:, h, 1, :], wu[x][:, 1, hs(h)], start=h == 0, stop=False,
                          skip_group_check=True)
                pe.matmul(y[:, hs(h)], gm[x][:, h, 3, :], v_n[u][:, 2 * g + x, hs(h)], start=False, stop=False,
                          skip_group_check=True)
        for x in range(2):
            pe.wait_ge(sem["q_sb"][x], n + 1)
            y = bank(2) if x == 0 else bank(5)
            for c in range(2):
                if x == c == 0 and g == 0:
                    pe.wait_ge(sem["zero"], p + 1)
                else:
                    pe.wait_ge(sem["s_new"], n * 4 + (2 * x + c))
                pe.wait_ge(sem["mg_sb"][x], n * 2 + (c + 1))
                out = bank(c if x == 0 else 3 + c)
                pe.matmul(out[:, 0:P], mg[x][c][:, 0, :], state[c][:, :], start=True, stop=True
                          ).then_inc(sem["s_ps"], 1)
                last = pe.matmul(y[hs(c), 0:P], q_t[x][:, hs(c)], state[c][:, :], start=False, stop=c == 1,
                                 skip_group_check=True)
            last.then_inc(sem["y_ps"][x], 1)

    def group_act(act, p, u, g):
        n = p * 4 + g
        for x in range(2):
            blk = 2 * g + x
            act.wait_ge(sem["t_ps"][x], n + 1)
            if g or not first(p):
                act.wait_ge(sem["s_ps"], n * 4)
            if g == 0 and not first(p, 2):
                act.wait_ge(sem["tp"], p)
            act.activation(au[x][:, :, 0:64], bank(0)[:, 0:P].rearrange("p (h n) -> p h n", n=64), ACT.Copy
                           ).then_inc(sem["t_sb"][x], 1)
            act.activation(bk[x][:, :, :].rearrange("p i c -> p (i c)"), bank(0)[:, P:3 * P], ACT.Copy
                           ).then_inc(sem["t_sb"][x], 1)
            act.activation(v_n[u][:, blk, :], bank(0)[:, 3 * P:4 * P], ACT.Copy).then_inc(sem["t_sb"][x], 1)
            for h in range(2):
                act.wait_ge(sem["g_ps"][x], n * 4 + (3 + h))
                act.activation(n_t[x][:, h, :], bank(1 + h)[:, 0:P], ACT.Copy).then_inc(sem["n_sb"][x], 1)
        for x in range(2):
            act.wait_ge(sem["up_ps"][x], n + 1)
            act.activation(au[x][:, :, 64:P], bank(4 + x)[:, 0:P].rearrange("p (h n) -> p h n", n=64), ACT.Copy
                           ).then_inc(sem["up_sb"][x], 1)
        for lv in LV:
            for x in range(2):
                act.wait_ge(sem["z_ps"][x], n * 5 + lv)
                act.activation(z[x][:, :, :].rearrange("p h c -> p (h c)"), bank(x)[:, 0:2 * P], ACT.Copy
                               ).then_inc(sem["z_sb"][x], 1)
        for x in range(2):
            act.wait_ge(sem["wu_ps"][x], n + 1)
            act.activation(wu[x][:, :, :].rearrange("p w (h n) -> p w h n", n=64),
                           bank(4 + x)[:, 0:2 * P].rearrange("p (h w n) -> p w h n", h=2, w=2), ACT.Copy
                           ).then_inc(sem["wu_sb"][x], 1)
        for x in range(2):
            act.wait_ge(sem["y_ps"][x], n + 1)
            act.activation(y_n[u][:, 2 * g + x, :], (bank(2) if x == 0 else bank(5))[:, 0:P], ACT.Copy
                           ).then_inc(sem["y_sb"][x], 1)

    def group_dve(dve, p, u, g):
        n = p * 4 + g
        ident4 = k.ident[:, :].unsqueeze(1).to_broadcast([P, 4, P])

        def lmask(lv, part=None):
            if part is None:
                return level[:, lv, :].unsqueeze(1).to_broadcast([P, 2, 2 * P])
            return level[:, lv, part * P:(part + 1) * P].unsqueeze(1).to_broadcast([P, 2, P])

        for x in range(2):
            if g or not first(p):
                dve.wait_ge(sem["s_ps"], n * 4)
            for h in range(2):
                dve.wait_ge(sem["g_ps"][x], n * 4 + (1 + h))
                dve.tensor_tensor(gm[x][:, h, :, :].rearrange("p (j i) c -> p j i c", i=2),
                                  bank(4 + h).rearrange("p (j i c) -> p j i c", i=2, c=P),
                                  upper[:, :, :].unsqueeze(1).to_broadcast([P, 2, 2, P]), ALU.mult).then_inc(sem["g_sb"][x], 1)
            dve.wait_ge(sem["g_sb"][x], n * 2 + 2)
            dve.wait_ge(sem["n_sb"][x], n * 2 + 2)
            dve.tensor_copy(xx[x][:, :, :, :].rearrange("p h i c -> p (h i) c"), ident4).then_inc(sem["x_up"][x], 1)
            dve.wait_ge(sem["x_up"][x], n * 8 + 1)
            dve.sem_inc(sem["seen"], 1)
            dve.copy_predicated(xx[x][:, :, 0, :], lmask(0, 0), gm[x][:, :, 0, :]).then_inc(sem["x_up"][x], 1)
            dve.copy_predicated(xx[x][:, :, 1, :], lmask(0, 1), n_t[x][:, :, :]).then_inc(sem["x_up"][x], 1)
        for lv in LV:
            for x in range(2):
                dve.wait_ge(sem["x_ps"][x], n * 5 + lv)
                dve.sem_inc(sem["seen"], 1)
                dve.copy_predicated(xx[x][:, :, :, :].rearrange("p h i c -> p h (i c)"), lmask(lv),
                                    bank(2 + x).rearrange("p (h c) -> p h c", h=2)).then_inc(sem["x_up"][x], 1)
        for x in range(2):
            dve.wait_ge(sem["q_ps"][x], n + 1)
            dve.tensor_tensor(q_t[x][:, :], bank(4 + x)[:, 0:P], ar[u][:, 2 * g + x, 1, :], ALU.add
                              ).then_inc(sem["q_sb"][x], 1)
            for c in range(2):
                dve.wait_ge(sem["mg_ps"][x], n * 2 + (c + 1))
                out = bank(c) if x == 0 else bank(3 + c)
                dve.tensor_tensor(mg[x][c][:, :, :], out[:, 0:2 * P].rearrange("p (i c) -> p i c", c=P),
                                  diag[:, :].unsqueeze(1).to_broadcast([P, 2, P]), ALU.mult).then_inc(sem["mg_sb"][x], 1)
        if g == 0:
            if not first(p):
                dve.wait_ge(sem["s_new"], n * 4)
            dve.memset(state[0][:, :], 0.0).then_inc(sem["zero"], 1)
            dve.wait_ge(sem["zero"], p + 1)
        for x in range(2):
            for c in range(2):
                e = n * 4 + (2 * x + c)
                if not (x == c == 0 and g == 0):
                    dve.wait_ge(sem["s_new"], e)
                dve.wait_ge(sem["mg_sb"][x], n * 2 + (c + 1))
                if x == c == g == 0:
                    dve.wait_ge(sem["pend"], p + 1)
                blk = 2 * g + x
                dve.scalar_tensor_tensor(out=gp[:, :], in0=state[c][:, :], scalar=p_end[u][:, 2 * blk + c:2 * blk + c + 1],
                                         in1=mg[x][c][:, 1, :], op0=ALU.mult, op1=ALU.add).then_inc(sem["gp"], 1)
                dve.wait_ge(sem["gp"], e + 1)
                dve.wait_ge(sem["s_ps"], e + 1)
                dve.tensor_tensor(state[1 - c][:, :], gp[:, :], bank(c if x == 0 else 3 + c)[:, 0:P], ALU.add
                                  ).then_inc(sem["s_new"], 1)

    def pair(eng, p, u, group, prep, post, do_post=True, do_prep=True):
        for g in range(4):
            if do_prep and prep:
                prep(eng, p + 1, 1 - u, g)
            if do_post and post:
                post(eng, p - 1, 1 - u, g)
            if group:
                group(eng, p, u, g)

    def whole(eng, group, prep, post):
        if prep:
            for piece in range(4):
                prep(eng, 0, 0, piece)
        pair(eng, 0, 0, group, prep, post, do_post=False)
        with eng.Fori(0, 3) as i:
            pair(eng, i * 2 + 1, 1, group, prep, post)
            pair(eng, i * 2 + 2, 0, group, prep, post)
        pair(eng, PAIRS - 1, 1, group, prep, post, do_prep=False)
        if post:
            for piece in range(4):
                post(eng, PAIRS - 1, 1, piece)

    def pe_all(pe):
        pe.sem_inc(sem["tp"], 1)
        pe.wait_ge(sem["masks"], 1)
        whole(pe, group_pe, prep_pe, post_pe)

    def act_all(act):
        whole(act, group_act, prep_act, post_act)

    def dve_all(dve):
        dve.wait_ge(sem["masks"], 1)
        dve.wait_ge(sem["omka"], 1)
        whole(dve, group_dve, prep_dve, post_dve)

    def pool_all(pool):
        pool_const(pool)
        whole(pool, None, prep_pool, post_pool)

    k.parts["sp"].append(sp_part)
    k.parts["pool"].append(pool_all)
    k.parts["dve"].append(dve_const)
    k.parts["pe"].append(pe_all)
    k.parts["act"].append(act_all)
    k.parts["dve"].append(dve_all)
    stage_end(k)
    y_back = k.sem("rc_y_back")
    blocks_done = 3 * k.stages

    def sp_back(sp):
        sp.wait_ge(k.stage_done, blocks_done)
        for kt in range(KT):
            sp.dma_start(y_t[:, kt, :], yscr[kt, :, :]).then_inc(y_back, 16)

    k.parts["sp"].append(sp_back)
    for name in ("act", "dve"):
        k.parts[name].append(lambda eng: eng.wait_ge(y_back, 16 * KT))
    lo_done = split_tiles(k, "rc_y", y_t, y_hi, y_lo)
    project_residual(k, "rc", a.b_w_o[0].rearrange("(k p) n -> p k n", p=P), y_hi, y_lo, lo_done, mod_col(1, 2))
    stage_end(k)


def out_stage(k, a):
    nc = k.nc
    with ExitStack() as st:
        y = st.enter_context(nc.sbuf_tensor("y", [P, KT, S], F32))
        row = [st.enter_context(nc.sbuf_tensor(f"out_row{i}", [P, D], F32)) for i in range(2)]
        norm_stage(k, PCOL["norm_final"], plain=lambda kt: y[:, kt, :])
    n = k.norms - 1
    o_t = k.sem("o_t")
    o_copied = k.sem("o_copied")
    o_stored = [k.sem(f"o_stored{i}") for i in range(2)]

    def pe_part(pe):
        pe.wait_ge(k.nm["t"], KT * (n + 1))
        for tt in range(TT):
            if tt >= 2:
                pe.wait_ge(o_copied, tt - 1)
            for kt in range(KT):
                last = pe.transpose(k.ps[2 + tt % 2][:, kt * P:(kt + 1) * P], y[:, kt, tt * P:(tt + 1) * P],
                                    k.ident[:, :])
            last.then_inc(o_t, 1)

    def act_part(act):
        for tt in range(TT):
            act.wait_ge(o_t, tt + 1)
            if tt >= 2:
                act.wait_ge(o_stored[tt % 2], 16 * (tt // 2))
            act.activation(row[tt % 2][:, :], k.ps[2 + tt % 2][:, :], ACT.Copy).then_inc(o_copied, 1)

    def sp_part(sp):
        for tt in range(TT):
            sp.wait_ge(o_copied, tt + 1)
            sp.dma_start(a.out[0, tt * P:(tt + 1) * P, :], row[tt % 2][:, :]).then_inc(o_stored[tt % 2], 16)
        for i in range(2):
            sp.wait_ge(o_stored[i], 16 * (TT // 2))

    for name, part in (("pe", pe_part), ("act", act_part), ("sp", sp_part)):
        k.parts[name].append(part)


def build(nc, a, stages=("dsa", "ffn0", "rwkv", "ffn1")):
    k = Kern()
    k.nc = nc
    with ExitStack() as stack:
        alloc(k, stack)
        setup_stage(k, a)
        stage_end(k)
        if "dsa" in stages:
            dsa_stage(k, a)
        if "ffn0" in stages:
            ffn_stage(k, a, 0)
        if "rwkv" in stages:
            rwkv_stage(k, a)
        if "ffn1" in stages:
            ffn_stage(k, a, 1)
        out_stage(k, a)
        block = stack.enter_context(nc.Block())

        @block.sync
        def _(eng):
            for part in k.parts["sp"]:
                part(eng)

        @block.gpsimd
        def _(eng):
            for part in k.parts["pool"]:
                part(eng)

        @block.tensor
        def _(eng):
            for part in k.parts["pe"]:
                part(eng)

        @block.scalar
        def _(eng):
            for part in k.parts["act"]:
                part(eng)

        @block.vector
        def _(eng):
            for part in k.parts["dve"]:
                part(eng)


_INS = ['x', 'c', 'ada_w', 'ada_b', 'norm_mix', 'norm_ffn', 'norm_final',
        'a_w_in', 'a_q_norm', 'a_kv_norm', 'a_kidx_g', 'a_kidx_b', 'a_w_uq', 'a_w_qi', 'a_w_uk', 'a_w_uv', 'a_w_o',
        'b_mu', 'b_w_r', 'b_w_k', 'b_w_v', 'b_w_o', 'b_w0', 'b_w1', 'b_w2', 'b_a0', 'b_a1', 'b_a2', 'b_g1', 'b_g2',
        'b_k_k', 'b_k_a', 'b_r_k', 'b_gn_g', 'b_gn_b', 'f_w_up', 'f_conv_w', 'f_conv_b', 'f_w_down']


Args = namedtuple("Args", _INS + ["out"])


def kernel(**inputs):
    import numpy as _np
    import concourse.bacc as _bacc
    from concourse import mybir as _mybir
    from concourse.bass_utils import run_bass_kernel_spmd as _run

    nc = _bacc.Bacc("TRN2", target_bir_lowering=False, num_devices=1)
    arrays, views = {}, {}
    for name in _INS:
        v = _np.ascontiguousarray(inputs[name])
        arrays[f"in_{name}_dram"] = v
        views[name] = nc.dram_tensor(f"in_{name}_dram", v.shape, _mybir.dt.from_np(v.dtype), kind="ExternalInput").ap()
    views["out"] = nc.dram_tensor("out_0_dram", (1, S, D), F32, kind="ExternalOutput").ap()
    build(nc, Args(**views))
    r = _run(nc, [arrays], core_ids=[0])
    return r.results[0]["out_0_dram"]
```

```python
from collections import namedtuple
from contextlib import ExitStack

import concourse.bass as bass
from concourse import mybir

F32 = mybir.dt.float32
F32R = mybir.dt.float32r
U8 = mybir.dt.uint8
ACT = mybir.ActivationFunctionType
ALU = mybir.AluOpType
AX_X = mybir.AxisListType.X

P = 128
S = 1024
D = 1024
KT = D // P
TT = S // P
HALF = 512
NH = S // HALF
CHUNK = 64
EPS = 1e-6
GN_EPS = 64e-5

A_HEADS, A_DH = 16, 64
Q_RANK, KV_RANK = 256, 128
IDX_HEADS, IDX_DIM = 8, 64
TOPK = 256
A_PROJ = Q_RANK + KV_RANK + IDX_DIM + IDX_HEADS

D_FF = 2816
FT = D_FF // P
CONV_W = 3
FF_TILES = 2
PARTS = FT // FF_TILES

UNSELECTED = 1e30
INADMISSIBLE = -2e38
TAKEN = -3e38

PARAM_ROWS = [
    [("c", KT), ("ada_b", 96), ("norm_mix", 16)],
    [("norm_ffn", 16), ("norm_final", 8), ("b_mu", 48), ("b_w0", 8), ("b_a0", 8), ("b_k_k", 8),
     ("b_k_a", 8), ("b_r_k", 8), ("b_gn_b", 8)],
    [("f_conv_b", 88), ("a_q_norm", 2), ("a_kv_norm", 1), ("kidx_g", 1), ("kidx_b", 1)],
    [("f_conv_w0", 128)],
    [("f_conv_w1", 128)],
    [("f_conv_w2", 8)],
]


def param_columns():
    col, at, rows = {}, 0, []
    for tile in PARAM_ROWS:
        here = 0
        for name, n in tile:
            col[name] = at + here
            here += n
        rows.append((at, here))
        at += here
    return col, rows, at


PCOL, PTILES, NPCOL = param_columns()


class Kern:
    pass


def alloc(k, stack):
    nc = k.nc
    k.sb = lambda name, shape, dt=F32: stack.enter_context(nc.sbuf_tensor(name, shape, dt))
    k.sem = lambda name: stack.enter_context(nc.semaphore(name))
    k.h = k.sb("h", [P, KT, S])
    k.ident = k.sb("ident", [P, P])
    k.ones = k.sb("ones", [P, 2])
    k.pc = k.sb("pc", [P, NPCOL])
    k.cact = k.sb("cact", [P, KT])
    k.mod = k.sb("mod", [P, 96])
    k.scl = k.sb("scl", [P, 4 * KT])
    k.ps = [stack.enter_context(nc.psum_tensor(f"ps{i}", [P, S], F32)) for i in range(4)]
    k.w_raw = [k.sb(f"w_raw{i}", [P, KT, P]) for i in range(2)]
    k.w_hi = [k.sb(f"w_hi{i}", [P, KT, P], F32R) for i in range(2)]
    k.w_lo = [k.sb(f"w_lo{i}", [P, KT, P], F32R) for i in range(2)]
    k.w_landed = [k.sem(f"w_landed{i}") for i in range(2)]
    k.w_hi_done = k.sem("w_hi_done")
    k.w_half = k.sem("w_half")
    k.w_split = k.sem("w_split")
    k.w_used = k.sem("w_used")
    k.stage_done = k.sem("stage_done")
    k.stages = 0
    k.blocks = 0
    k.landed = [0, 0]
    k.parts = {"pe": [], "act": [], "dve": [], "pool": [], "sp": []}
    k.norms = k.norm_lo = k.norm_hi = 0
    k.nm = {n: k.sem("nm_" + n) for n in
            ("scale", "sq", "sum", "ms", "root", "rinv", "bcast", "t", "hi", "lo")}


def mod_col(layer, which, t=0):
    return layer * 48 + which * KT + t


def stage_end(k):
    k.stages += 1
    n = 3 * k.stages
    for name in ("pe", "act", "dve"):
        def barrier(eng, n=n):
            eng.drain().then_inc(k.stage_done, 1)
            eng.wait_ge(k.stage_done, n)
        k.parts[name].append(barrier)
    return n


def passes3(pe, out, w_hi, w_lo, x_hi, x_lo, first, last):
    pe.matmul(out, w_hi, x_hi, start=first, stop=False)
    pe.matmul(out, w_hi, x_lo, start=False, stop=False)
    return pe.matmul(out, w_lo, x_hi, start=False, stop=last)


def split_block(k, pool, s, kts, b):
    for n, tiles in enumerate((slice(0, kts // 2), slice(kts // 2, kts))):
        raw, hi = k.w_raw[s][:, tiles, :], k.w_hi[s][:, tiles, :]
        one = k.ones[:, 0:1].unsqueeze(2).to_broadcast([P, kts // 2, P])
        pool.tensor_tensor(hi, raw, one, ALU.mult).then_inc(k.w_hi_done, 1)
        pool.wait_ge(k.w_hi_done, b * 2 + (n + 1))
        pool.tensor_tensor(k.w_lo[s][:, tiles, :], raw, hi.bitcast(F32), ALU.subtract
                           ).then_inc(k.w_split if n else k.w_half, 1)


def stream_loop(k, trips, blocks, extra=None):
    b0, landed0, count = k.blocks, list(k.landed), len(blocks)

    def load(sp, i):
        for n, (source, kts) in enumerate(blocks):
            if extra:
                extra(sp, i, n)
            sp.wait_ge(k.w_split, i * count + (b0 + n + 1))
            sp.dma_start(k.w_raw[n % 2][:, 0:kts, :], source(i)).then_inc(k.w_landed[n % 2], 16)

    def split(pool, i):
        for n, (_, kts) in enumerate(blocks):
            s, b = n % 2, i * count + (b0 + n)
            pool.wait_ge(k.w_landed[s], i * (8 * count) + (landed0[s] + 16 * (n // 2) + 16))
            pool.wait_ge(k.w_used, b + 1)
            split_block(k, pool, s, kts, b)

    def sp_part(sp):
        if trips is None:
            load(sp, 0)
        else:
            with sp.Fori(0, trips) as i:
                load(sp, i)

    def pool_part(pool):
        if trips is None:
            split(pool, 0)
        else:
            with pool.Fori(0, trips) as i:
                split(pool, i)

    k.parts["sp"].append(sp_part)
    k.parts["pool"].append(pool_part)
    total = count * (trips or 1)
    k.blocks += total
    for s in range(2):
        k.landed[s] += 8 * total
    return b0


def stream_weights(k, count, source):
    return stream_loop(k, count // 2, [(lambda i, s=s: source(i, s), KT) for s in range(2)])


def stream_pieces(k, blocks):
    b0, landed = k.blocks, list(k.landed)
    waits = []
    for n, pieces in enumerate(blocks):
        landed[n % 2] += 16 * len(pieces)
        waits.append(landed[n % 2])

    def sp_part(sp):
        for n, pieces in enumerate(blocks):
            sp.wait_ge(k.w_split, b0 + n + 1)
            for c0, c1, src in pieces:
                sp.dma_start(k.w_raw[n % 2][:, :, c0:c1], src).then_inc(k.w_landed[n % 2], 16)

    def pool_part(pool):
        for n in range(len(blocks)):
            pool.wait_ge(k.w_landed[n % 2], waits[n])
            pool.wait_ge(k.w_used, b0 + n + 1)
            split_block(k, pool, n % 2, KT, b0 + n)

    k.parts["sp"].append(sp_part)
    k.parts["pool"].append(pool_part)
    k.blocks += len(blocks)
    k.landed = landed
    return b0


def block_done(k, eng, b):
    eng.wait_ge(k.w_used, b + 3)


def wait_split(k, pe, b, kt=None, kts=KT):
    if kt == 0:
        pe.wait_ge(k.w_half, b + 1)
    elif kt is None or kt == kts // 2:
        pe.wait_ge(k.w_split, b + 3)


def setup_stage(k, a):
    nc = k.nc
    RING = 8
    sems, owned = ExitStack(), []

    def sem(name):
        owned.append(sems.enter_context(nc.semaphore(name)))
        return owned[-1]

    with ExitStack() as st:
        sb = lambda name, shape, dt=F32: st.enter_context(nc.sbuf_tensor(name, shape, dt))
        xin = sb("xin", [P, TT, D])
        prow = sb("prow", [P, len(PTILES), P])
        ada_w = [sb(f"ada_w{i}", [P, D]) for i in range(RING)]
        ada_acc = sb("ada_acc", [P, D])
    cact = k.cact
    const_ready = sem("const_ready")
    prow_landed = sem("prow_landed")
    x_landed = [sem(f"x_landed{i}") for i in range(2)]
    par_t = sem("par_t")
    par_done = sem("par_done")
    x_t = sem("x_t")
    x_act = sem("x_act")
    x_dve = sem("x_dve")
    c_act = sem("c_act")
    ada_landed = [sem(f"ada_landed{i}") for i in range(RING)]
    ada_acc_done = sem("ada_acc_done")
    ada_pe = sem("ada_pe")
    ada_mod = sem("ada_mod")

    srcs = {
        "c": a.c.rearrange("b (t p) -> (b t) p", p=P),
        "ada_b": a.ada_b.rearrange("l (t p) -> (l t) p", p=P),
        "norm_mix": a.norm_mix.rearrange("l (t p) -> (l t) p", p=P),
        "norm_ffn": a.norm_ffn.rearrange("l (t p) -> (l t) p", p=P),
        "norm_final": a.norm_final.rearrange("(t p) -> t p", p=P),
        "b_mu": a.b_mu.rearrange("l m (t p) -> (l m t) p", p=P),
        "b_w0": a.b_w0.rearrange("l (t p) -> (l t) p", p=P),
        "b_a0": a.b_a0.rearrange("l (t p) -> (l t) p", p=P),
        "b_k_k": a.b_k_k.rearrange("l (t p) -> (l t) p", p=P),
        "b_k_a": a.b_k_a.rearrange("l (t p) -> (l t) p", p=P),
        "b_r_k": a.b_r_k.rearrange("l (t h) n -> (l t) (h n)", h=2),
        "b_gn_b": a.b_gn_b.rearrange("l (t p) -> (l t) p", p=P),
        "f_conv_b": a.f_conv_b.rearrange("l (t p) -> (l t) p", p=P),
        "a_q_norm": a.a_q_norm.rearrange("l (t p) -> (l t) p", p=P),
        "a_kv_norm": a.a_kv_norm.rearrange("l (t p) -> (l t) p", p=P),
    }
    conv_rows = a.f_conv_w.rearrange("l w (t p) -> (l w t) p", p=P)

    def sp_part(sp):
        for t in range(TT):
            sp.dma_start(xin[:, t, :], a.x[0, t * P:(t + 1) * P, :]).then_inc(x_landed[t // 4], 16)
        with sp.Fori(0, 2) as w:
            for kt in range(KT):
                sp.wait_ge(ada_acc_done, w * KT + kt + 1)
                sp.dma_start(ada_w[kt][:, :], a.ada_w[0, kt * P:(kt + 1) * P, bass.ds(w * D, D)]
                             ).then_inc(ada_landed[kt], 16)

    k.n_param_dmas = sum(2 if n.startswith("kidx") else 1 for tile in PARAM_ROWS for n, _ in tile)

    def pool_part(pool):
        pool.sem_inc(k.w_split, 2)
        pool.memset(k.ident[:, :], 0.0).then_inc(const_ready, 1)
        pool.memset(k.ones[:, :], 1.0).then_inc(const_ready, 1)
        pool.wait_ge(const_ready, 2)
        pool.affine_select(out=k.ident[:, :], in_=k.ident[:, :], compare_op=ALU.not_equal, fill=1.0, base=0,
                           pattern=[[-1, P]], channel_multiplier=1).then_inc(const_ready, 1)

    def pe_part(pe):
        pe.sem_inc(k.w_used, 2)
        pe.sem_inc(ada_pe, 1)
        pe.wait_ge(const_ready, 3)
        pe.wait_ge(prow_landed, 16 * k.n_param_dmas)
        for i, (at, rows) in enumerate(PTILES):
            last = pe.transpose(k.ps[0][:, i * P:i * P + rows], prow[0:rows, i, :], k.ident[0:rows, 0:rows])
        last.then_inc(par_t, 1)
        pe.wait_ge(x_landed[0], 64)
        pe.wait_ge(x_landed[1], 64)
        for g in range(2 * KT):
            kt, half, bank = g // 2, g % 2, g % 6
            if g >= 6:
                pe.wait_ge(x_act if g % 2 == 0 else x_dve, (g - 6) // 2 + 1)
            out = k.ps[1 + bank // 2][:, (bank % 2) * HALF:(bank % 2 + 1) * HALF]
            for q in range(4):
                t = 4 * half + q
                last = pe.transpose(out[:, q * P:(q + 1) * P], xin[:, t, kt * P:(kt + 1) * P], k.ident[:, :])
            last.then_inc(x_t, 1)
        pe.wait_ge(par_done, len(PTILES))
        with pe.Fori(0, 2) as job:
            pe.wait_ge(ada_acc_done, KT + KT * job + KT)
            for m in range(KT):
                last = pe.matmul(k.ps[0][:, m:m + 1], ada_acc[:, m * P:(m + 1) * P], k.ones[:, 0:1],
                                 start=True, stop=True)
            last.then_inc(ada_pe, 1)

    def act_part(act):
        n = 0
        for i, tile in enumerate(PARAM_ROWS):
            at = 0
            for name, rows in tile:
                if name.startswith("f_conv_w"):
                    r0 = P * int(name[-1])
                    act.dma_start(prow[0:rows, i, :], conv_rows[r0:r0 + rows, :]).then_inc(prow_landed, 16)
                    n += 1
                elif name.startswith("kidx"):
                    src = a.a_kidx_g if name == "kidx_g" else a.a_kidx_b
                    for half in range(2):
                        act.dma_start(prow[at:at + 1, i, half * 64:half * 64 + 64], src).then_inc(prow_landed, 16)
                        n += 1
                else:
                    act.dma_start(prow[at:at + rows, i, :], srcs[name]).then_inc(prow_landed, 16)
                    n += 1
                at += rows
        assert n == k.n_param_dmas
        act.wait_ge(par_done, 1)
        act.activation(cact[:, :], k.pc[:, PCOL["c"]:PCOL["c"] + KT], ACT.Silu).then_inc(c_act, 1)
        for g in range(0, 2 * KT, 2):
            bank = g % 6
            act.wait_ge(x_t, g + 1)
            act.activation(k.h[:, g // 2, 0:HALF], k.ps[1 + bank // 2][:, (bank % 2) * HALF:(bank % 2 + 1) * HALF],
                           ACT.Copy).then_inc(x_act, 1)

    def dve_part(dve):
        dve.wait_ge(par_t, 1)
        for i, (at, rows) in enumerate(PTILES):
            dve.tensor_copy(k.pc[:, at:at + rows], k.ps[0][:, i * P:i * P + rows]).then_inc(par_done, 1)
        for g in range(1, 2 * KT, 2):
            bank = g % 6
            dve.wait_ge(x_t, g + 1)
            dve.tensor_copy(k.h[:, g // 2, HALF:S], k.ps[1 + bank // 2][:, (bank % 2) * HALF:(bank % 2 + 1) * HALF]
                            ).then_inc(x_dve, 1)
        dve.wait_ge(par_done, len(PTILES))
        dve.sem_inc(ada_acc_done, KT)
        dve.wait_ge(c_act, 1)
        with dve.Fori(0, 2) as job:
            dve.wait_ge(ada_pe, job + 1)
            for kt in range(KT):
                dve.wait_ge(ada_landed[kt], 16 * job + 16)
                if kt == 0:
                    dve.tensor_scalar(ada_acc[:, :], ada_w[0][:, :], cact[:, 0:1], None, ALU.mult
                                      ).then_inc(ada_acc_done, 1)
                else:
                    dve.wait_ge(ada_acc_done, KT + KT * job + kt)
                    dve.scalar_tensor_tensor(out=ada_acc[:, :], in0=ada_w[kt][:, :], scalar=cact[:, kt:kt + 1],
                                             in1=ada_acc[:, :], op0=ALU.mult, op1=ALU.add
                                             ).then_inc(ada_acc_done, 1)
            dve.wait_ge(ada_pe, job + 2)
            dve.tensor_tensor(k.mod[:, bass.ds(job * KT, KT)], k.ps[0][:, 0:KT],
                              k.pc[:, bass.ds(job * KT + PCOL["ada_b"], KT)], ALU.add).then_inc(ada_mod, 1)

    for name, part in (("sp", sp_part), ("pool", pool_part), ("pe", pe_part), ("act", act_part), ("dve", dve_part)):
        k.parts[name].append(part)
    stage_end(k)

    def clear(dve):
        for s in owned:
            dve.sem_clear(s)

    k.parts["dve"].append(clear)
    stage_end(k)
    sems.close()


def norm_stage(k, gain, layer=None, which=None, hi=None, lo=None, plain=None, keep=None):
    n = k.norms
    k.norms += 1
    nm = k.nm
    lo0, hi0 = k.norm_lo, k.norm_hi
    k.norm_lo += KT if hi is not None else 0
    k.norm_hi += KT if layer is not None else 0
    with ExitStack() as own:
        st = keep or own
        sq = [st.enter_context(k.nc.sbuf_tensor(f"nm_sq{n}_{i}", [P, S], F32)) for i in range(2)]
        t = [st.enter_context(k.nc.sbuf_tensor(f"nm_t{n}_{i}", [P, S], F32)) for i in range(2)]
        small = st.enter_context(k.nc.sbuf_tensor(f"nm_small{n}", [P, 3, TT], F32))
    ms, root, rinv = small[:, 0, :], small[:, 1, :], small[:, 2, :]
    sums, bcast = k.ps[0], k.ps[1]
    modulated = layer is not None
    scale = k.scl[:, 8 * (n % 4):8 * (n % 4) + 8] if modulated else k.pc[:, gain:gain + KT]
    split = hi is not None

    def shift(kt):
        c = mod_col(layer, which, kt)
        return k.mod[:, c:c + 1]

    def act_part(act):
        for kt in range(KT):
            if kt >= 2:
                act.wait_ge(nm["sum"], 8 * n + kt - 1)
            act.activation(sq[kt % 2][:, :], k.h[:, kt, :], ACT.Square).then_inc(nm["sq"], 1)
        act.wait_ge(nm["ms"], n + 1)
        act.activation(root, ms, ACT.Sqrt).then_inc(nm["root"], 1)
        if modulated:
            for kt in range(KT):
                act.wait_ge(nm["t"], 8 * n + kt + 1)
                out = hi[:, kt, :] if split else plain(kt)
                act.activation(out, t[kt % 2][:, :], ACT.Identity, bias=shift(kt)).then_inc(nm["hi"], 1)

    def pe_part(pe):
        for kt in range(KT):
            pe.wait_ge(nm["sq"], 8 * n + kt + 1)
            for tt in range(TT):
                last = pe.matmul(sums[:, tt:tt + 1], sq[kt % 2][:, tt * P:(tt + 1) * P], k.ones[:, 0:1],
                                 start=(kt == 0 and tt == 0), stop=(kt == KT - 1), skip_group_check=True)
            last.then_inc(nm["sum"], 1)
        pe.wait_ge(nm["rinv"], n + 1)
        for tt in range(TT):
            last = pe.transpose(bcast[:, tt * P:(tt + 1) * P], rinv[:, tt:tt + 1].to_broadcast([P, P]), k.ident[:, :])
        last.then_inc(nm["bcast"], 1)

    def dve_part(dve):
        if modulated:
            c = mod_col(layer, which + 1)
            dve.tensor_scalar(scale, k.mod[:, c:c + KT], 1.0, None, ALU.add).then_inc(nm["scale"], 1)
            dve.wait_ge(nm["scale"], 2 * n + 1)
            dve.tensor_tensor(scale, scale, k.pc[:, gain:gain + KT], ALU.mult).then_inc(nm["scale"], 1)
        dve.wait_ge(nm["sum"], 8 * n + 8)
        dve.tensor_scalar(ms, sums[:, 0:TT], 1.0 / D, EPS, ALU.mult, ALU.add).then_inc(nm["ms"], 1)
        dve.wait_ge(nm["root"], n + 1)
        dve.reciprocal(rinv, root).then_inc(nm["rinv"], 1)
        dve.wait_ge(nm["bcast"], n + 1)
        if modulated:
            dve.wait_ge(nm["scale"], 2 * n + 2)

        def low(kt):
            dve.wait_ge(nm["hi"], hi0 + kt + 1)
            dve.scalar_tensor_tensor(out=lo[:, kt, :], in0=t[kt % 2][:, :], scalar=shift(kt),
                                     in1=hi[:, kt, :].bitcast(F32), op0=ALU.add, op1=ALU.subtract
                                     ).then_inc(nm["lo"], 1)

        for kt in range(KT):
            if modulated and not split and kt >= 2:
                dve.wait_ge(nm["hi"], hi0 + kt - 1)
            if split and kt >= 2:
                dve.wait_ge(nm["lo"], lo0 + kt - 1)
            out = t[kt % 2][:, :] if modulated else plain(kt)
            dve.scalar_tensor_tensor(out=out, in0=k.h[:, kt, :], scalar=scale[:, kt:kt + 1], in1=bcast[:, :],
                                     op0=ALU.mult, op1=ALU.mult).then_inc(nm["t"], 1)
            if split and kt >= 1:
                low(kt - 1)
        if split:
            low(KT - 1)

    for name, part in (("pe", pe_part), ("act", act_part), ("dve", dve_part)):
        k.parts[name].append(part)
    return lo0


def ffn_stage(k, a, layer):
    nc = k.nc
    if layer == 0:
        k.ffn = {n: k.sem("ffn_" + n) for n in
                 ("zero", "u_copy", "u_lin", "tap", "silu", "gated", "g_hi", "g_free", "resid")}
    f = k.ffn
    with ExitStack() as st:
        sb = lambda name, shape, dt=F32: st.enter_context(nc.sbuf_tensor(f"{name}_{layer}", shape, dt))
        hn_hi, hn_lo = sb("hn_hi", [P, KT, S], F32R), sb("hn_lo", [P, KT, S], F32R)
        norm0 = norm_stage(k, PCOL["norm_ffn"] + layer * KT, layer, 3, hn_hi, hn_lo)
        g_hi = sb("g_hi", [P, 2 * FF_TILES, S], F32R)
        g_lo = sb("g_lo", [P, 2 * FF_TILES, S], F32R)
        u = [sb(f"u{i}", [P, S + 2]) for i in range(2)]
        c = [sb(f"uc{i}", [P, S]) for i in range(2)]
        sg = sb("sg", [P, S])
        ada_w = [sb(f"f_ada_w{i}", [P, D]) for i in range(4)] if layer == 0 else None
        ada_acc = sb("f_ada_acc", [P, D]) if layer == 0 else None
    if layer == 0:
        before = 3 * k.stages
        m_landed = [k.sem(f"m_landed{i}") for i in range(4)]
        m_acc = k.sem("m_acc")
        m_ps = k.sem("m_ps")
        m_done = k.sem("m_done")
    w_up = a.f_w_up[layer].rearrange("(k p) n -> p k n", p=P)
    w_down = a.f_w_down[layer].rearrange("(k p) n -> p k n", p=P)
    bcol = PCOL["f_conv_b"] + 2 * FT * layer
    wcol = PCOL["f_conv_w0"] + CONV_W * 2 * FT * layer
    tiles0, outs0 = FT * layer, KT * PARTS * layer

    def up_block(i, q, n):
        return w_up[:, :, bass.ds(i * (2 * FF_TILES * P) + (q * FF_TILES * P + (n // 2) * P + (n % 2) * D_FF), P)]

    def down_block(i, q, m):
        if isinstance(i, int):
            r0 = FF_TILES * (2 * i + q)
            return w_down[:, r0:r0 + FF_TILES, m * P:(m + 1) * P]
        return w_down[:, bass.ds(i * (2 * FF_TILES) + q * FF_TILES, FF_TILES), m * P:(m + 1) * P]

    UPS = 2 * FF_TILES
    STEP = UPS + KT
    def load_mod(sp, w, half, n):
        if half or not isinstance(w, int):
            sp.wait_ge(m_acc, w * KT + (4 * half - 4 + n + 1))
        else:
            sp.wait_ge(k.stage_done, before)
        r0 = (4 * half + n) * P
        sp.dma_start(ada_w[n][:, :], a.ada_w[1, r0:r0 + P, bass.ds(w * D, D)]).then_inc(m_landed[n], 16)

    def dve_mod(dve, w, half):
        for n in range(4):
            dve.wait_ge(m_landed[n], w * 32 + (16 * half + 16))
            kt = 4 * half + n
            if kt == 0:
                dve.tensor_scalar(ada_acc[:, :], ada_w[0][:, :], k.cact[:, 0:1], None, ALU.mult).then_inc(m_acc, 1)
            else:
                dve.wait_ge(m_acc, w * KT + kt)
                dve.scalar_tensor_tensor(out=ada_acc[:, :], in0=ada_w[n][:, :], scalar=k.cact[:, kt:kt + 1],
                                         in1=ada_acc[:, :], op0=ALU.mult, op1=ALU.add).then_inc(m_acc, 1)

    def pe_mod(pe, w):
        pe.wait_ge(m_acc, w * KT + KT)
        for m in range(KT):
            last = pe.matmul(k.ps[3][:, m:m + 1], ada_acc[:, m * P:(m + 1) * P], k.ones[:, 0:1], start=True, stop=True)
        last.then_inc(m_ps, 1)

    def dve_mod_end(dve, w):
        dve.wait_ge(m_ps, w + 1)
        dve.tensor_tensor(k.mod[:, bass.ds(w * KT + 48, KT)], k.ps[3][:, 0:KT],
                          k.pc[:, bass.ds(w * KT + (PCOL["ada_b"] + 48), KT)], ALU.add).then_inc(m_done, 1)

    def first_loads(sp, i, n):
        if layer == 0:
            load_mod(sp, 0, 0, n)

    def loads(sp, i, n):
        if layer == 0 and n % STEP in (5, 7, 9, 11):
            load_mod(sp, i + 1, n // STEP, (n % STEP - 5) // 2)

    b0 = stream_loop(k, None, [(lambda i, n=n: up_block(0, 0, n), KT) for n in range(UPS)], first_loads)
    if layer == 0:
        def second_loads(sp):
            for n in range(4):
                load_mod(sp, 0, 1, n)
        k.parts["sp"].append(second_loads)
    body = []
    for q in range(2):
        body += [(lambda i, q=q, n=n: up_block(i, q + 1, n), KT) for n in range(UPS)]
        body += [(lambda i, q=q, m=m: down_block(i, q, m), FF_TILES) for m in range(KT)]
    b1 = stream_loop(k, PARTS // 2, body, loads)
    b2 = stream_loop(k, None, [(lambda i, m=m: down_block(PARTS // 2, 0, m), FF_TILES) for m in range(KT)])

    def pe_up(pe, T, O, b, first=False, mod=None):
        for n in range(UPS):
            if mod is not None and n == 2:
                pe.wait_ge(f["u_lin"], T * 2 + 4)
                pe.wait_ge(f["resid"], O + 4)
                pe_mod(pe, mod)
            if mod is not None and n == 3:
                pe.wait_ge(m_done, mod + 1)
            pe.wait_ge(f["u_lin"], T * 2 + (n + 1))
            pe.wait_ge(f["resid"], O + (n + 1))
            for kt in range(KT):
                wait_split(k, pe, b + n, kt)
                if first and n == 0:
                    pe.wait_ge(k.nm["lo"], norm0 + kt + 1)
                for half in range(NH):
                    cols = slice(half * HALF, (half + 1) * HALF)
                    last = passes3(pe, k.ps[n][:, cols], k.w_hi[n % 2][:, kt, :], k.w_lo[n % 2][:, kt, :],
                                   hn_hi[:, kt, cols], hn_lo[:, kt, cols], kt == 0, kt == KT - 1)
            last.then_inc(k.w_used, 1)

    def pe_down(pe, T, O, b, q, T_up=None):
        for m in range(KT):
            if T_up is not None and m < 4:
                pe.wait_ge(f["u_lin"], T_up * 2 + (4 + m + 1))
            if m == 0:
                pe.wait_ge(f["g_free"], T + (FF_TILES + 1))
            pe.wait_ge(f["resid"], O + (m + 1))
            for kt in range(FF_TILES):
                wait_split(k, pe, b + m, kt, FF_TILES)
                for half in range(NH):
                    cols = slice(half * HALF, (half + 1) * HALF)
                    last = passes3(pe, k.ps[m % 4][:, cols], k.w_hi[m % 2][:, kt, :], k.w_lo[m % 2][:, kt, :],
                                   g_hi[:, q * FF_TILES + kt, cols], g_lo[:, q * FF_TILES + kt, cols],
                                   kt == 0, kt == FF_TILES - 1)
            last.then_inc(k.w_used, 1)

    def pe_part(pe):
        if layer == 0:
            pe.sem_inc(f["u_lin"], 4)
            pe.sem_inc(f["resid"], 4)
        pe_up(pe, tiles0, outs0, b0, first=True)
        with pe.Fori(0, PARTS // 2) as i:
            for q in range(2):
                T, O = i * (2 * FF_TILES) + (tiles0 + q * FF_TILES), i * (2 * KT) + (outs0 + q * KT)
                b = i * (2 * STEP) + (b1 + q * STEP)
                pe_up(pe, T + FF_TILES, O, b, mod=i if layer == 0 and q == 1 else None)
                pe_down(pe, T, O, b + UPS, q, T + FF_TILES)
        pe_down(pe, tiles0 + FT - FF_TILES, outs0 + (PARTS - 1) * KT, b2, 0)
        if layer == 0:
            pe.wait_ge(f["resid"], outs0 + PARTS * KT + 4)
            pe_mod(pe, 5)

    def act_up(act, i, q, T, b, slot):
        col = lambda base, s: k.pc[:, bass.ds(i * (2 * FF_TILES) + (q * FF_TILES + s + base), 1)]
        for s in range(FF_TILES):
            for wi in range(2):
                block_done(k, act, b + (2 * s + wi))
                act.wait_ge(f["g_free"], T + (s + 1))
                act.activation(u[wi][:, 2:S + 2], k.ps[2 * s + wi][:, :], ACT.Copy).then_inc(f["u_copy"], 1)
                act.activation(c[wi][:, :], k.ps[2 * s + wi][:, :], ACT.Identity, bias=col(bcol + wi * FT, s),
                               scale=col(wcol + 4 * FT + wi * FT, s)).then_inc(f["u_lin"], 1)
            act.wait_ge(f["tap"], T * 4 + (4 * s + 2))
            act.activation(sg[:, :], c[0][:, :], ACT.Silu).then_inc(f["silu"], 1)
            act.wait_ge(f["gated"], T + (s + 1))
            act.activation(g_hi[:, slot * FF_TILES + s, :], c[1][:, :], ACT.Copy).then_inc(f["g_hi"], 1)

    def dve_up(dve, i, q, T, slot, between=None):
        for s in range(FF_TILES):
            for wi in range(2):
                dve.wait_ge(f["u_lin"], T * 2 + (4 + 2 * s + wi + 1))
                for tap in (1, 0):
                    if tap == 0:
                        dve.wait_ge(f["tap"], T * 4 + (4 * s + 2 * wi + 1))
                    col = q * FF_TILES + s + wcol + 2 * FT * tap + wi * FT
                    dve.scalar_tensor_tensor(
                        out=c[wi][:, :], in0=u[wi][:, tap:tap + S], scalar=k.pc[:, bass.ds(i * (2 * FF_TILES) + col, 1)],
                        in1=c[wi][:, :], op0=ALU.mult, op1=ALU.add).then_inc(f["tap"], 1)
            dve.wait_ge(f["silu"], T + (s + 1))
            dve.wait_ge(f["tap"], T * 4 + (4 * s + 4))
            dve.tensor_tensor(c[1][:, :], c[1][:, :], sg[:, :], ALU.mult).then_inc(f["gated"], 1)
            dve.wait_ge(f["g_hi"], T + (s + 1))
            dve.tensor_tensor(g_lo[:, slot * FF_TILES + s, :], c[1][:, :],
                              g_hi[:, slot * FF_TILES + s, :].bitcast(F32), ALU.subtract).then_inc(f["g_free"], 1)
            if s == 0 and between:
                between()

    def dve_down(dve, b):
        for m in range(KT):
            block_done(k, dve, b + m)
            gate = mod_col(layer, 5, m)
            dve.scalar_tensor_tensor(out=k.h[:, m, :], in0=k.ps[m % 4][:, :], scalar=k.mod[:, gate:gate + 1],
                                     in1=k.h[:, m, :], op0=ALU.mult, op1=ALU.add).then_inc(f["resid"], 1)

    def act_part(act):
        act.wait_ge(f["zero"], 2 * layer + 2)
        act_up(act, 0, 0, tiles0, b0, 0)
        with act.Fori(0, PARTS // 2) as i:
            for q in range(2):
                act_up(act, i, q + 1, i * (2 * FF_TILES) + (tiles0 + (q + 1) * FF_TILES),
                       i * (2 * STEP) + (b1 + q * STEP), 1 - q)

    def dve_part(dve):
        dve.wait_ge(k.nm["lo"], norm0 + KT)
        for i in range(2):
            dve.memset(u[i][:, 0:2], 0.0).then_inc(f["zero"], 1)
        if layer == 0:
            dve.sem_inc(f["g_free"], 1)
        dve_up(dve, 0, 0, tiles0, 0, (lambda: dve_mod(dve, 0, 0)) if layer == 0 else None)
        with dve.Fori(0, PARTS // 2) as i:
            for q in range(2):
                def between():
                    if q == 0:
                        dve_mod(dve, i, 1)
                    else:
                        dve_mod_end(dve, i)
                        dve_mod(dve, i + 1, 0)
                dve_up(dve, i, q + 1, i * (2 * FF_TILES) + (tiles0 + (q + 1) * FF_TILES), 1 - q,
                       between if layer == 0 else None)
                dve_down(dve, i * (2 * STEP) + (b1 + q * STEP + UPS))
        if layer == 0:
            dve_mod(dve, 5, 1)
        dve_down(dve, b2)
        if layer == 0:
            dve_mod_end(dve, 5)

    k.parts["pe"].append(pe_part)
    k.parts["act"].append(act_part)
    k.parts["dve"].append(dve_part)
    stage_end(k)


def split_tiles(k, name, src, hi, lo, landed=None):
    hi_done, lo_done = k.sem(name + "_hi_done"), k.sem(name + "_lo_done")

    def act_part(act):
        for kt in range(KT):
            if landed:
                act.wait_ge(landed[kt], 16)
            act.activation(hi[:, kt, :], src[:, kt, :], ACT.Copy).then_inc(hi_done, 1)

    def dve_part(dve):
        for kt in range(KT):
            dve.wait_ge(hi_done, kt + 1)
            dve.tensor_tensor(lo[:, kt, :], src[:, kt, :], hi[:, kt, :].bitcast(F32), ALU.subtract
                              ).then_inc(lo_done, 1)

    k.parts["act"].append(act_part)
    k.parts["dve"].append(dve_part)
    return lo_done


def project_residual(k, name, w, x_hi, x_lo, x_ready, gate_col):
    b0 = stream_weights(k, KT, lambda i, s: w[:, :, bass.ds(i * (2 * P) + s * P, P)])
    resid = k.sem(name + "_resid")

    def pe_part(pe):
        pe.sem_inc(resid, 2)
        with pe.Fori(0, KT // 2) as i:
            for s in range(2):
                pe.wait_ge(resid, i * 2 + (s + 1))
                for kt in range(KT):
                    wait_split(k, pe, i * 2 + (b0 + s), kt)
                    pe.wait_ge(x_ready, kt + 1)
                    for n in range(NH):
                        cols = slice(n * HALF, (n + 1) * HALF)
                        last = passes3(pe, k.ps[s][:, cols], k.w_hi[s][:, kt, :], k.w_lo[s][:, kt, :],
                                       x_hi[:, kt, cols], x_lo[:, kt, cols], kt == 0, kt == KT - 1)
                last.then_inc(k.w_used, 1)

    def dve_part(dve):
        with dve.Fori(0, KT // 2) as i:
            for s in range(2):
                block_done(k, dve, i * 2 + (b0 + s))
                hm = k.h[:, bass.ds(i * 2 + s, 1), :]
                dve.scalar_tensor_tensor(out=hm, in0=k.ps[s][:, :].unsqueeze(1),
                                         scalar=k.mod[:, bass.ds(i * 2 + (s + gate_col), 1)], in1=hm,
                                         op0=ALU.mult, op1=ALU.add).then_inc(resid, 1)

    k.parts["pe"].append(pe_part)
    k.parts["dve"].append(dve_part)


def dsa_stage(k, a):
    nc = k.nc
    perm, early, scratch = ExitStack(), ExitStack(), ExitStack()
    sb = lambda st, name, shape, dt=F32: st.enter_context(nc.sbuf_tensor("d_" + name, shape, dt))
    before = 3 * k.stages
    q_lat = sb(perm, "q_lat", [P, 2, S])
    ckv_t = sb(perm, "ckv_t", [P, S])
    ckv_n = sb(perm, "ckv_n", [P, TT, P])
    kidx = sb(perm, "kidx", [P, S])
    w_uq = sb(perm, "w_uq", [P, 2, A_HEADS * A_DH])
    w_qi = sb(perm, "w_qi", [P, 2, IDX_HEADS * IDX_DIM])
    w_uk_t = sb(perm, "w_uk_t", [P, A_HEADS // 2, P])
    w_uv = sb(perm, "w_uv", [P, A_HEADS, A_DH])
    w_ix = sb(perm, "w_ix", [P, KT, IDX_HEADS])
    w_ix_hi = sb(perm, "w_ix_hi", [P, KT, IDX_HEADS], F32R)
    w_ix_lo = sb(perm, "w_ix_lo", [P, KT, IDX_HEADS], F32R)
    wi = sb(perm, "wi", [P, TT, IDX_HEADS])
    stat = sb(perm, "stat", [P, 4, 4 * TT])
    small = sb(perm, "small", [P, 4, A_HEADS])
    top8 = sb(perm, "top8", [P, 8])
    diag = [sb(perm, f"diag{i}", [P, P]) for i in range(2)]
    hn_hi, hn_lo = sb(early, "hn_hi", [P, KT, S], F32R), sb(early, "hn_lo", [P, KT, S], F32R)
    norm0 = norm_stage(k, PCOL["norm_mix"], 0, 0, hn_hi, hn_lo, keep=early)
    w_in = a.a_w_in[0].rearrange("(k p) n -> p k n", p=P)
    c2 = Q_RANK + KV_RANK
    b0 = stream_pieces(k, [[(0, P, w_in[:, :, 0:P])], [(0, P, w_in[:, :, P:2 * P])],
                           [(0, P, w_in[:, :, Q_RANK:c2])],
                           [(0, 64, w_in[:, :, c2:c2 + IDX_DIM]), (64, P, w_in[:, :, c2:c2 + IDX_DIM])]])
    ada_w = [sb(early, f"ada_w{i}", [P, D]) for i in range(4)]
    ada_acc = [sb(early, f"ada_acc{i}", [P, D]) for i in range(2)]
    early.close()
    sq = sb(early, "sq", [P, 3, S])
    w_uk = sb(early, "w_uk", [P, A_HEADS, A_DH])
    early.close()
    o_t = sb(perm, "o_t", [P, KT, S])
    q_t = sb(scratch, "q_t", [P, A_HEADS // 2, P])
    qi_t = sb(scratch, "qi_t", [P, IDX_HEADS // 2, P])
    q_abs = sb(scratch, "q_abs", [P, 2, A_HEADS // 2, P])
    work = [sb(scratch, f"work{i}", [P, S]) for i in range(2)]
    dist = [sb(scratch, f"dist{i}", [P, S]) for i in range(2)]
    rel = [sb(scratch, f"rel{i}", [P, S]) for i in range(2)]
    x = [sb(scratch, f"x{i}", [P, S]) for i in range(3)]
    p_t = [sb(scratch, f"p_t{i}", [P, TT, P]) for i in range(2)]
    o_lat = [sb(scratch, f"o_lat{i}", [P, P]) for i in range(2)]
    scratch.close()
    o_hi, o_lo = sb(scratch, "o_hi", [P, KT, S], F32R), sb(scratch, "o_lo", [P, KT, S], F32R)
    scratch.close()
    perm.close()

    sems = ExitStack()
    sem = {n: sems.enter_context(nc.semaphore("d_" + n)) for n in (
        "w_landed",
        "m_acc",
        "m_ps",
        "m_done",
        "evac",
        "wi_split",
        "wi_ps",
        "wi_done",
        "sq",
        "sum", "ms", "root", "rinv", "bcast", "cent",
        "sq2", "sum2", "ms2", "root2", "rinv2", "bcast2", "kidx",
        "lat",
        "ckv_ps", "uk_ps", "ckv_n", "uk_t",
        "qT_ps", "qT_sb", "qi_ps", "qi_sb", "qa_ps", "qa_sb",
        "sc_ps", "relu", "scaled", "acc", "iota", "dist", "mask", "top", "take",
        "qk_ps", "x_max", "nbias", "x_exp", "rinv_h", "x_norm", "p_ps", "p_sb", "ol_ps", "ol_sb", "o_ps", "o_sb",
        "mask_d", "unsel")}

    m_landed = [sems.enter_context(nc.semaphore(f"d_m_landed{i}")) for i in range(4)]

    def slope(h):
        return 2.0 ** (-8.0 * (h + 1) / A_HEADS)

    def keys(s):
        return (s + 1) * P

    EARLY = 8
    INDEXED = range(TOPK // P, TT)

    def sp_part(sp):
        sp.wait_ge(k.stage_done, before)
        for dst, src in ((w_uq[:, :, :], a.a_w_uq[0].rearrange("(t p) n -> p t n", p=P)),
                         (w_qi[:, :, :], a.a_w_qi[0].rearrange("(t p) n -> p t n", p=P)),
                         (w_uv[:, :, :], a.a_w_uv[0].rearrange("h c d -> c h d")),
                         (w_ix[:, :, :], w_in[:, :, c2 + IDX_DIM:A_PROJ])):
            sp.dma_start(dst, src).then_inc(sem["w_landed"], 16)
        for n in range(4 * KT):
            if n >= 4:
                sp.wait_ge(sem["m_acc"], n - 3)
            sp.dma_start(ada_w[n % 4][:, :], a.ada_w[0, (n % KT) * P:(n % KT + 1) * P, (2 + n // KT) * D:(3 + n // KT) * D]
                         ).then_inc(m_landed[n % 4], 16)
        sp.wait_ge(sem["wi_ps"], 1)
        sp.dma_start(w_uk[:, :, :], a.a_w_uk[0].rearrange("h c d -> c h d")).then_inc(sem["w_landed"], 16)

    def pe_mod(pe, w):
        pe.wait_ge(sem["m_acc"], KT * (w + 1))
        if w == 0:
            pe.wait_ge(sem["evac"], 1)
        for m in range(KT):
            last = pe.matmul(k.ps[0][:, HALF + KT * w + m:HALF + KT * w + m + 1],
                             ada_acc[w % 2][:, m * P:(m + 1) * P], k.ones[:, 0:1], start=True, stop=True)
        last.then_inc(sem["m_ps"], 1)

    def dve_mods(dve):
        for w in range(4):
            acc = ada_acc[w % 2]
            if w >= 2:
                dve.wait_ge(sem["m_ps"], w - 1)
            for kt in range(KT):
                n = KT * w + kt
                dve.wait_ge(m_landed[n % 4], 16 * (n // 4) + 16)
                if kt == 0:
                    dve.tensor_scalar(acc[:, :], ada_w[n % 4][:, :], k.cact[:, 0:1], None, ALU.mult
                                      ).then_inc(sem["m_acc"], 1)
                else:
                    dve.wait_ge(sem["m_acc"], n)
                    dve.scalar_tensor_tensor(out=acc[:, :], in0=ada_w[n % 4][:, :], scalar=k.cact[:, kt:kt + 1],
                                             in1=acc[:, :], op0=ALU.mult, op1=ALU.add).then_inc(sem["m_acc"], 1)
        dve.wait_ge(sem["m_ps"], 4)
        c = 2 * KT
        dve.tensor_tensor(k.mod[:, c:c + 4 * KT], k.ps[0][:, HALF:HALF + 4 * KT],
                          k.pc[:, PCOL["ada_b"] + c:PCOL["ada_b"] + c + 4 * KT], ALU.add).then_inc(sem["m_done"], 1)

    def pe_prep(pe):
        for m in range(4):
            if m >= 2:
                pe_mod(pe, m - 2)
            for kt in range(KT):
                wait_split(k, pe, b0 + m, kt)
                if m == 0:
                    pe.wait_ge(k.nm["lo"], norm0 + kt + 1)
                for n in range(NH):
                    cols = slice(n * HALF, (n + 1) * HALF)
                    last = passes3(pe, k.ps[m][:, cols], k.w_hi[m % 2][:, kt, :], k.w_lo[m % 2][:, kt, :],
                                   hn_hi[:, kt, cols], hn_lo[:, kt, cols], kt == 0, kt == KT - 1)
            last.then_inc(k.w_used, 1)
        pe.wait_ge(sem["wi_split"], 2)
        pe.wait_ge(sem["evac"], 1)
        for tt in range(TT):
            toks = slice(tt * P, (tt + 1) * P)
            for kt in range(KT):
                last = passes3(pe, k.ps[0][:, tt * 8:tt * 8 + 8], hn_hi[:, kt, toks], hn_lo[:, kt, toks],
                               w_ix_hi[:, kt, :], w_ix_lo[:, kt, :], kt == 0, kt == KT - 1)
        last.then_inc(sem["wi_ps"], 1)
        pe_mod(pe, 2)
        pe_mod(pe, 3)
        pe.wait_ge(sem["sq"], 3)
        pe.wait_ge(sem["evac"], 4)
        for tt in range(TT):
            toks = slice(tt * P, (tt + 1) * P)
            for m in range(2):
                pe.matmul(k.ps[1][:, tt:tt + 1], sq[:, m, toks], k.ones[:, 0:1], start=m == 0, stop=m == 1)
            pe.matmul(k.ps[1][:, TT + tt:TT + tt + 1], sq[:, 2, toks], k.ones[:, 0:1], start=True, stop=True)
            last = pe.matmul(k.ps[1][:, 2 * TT + tt:2 * TT + tt + 1], kidx[:, toks], k.ones[:, 0:1],
                             start=True, stop=True)
        last.then_inc(sem["sum"], 1)
        pe.wait_ge(sem["rinv"], 1)
        pe.wait_ge(sem["wi_done"], 1)
        pe.wait_ge(sem["m_done"], 1)
        for j, dst in ((2, k.ps[0]), (0, k.ps[2]), (1, k.ps[3])):
            for tt in range(TT):
                last = pe.transpose(dst[:, tt * P:(tt + 1) * P],
                                    stat[:, 2, j * TT + tt:j * TT + tt + 1].to_broadcast([P, P]), k.ident[:, :])
            last.then_inc(sem["bcast"], 1)
        pe.wait_ge(sem["sq2"], 1)
        for tt in range(TT):
            last = pe.matmul(k.ps[1][:, tt:tt + 1], sq[:, 0, tt * P:(tt + 1) * P], k.ones[:, 0:1],
                             start=True, stop=True)
        last.then_inc(sem["sum2"], 1)
        pe.wait_ge(sem["rinv2"], 1)
        for tt in range(TT):
            last = pe.transpose(k.ps[1][:, tt * P:(tt + 1) * P],
                                stat[:, 2, 3 * TT + tt:3 * TT + tt + 1].to_broadcast([P, P]), k.ident[:, :])
        last.then_inc(sem["bcast2"], 1)
        pe.wait_ge(sem["lat"], 3)
        for tt in range(TT):
            last = pe.transpose(k.ps[2][:, tt * P:(tt + 1) * P], ckv_t[:, tt * P:(tt + 1) * P], k.ident[:, :])
        last.then_inc(sem["ckv_ps"], 1)
        pe.wait_ge(sem["w_landed"], 16 * 5)
        for m in range(A_HEADS // 2):
            last = pe.transpose(k.ps[3][:, m * P:(m + 1) * P],
                                w_uk[:, 2 * m:2 * m + 2, :].rearrange("p h d -> p (h d)"), k.ident[:, :])
        last.then_inc(sem["uk_ps"], 1)

    def act_prep(act):
        for m, dst in enumerate((q_lat[:, 0, :], q_lat[:, 1, :], ckv_t[:, :], kidx[:, :])):
            block_done(k, act, b0 + m)
            act.activation(dst, k.ps[m][:, :], ACT.Copy).then_inc(sem["evac"], 1)
        act.wait_ge(sem["wi_ps"], 1)
        act.wait_ge(sem["evac"], 3)
        for m, src in enumerate((q_lat[:, 0, :], q_lat[:, 1, :], ckv_t[:, :])):
            act.activation(sq[:, m, :], src, ACT.Square).then_inc(sem["sq"], 1)
        act.wait_ge(sem["ms"], 3)
        act.activation(stat[:, 1, 0:2 * TT], stat[:, 0, 0:2 * TT], ACT.Sqrt).then_inc(sem["root"], 1)
        act.wait_ge(sem["cent"], 1)
        act.wait_ge(sem["sum"], 1)
        act.activation(sq[:, 0, :], kidx[:, :], ACT.Square).then_inc(sem["sq2"], 1)
        act.wait_ge(sem["ms2"], 1)
        act.activation(stat[:, 1, 3 * TT:4 * TT], stat[:, 0, 3 * TT:4 * TT], ACT.Sqrt).then_inc(sem["root2"], 1)
        act.wait_ge(sem["ckv_ps"], 1)
        act.activation(ckv_n[:, :, :].rearrange("p t c -> p (t c)"), k.ps[2][:, :], ACT.Copy).then_inc(sem["ckv_n"], 1)
        act.wait_ge(sem["uk_ps"], 1)
        for h in range(A_HEADS):
            m, half = h // 2, slice(64 * (h % 2), 64 * (h % 2) + 64)
            act.activation(w_uk_t[half, m, :], k.ps[3][half, m * P:(m + 1) * P], ACT.Copy,
                           scale=A_DH ** -0.5 / slope(h)).then_inc(sem["uk_t"], 1)

    def dve_prep(dve):
        dve.wait_ge(sem["w_landed"], 16 * 4)
        dve.tensor_copy(w_ix_hi[:, :, :], w_ix[:, :, :]).then_inc(sem["wi_split"], 1)
        dve.wait_ge(sem["wi_split"], 1)
        dve.tensor_tensor(w_ix_lo[:, :, :], w_ix[:, :, :], w_ix_hi[:, :, :].bitcast(F32), ALU.subtract
                          ).then_inc(sem["wi_split"], 1)
        dve_mods(dve)
        dve.wait_ge(sem["wi_ps"], 1)
        dve.tensor_scalar(wi[:, :, :].rearrange("p t h -> p (t h)"), k.ps[0][:, 0:64],
                          IDX_HEADS ** -0.5 * IDX_DIM ** -0.5, None, ALU.mult).then_inc(sem["wi_done"], 1)
        dve.wait_ge(sem["sum"], 1)
        dve.tensor_scalar(stat[:, 0, 0:TT], k.ps[1][:, 0:TT], 1.0 / Q_RANK, EPS, ALU.mult, ALU.add
                          ).then_inc(sem["ms"], 1)
        dve.tensor_scalar(stat[:, 0, TT:2 * TT], k.ps[1][:, TT:2 * TT], 1.0 / KV_RANK, EPS, ALU.mult, ALU.add
                          ).then_inc(sem["ms"], 1)
        dve.tensor_scalar(stat[:, 2, 2 * TT:3 * TT], k.ps[1][:, 2 * TT:3 * TT], 1.0 / (2 * IDX_DIM), None, ALU.mult
                          ).then_inc(sem["ms"], 1)
        dve.wait_ge(sem["root"], 1)
        dve.reciprocal(stat[:, 2, 0:2 * TT], stat[:, 1, 0:2 * TT]).then_inc(sem["rinv"], 1)
        dve.wait_ge(sem["bcast"], 1)
        dve.tensor_tensor(kidx[:, :], kidx[:, :], k.ps[0][:, :], ALU.subtract).then_inc(sem["cent"], 1)
        for m, (dst, gain) in enumerate(((q_lat[:, 0, :], PCOL["a_q_norm"]), (q_lat[:, 1, :], PCOL["a_q_norm"] + 1),
                                         (ckv_t[:, :], PCOL["a_kv_norm"]))):
            dve.wait_ge(sem["bcast"], 2 if m < 2 else 3)
            dve.scalar_tensor_tensor(out=dst, in0=dst, scalar=k.pc[:, gain:gain + 1],
                                     in1=k.ps[2 if m < 2 else 3][:, :], op0=ALU.mult, op1=ALU.mult
                                     ).then_inc(sem["lat"], 1)
        dve.wait_ge(sem["sum2"], 1)
        dve.tensor_scalar(stat[:, 0, 3 * TT:4 * TT], k.ps[1][:, 0:TT], 1.0 / (2 * IDX_DIM), EPS, ALU.mult, ALU.add
                          ).then_inc(sem["ms2"], 1)
        dve.wait_ge(sem["root2"], 1)
        dve.reciprocal(stat[:, 2, 3 * TT:4 * TT], stat[:, 1, 3 * TT:4 * TT]).then_inc(sem["rinv2"], 1)
        dve.wait_ge(sem["bcast2"], 1)
        dve.scalar_tensor_tensor(out=kidx[:, :], in0=kidx[:, :], scalar=k.pc[:, PCOL["kidx_g"]:PCOL["kidx_g"] + 1],
                                 in1=k.ps[1][:, :], op0=ALU.mult, op1=ALU.mult).then_inc(sem["kidx"], 1)
        dve.wait_ge(sem["kidx"], 1)
        dve.tensor_scalar(kidx[:, :], kidx[:, :], k.pc[:, PCOL["kidx_b"]:PCOL["kidx_b"] + 1], None, ALU.add
                          ).then_inc(sem["kidx"], 1)

    k.parts["sp"].append(sp_part)
    k.parts["pe"].append(pe_prep)
    k.parts["act"].append(act_prep)
    k.parts["dve"].append(dve_prep)
    stage_end(k)
    prep_done = 3 * k.stages

    def banks(s, i):
        return k.ps[(i + i // 2 if s + 2 in INDEXED else i) % 2]

    def pe_step(pe, s):
        n, qs = keys(s), slice(s * P, (s + 1) * P)
        if s:
            pe.wait_ge(sem["x_max"], 16 * s)
            pe.wait_ge(sem["p_sb"], 16 * s)
            pe.wait_ge(sem["ol_sb"], 16 * s)
            pe.wait_ge(sem["o_sb"], 8 * s)
        for m in range(A_HEADS // 2):
            for t in range(2):
                last = pe.matmul(k.ps[0][:, m * P:(m + 1) * P], w_uq[:, t, m * P:(m + 1) * P], q_lat[:, t, qs],
                                 start=t == 0, stop=t == 1)
        last.then_inc(sem["qT_ps"], 1)
        indexed = s + 2 in INDEXED
        if indexed:
            qs2 = slice((s + 2) * P, (s + 3) * P)
            for m in range(IDX_HEADS // 2):
                for t in range(2):
                    last = pe.matmul(k.ps[1][:, m * P:(m + 1) * P], w_qi[:, t, m * P:(m + 1) * P],
                                     q_lat[:, t, qs2], start=t == 0, stop=t == 1)
            last.then_inc(sem["qi_ps"], 1)
        pe.wait_ge(sem["qT_sb"], s + 1)
        for parity in range(2):
            half = slice(64 * parity, 64 * parity + 64)
            for m in range(A_HEADS // 2):
                last = pe.matmul(k.ps[2 + parity][:, m * P:(m + 1) * P], w_uk_t[half, m, :], q_t[half, m, :],
                                 start=True, stop=True)
            last.then_inc(sem["qa_ps"], 1)
        uses = 0
        for i in range(A_HEADS + 4):
            if i < A_HEADS:
                A = 16 * s + i
                if i >= 2:
                    pe.wait_ge(sem["x_max"], A - 1 if not indexed or i % 2 == 0 else A)
                if indexed and i >= 2:
                    pe.wait_ge(sem["relu"], 8 * s + i // 2)
                pe.wait_ge(sem["qa_sb"], 2 * s + (1 if i == 0 else 2))
                for c in range(0, n, HALF):
                    e = min(c + HALF, n)
                    last = pe.matmul(k.ps[uses % 2][:, c:e], q_abs[:, i % 2, i // 2, :], ckv_t[:, c:e],
                                     start=True, stop=True)
                last.then_inc(sem["qk_ps"], 1)
                uses += 1
            if indexed and i < A_HEADS and i % 2 == 1:
                pe.wait_ge(sem["qi_sb"], s + 1)
                pe.wait_ge(sem["x_max"], A)
                j, n2 = i // 2, keys(s + 2)
                half = slice(64 * (j % 2), 64 * (j % 2) + 64)
                for c in range(0, n2, HALF):
                    e = min(c + HALF, n2)
                    last = pe.matmul(k.ps[uses % 2][:, c:e], qi_t[half, j // 2, :], kidx[half, c:e],
                                     start=True, stop=True)
                last.then_inc(sem["sc_ps"], 1)
                uses += 1
            if 0 <= i - 3 < A_HEADS:
                A = 16 * s + i - 3
                pe.wait_ge(sem["p_sb"], A + 1)
                if A:
                    pe.wait_ge(sem["ol_sb"], A)
                else:
                    pe.wait_ge(sem["qa_sb"], 2)
                for kt in range(s + 1):
                    last = pe.matmul(k.ps[3][:, 0:P], ckv_n[:, kt, :], p_t[A % 2][:, kt, :],
                                     start=kt == 0, stop=kt == s)
                last.then_inc(sem["ol_ps"], 1)
            if 0 <= i - 2 < A_HEADS:
                A = 16 * s + i - 2
                pe.wait_ge(sem["x_norm"], A + 1)
                pe.wait_ge(sem["qa_sb"], 2 * s + 2)
                if A:
                    pe.wait_ge(sem["p_sb"], A)
                for kt in range(s + 1):
                    last = pe.matmul(k.ps[2][:, kt * P:(kt + 1) * P], x[A % 3][:, kt * P:(kt + 1) * P],
                                     diag[A % 2][:, :], start=True, stop=True)
                last.then_inc(sem["p_ps"], 1)
            if 0 <= i - 4 < A_HEADS:
                h = i - 4
                A = 16 * s + h
                pe.wait_ge(sem["ol_sb"], A + 1)
                if h % 2 == 0 and A:
                    pe.wait_ge(sem["o_sb"], A // 2)
                pe.matmul(k.ps[3][64 * (h % 2):64 * (h % 2) + 64, HALF:HALF + P], w_uv[:, h, :],
                          o_lat[A % 2][:, :], start=True, stop=True).then_inc(sem["o_ps"], 1)

    def act_step(act, s):
        n = keys(s)
        act.wait_ge(sem["qT_ps"], s + 1)
        act.activation(q_t[:, :, :].rearrange("p m q -> p (m q)"), k.ps[0][:, :], ACT.Copy).then_inc(sem["qT_sb"], 1)
        indexed = s + 2 in INDEXED
        if indexed:
            act.wait_ge(sem["qi_ps"], s + 1)
            act.activation(qi_t[:, :, :].rearrange("p m q -> p (m q)"), k.ps[1][:, 0:HALF], ACT.Copy
                           ).then_inc(sem["qi_sb"], 1)
        for half in range(2):
            act.wait_ge(sem["qa_ps"], 2 * s + 1 + half)
            act.activation(q_abs[:, half, :, :].rearrange("p h q -> p (h q)"), k.ps[2 + half][:, :],
                           ACT.Copy).then_inc(sem["qa_sb"], 1)
        if s + 1 < TT:
            act.wait_ge(sem["iota"], s + 2)
            act.activation(dist[(s + 1) % 2][:, 0:keys(s + 1)], dist[(s + 1) % 2][:, 0:keys(s + 1)], ACT.Abs
                           ).then_inc(sem["dist"], 1)
        for i in range(A_HEADS + 4):
            if i < A_HEADS:
                A = 16 * s + i
                act.wait_ge(sem["x_max"], A + 1)
                act.activation(small[:, 1, i:i + 1], small[:, 0, i:i + 1], ACT.Copy, scale=-slope(i)
                               ).then_inc(sem["nbias"], 1)
                act.wait_ge(sem["nbias"], A + 1)
                act.activation(x[A % 3][:, 0:n], x[A % 3][:, 0:n], ACT.Exp, bias=small[:, 1, i:i + 1], scale=slope(i),
                               accum_out=small[:, 2, i:i + 1]).then_inc(sem["x_exp"], 1)
            if indexed and i < A_HEADS and i % 2 == 1:
                j, n2 = i // 2, keys(s + 2)
                act.wait_ge(sem["sc_ps"], 8 * s + j + 1)
                if 8 * s + j >= 2:
                    act.wait_ge(sem["acc"], 8 * s + j - 1)
                act.activation(rel[j % 2][:, 0:n2], k.ps[(i + j + 1) % 2][:, 0:n2], ACT.Relu).then_inc(sem["relu"], 1)
                act.wait_ge(sem["relu"], 8 * s + j + 1)
                col = wi[:, s + 2, j:j + 1]
                if j == 0:
                    act.wait_ge(sem["mask_d"], s + 1)
                    act.activation(work[s % 2][:, 0:n2], rel[0][:, 0:n2], ACT.Copy, scale=col).then_inc(sem["acc"], 1)
                else:
                    act.activation(rel[j % 2][:, 0:n2], rel[j % 2][:, 0:n2], ACT.Copy, scale=col
                                   ).then_inc(sem["scaled"], 1)
            if 0 <= i - 2 < A_HEADS:
                A = 16 * s + i - 2
                act.wait_ge(sem["p_ps"], A + 1)
                if A >= 2:
                    act.wait_ge(sem["ol_ps"], A - 1)
                act.activation(p_t[A % 2][:, 0:s + 1, :].rearrange("p t q -> p (t q)"), k.ps[2][:, 0:n], ACT.Copy
                               ).then_inc(sem["p_sb"], 1)
            if 0 <= i - 3 < A_HEADS:
                A = 16 * s + i - 3
                act.wait_ge(sem["ol_ps"], A + 1)
                if A >= 2:
                    act.wait_ge(sem["o_ps"], A - 1)
                act.activation(o_lat[A % 2][:, :], k.ps[3][:, 0:P], ACT.Copy).then_inc(sem["ol_sb"], 1)
            if 0 <= i - 4 < A_HEADS and i % 2 == 1:
                h = i - 4
                act.wait_ge(sem["o_ps"], 16 * s + h + 1)
                act.activation(o_t[:, h // 2, s * P:(s + 1) * P], k.ps[3][:, HALF:HALF + P], ACT.Copy
                               ).then_inc(sem["o_sb"], 1)

    def dve_step(dve, s):
        n, n1 = keys(s), keys(s + 1)
        searching = s + 1 in INDEXED
        w1 = work[(s + 1) % 2][:, 0:n1] if searching else None
        if searching:
            dve.wait_ge(sem["mask"], s)
            t0 = (TOPK // 8) * (s + 1 - TOPK // P)

        def search(r):
            if t0 + r:
                dve.wait_ge(sem["take"], t0 + r)
            dve.max(top8[:, :], w1).then_inc(sem["top"], 1)
            dve.wait_ge(sem["top"], t0 + r + 1)
            dve.match_replace(w1, top8[:, :], w1, TAKEN).then_inc(sem["take"], 1)

        rounds = 0
        if searching:
            for rounds in range(EARLY):
                search(rounds)
            rounds = EARLY
        for i in range(A_HEADS):
            A = 16 * s + i
            dve.wait_ge(sem["qk_ps"], A + 1)
            if A >= 3:
                dve.wait_ge(sem["p_ps"], A - 2)
            if i == 0:
                dve.wait_ge(sem["dist"], s + 1)
                dve.wait_ge(sem["mask_d"], s + 1)
            dve.tensor_tensor_reduce(x[A % 3][:, 0:n], banks(s, i)[:, 0:n], dist[s % 2][:, 0:n], 1.0, TAKEN,
                                     ALU.subtract, ALU.max, small[:, 0, i:i + 1]).then_inc(sem["x_max"], 1)
            if searching:
                upto = EARLY + ((TOPK // 8 - EARLY) * (i + 1)) // A_HEADS
                while rounds < upto:
                    search(rounds)
                    rounds += 1
            if i >= 1:
                dve.wait_ge(sem["x_exp"], A)
                dve.reciprocal(small[:, 3, i - 1:i], small[:, 2, i - 1:i]).then_inc(sem["rinv_h"], 1)
        dve.wait_ge(sem["x_exp"], 16 * s + 16)
        dve.reciprocal(small[:, 3, 15:16], small[:, 2, 15:16]).then_inc(sem["rinv_h"], 1)
        if s + 2 in INDEXED:
            n2 = keys(s + 2)
            dve.wait_ge(sem["acc"], 8 * s + 8)
            dve.memset(work[s % 2][0:CHUNK, n2 - CHUNK:n2], INADMISSIBLE).then_inc(sem["mask"], 1)
        if s + 1 < TT:
            finish_dist(dve, s + 1)

    def finish_dist(dve, s):
        n, d = keys(s), dist[s % 2]
        dve.wait_ge(sem["dist"], s + 1)
        if s in INDEXED:
            w = work[s % 2][:, 0:n]
            dve.wait_ge(sem["take"], (TOPK // 8) * (s + 1 - TOPK // P))
            dve.tensor_scalar(w, w, (INADMISSIBLE + TAKEN) / 2, UNSELECTED, ALU.is_gt, ALU.mult
                              ).then_inc(sem["unsel"], 1)
            dve.wait_ge(sem["unsel"], s + 1 - TOPK // P)
            dve.tensor_tensor(d[:, 0:n], d[:, 0:n], w, ALU.add).then_inc(sem["mask_d"], 1)
        else:
            dve.memset(d[0:CHUNK, n - CHUNK:n], UNSELECTED).then_inc(sem["mask_d"], 1)


    def pool_step(pool, s):
        if s + 1 < TT:
            if s:
                pool.wait_ge(sem["x_max"], 16 * s)
            pool.iota(dist[(s + 1) % 2][:, 0:keys(s + 1)], [[-1, keys(s + 1)]], base=(s + 1) * P,
                      channel_multiplier=1, allow_small_or_imprecise_dtypes=True).then_inc(sem["iota"], 1)
        for i in range(A_HEADS):
            A = 16 * s + i
            pool.wait_ge(sem["rinv_h"], A + 1)
            if A >= 2:
                pool.wait_ge(sem["p_ps"], A - 1)
            pool.tensor_scalar(diag[A % 2][:, :], k.ident[:, :], small[:, 3, i:i + 1], None, ALU.mult
                               ).then_inc(sem["x_norm"], 1)
            if s + 2 in INDEXED and i % 2 == 1 and i > 1:
                j, n2 = i // 2, keys(s + 2)
                w = work[s % 2][:, 0:n2]
                pool.wait_ge(sem["scaled"], 7 * s + j)
                pool.wait_ge(sem["acc"], 8 * s + j)
                pool.tensor_tensor(w, w, rel[j % 2][:, 0:n2], ALU.add).then_inc(sem["acc"], 1)

    def pool_attention(pool):
        pool.wait_ge(k.stage_done, prep_done)
        pool.iota(dist[0][:, 0:P], [[-1, P]], base=0, channel_multiplier=1,
                  allow_small_or_imprecise_dtypes=True).then_inc(sem["iota"], 1)
        for s in range(TT):
            pool_step(pool, s)

    def act_attention(act):
        act.wait_ge(sem["iota"], 1)
        act.activation(dist[0][:, 0:P], dist[0][:, 0:P], ACT.Abs).then_inc(sem["dist"], 1)
        for s in range(TT):
            act_step(act, s)

    def dve_attention(dve):
        finish_dist(dve, 0)
        for s in range(TT):
            dve_step(dve, s)

    def pe_attention(pe):
        for s in range(TT):
            pe_step(pe, s)

    k.parts["pool"].append(pool_attention)
    k.parts["pe"].append(pe_attention)
    k.parts["act"].append(act_attention)
    k.parts["dve"].append(dve_attention)
    stage_end(k)

    def clear(dve):
        for s in list(sem.values()) + m_landed:
            dve.sem_clear(s)

    k.parts["dve"].append(clear)
    lo_done = split_tiles(k, "d_o", o_t, o_hi, o_lo)
    project_residual(k, "d", a.a_w_o[0].rearrange("(k p) n -> p k n", p=P), o_hi, o_lo, lo_done, mod_col(0, 2))
    stage_end(k)
    sems.close()


DECAY_C = 0.6065306597126334
PAIRS = KT
R_, K_, V_, W_, A_, G_ = range(6)


def rwkv_project(k, a, scr):
    nc = k.nc
    st = ExitStack()
    sb = lambda name, shape, dt=F32: st.enter_context(nc.sbuf_tensor("rp_" + name, shape, dt))
    sem = {n: k.sem("rp_" + n) for n in ("zero", "omu", "t", "x", "hi", "lo", "hid", "gh_lo", "ev", "w2", "sec")}
    stored = [k.sem(f"rp_stored{i}") for i in range(2)]
    before = 3 * k.stages
    hn = sb("hn", [P, KT, S + 1])
    omu = sb("omu", [P, 48])
    wa2 = sb("wa2", [P, D])
    wa_h = sb("wa_h", [P, S])
    stage = [sb(f"stage{i}", [P, S]) for i in range(2)]
    norm_stage(k, PCOL["norm_mix"] + KT, 1, 0, plain=lambda kt: hn[:, kt, 1:S + 1])
    hi0 = k.norm_hi
    x_hi, x_lo = sb("x_hi", [P, KT, S], F32R), sb("x_lo", [P, KT, S], F32R)
    t = [sb(f"t{i}", [P, S]) for i in range(2)]
    x = [sb(f"x{i}", [P, S]) for i in range(2)]
    g_hi, g_lo = sb("g_hi", [P, S], F32R), sb("g_lo", [P, S], F32R)
    st.close()

    def sp_part(sp):
        sp.wait_ge(k.stage_done, before)
        sp.dma_start(wa2[0:64, :], a.b_w2[0]).then_inc(sem["w2"], 16)
        sp.dma_start(wa2[64:P, :], a.b_a2[0]).then_inc(sem["w2"], 16)

    k.parts["sp"].append(sp_part)
    v = lambda w: w[0].rearrange("(k p) n -> p k n", p=P)
    b0 = stream_pieces(k, [[(0, 64, v(a.b_w1)), (64, P, v(a.b_w1))], [(0, 64, v(a.b_a1)), (64, P, v(a.b_a1))],
                           [(0, P, v(a.b_g1))], [(0, P, a.b_g2[0].rearrange("p (m n) -> p m n", n=P))]])
    big = []
    for w in (a.b_w_r, a.b_w_k, a.b_w_v):
        big.append(stream_weights(k, KT, lambda i, s, w=w: v(w)[:, :, bass.ds(i * (2 * P) + s * P, P)]))
    mixes = [(1, None), (4, b0), (5, b0 + 1), (0, b0 + 2), (2, big[0] + KT - 1), (3, big[1] + KT - 1)]

    def x_t(act, j, kt):
        n, c = KT * j + kt, mixes[j][0] * 8 + kt
        if n >= 2:
            act.wait_ge(sem["x"], n - 1)
        act.activation(t[n % 2][:, :], hn[:, kt, 1:S + 1], ACT.Copy, scale=omu[:, c:c + 1]).then_inc(sem["t"], 1)

    def x_act(act, j, kt):
        n, prev = KT * j + kt, mixes[j][1]
        act.wait_ge(sem["x"], n + 1)
        if kt == 0 and prev is not None:
            block_done(k, act, prev)
        act.activation(x_hi[:, kt, :], x[n % 2][:, :], ACT.Copy).then_inc(sem["hi"], 1)
        if kt < KT - 2:
            x_t(act, j, kt + 2)

    def x_ahead(act, j):
        for kt in range(2):
            x_t(act, j, kt)

    def x_dve(dve, j):
        def mixed(kt):
            n, c = KT * j + kt, PCOL["b_mu"] + mixes[j][0] * 8 + kt
            dve.wait_ge(sem["t"], n + 1)
            if n >= 2:
                dve.wait_ge(sem["lo"], n - 1)
            dve.scalar_tensor_tensor(out=x[n % 2][:, :], in0=hn[:, kt, 0:S], scalar=k.pc[:, c:c + 1],
                                     in1=t[n % 2][:, :], op0=ALU.mult, op1=ALU.add).then_inc(sem["x"], 1)

        mixed(0)
        mixed(1)
        for kt in range(KT):
            n = KT * j + kt
            dve.wait_ge(sem["hi"], n + 1)
            dve.tensor_tensor(x_lo[:, kt, :], x[n % 2][:, :], x_hi[:, kt, :].bitcast(F32), ALU.subtract
                              ).then_inc(sem["lo"], 1)
            if kt < KT - 2:
                mixed(kt + 2)

    def product(pe, out, slot, j, b):
        for kt in range(KT):
            wait_split(k, pe, b, kt)
            pe.wait_ge(sem["lo"], KT * j + kt + 1)
            for n in range(NH):
                cols = slice(n * HALF, (n + 1) * HALF)
                last = passes3(pe, out[:, cols], k.w_hi[slot][:, kt, :], k.w_lo[slot][:, kt, :],
                               x_hi[:, kt, cols], x_lo[:, kt, cols], kt == 0, kt == KT - 1)
        return last

    def pe_part(pe):
        for j in range(3):
            if j == 2:
                pe.wait_ge(sem["hid"], 1)
            product(pe, k.ps[2 + j % 2], j % 2, j, b0 + j).then_inc(k.w_used, 1)
        for o in range(2 * KT):
            half, m = slice(64 * (o // KT), 64 * (o // KT) + 64), o % KT
            if o == 0:
                pe.wait_ge(sem["hid"], 2)
                pe.wait_ge(sem["w2"], 32)
            pe.wait_ge(sem["ev"], o + 1)
            for n in range(NH):
                cols = slice(n * HALF, (n + 1) * HALF)
                last = pe.matmul(k.ps[o % 2][:, cols], wa2[half, m * P:(m + 1) * P], wa_h[half, cols],
                                 start=True, stop=True)
            last.then_inc(sem["sec"], 1)
        pe.wait_ge(sem["gh_lo"], 1)
        wait_split(k, pe, b0 + 3)
        for m in range(KT):
            o = 2 * KT + m
            pe.wait_ge(sem["ev"], o + 1)
            for n in range(NH):
                cols = slice(n * HALF, (n + 1) * HALF)
                last = passes3(pe, k.ps[o % 2][:, cols], k.w_hi[1][:, m, :], k.w_lo[1][:, m, :],
                               g_hi[:, cols], g_lo[:, cols], True, True)
            last.then_inc(sem["sec"], 1)
        pe.wait_ge(sem["ev"], 3 * KT + 2)
        pe.sem_inc(k.w_used, 1)
        for j, bb in enumerate(big):
            with pe.Fori(0, KT // 2) as i:
                for s in range(2):
                    pe.wait_ge(sem["ev"], i * 2 + (3 * KT + KT * j + s + 1))
                    product(pe, k.ps[s], s, 3 + j, i * 2 + (bb + s)).then_inc(k.w_used, 1)

    def act_part(act):
        act.sem_inc(sem["ev"], 2)
        for i in range(2):
            act.sem_inc(stored[i], 16)
        act.wait_ge(k.nm["hi"], hi0)
        act.wait_ge(sem["zero"], 1)
        act.wait_ge(sem["omu"], 1)
        x_ahead(act, 0)
        for j in range(3):
            for kt in range(KT):
                x_act(act, j, kt)
            if j < 2:
                x_ahead(act, j + 1)
            block_done(k, act, b0 + j)
            if j == 0:
                act.activation(wa_h[0:64, :], k.ps[2][0:64, :], ACT.Tanh).then_inc(sem["hid"], 1)
            elif j == 1:
                act.activation(wa_h[64:P, :], k.ps[3][64:P, :], ACT.Copy).then_inc(sem["hid"], 1)
            else:
                act.activation(t[0][:, :], k.ps[2][:, :], ACT.Sigmoid).then_inc(sem["hid"], 1)
                act.wait_ge(sem["hid"], 3)
                act.activation(g_hi[:, :], t[0][:, :], ACT.Copy).then_inc(sem["hid"], 1)
        for o in range(3 * KT):
            row, m, slot = (W_, A_, G_)[o // KT], o % KT, o % 2
            act.wait_ge(sem["sec"], o + 1)
            act.wait_ge(stored[slot], 16 * (o // 2) + 16)
            if row == G_:
                act.activation(stage[slot][:, :], k.ps[slot][:, :], ACT.Copy).then_inc(sem["ev"], 1)
            else:
                c = PCOL["b_w0" if row == W_ else "b_a0"] + m
                act.activation(stage[slot][:, :], k.ps[slot][:, :], ACT.Sigmoid, bias=k.pc[:, c:c + 1]
                               ).then_inc(sem["ev"], 1)
            act.wait_ge(sem["ev"], o + 3)
            act.dma_start(scr[row, m, :, :], stage[slot][:, :]).then_inc(stored[slot], 16)
            if o == 0:
                act.wait_ge(sem["gh_lo"], 1)
                x_ahead(act, 3)
            if o % 3 == 2:
                x_act(act, 3, o // 3)
        for j, row in enumerate((R_, K_, V_)):
            if j:
                for kt in range(KT):
                    x_act(act, 3 + j, kt)
            if j < 2:
                x_ahead(act, 4 + j)
            with act.Fori(0, KT // 2) as i:
                for s in range(2):
                    block_done(k, act, i * 2 + (big[j] + s))
                    act.wait_ge(stored[s], i * 16 + (16 * (3 + j) * KT // 2 + 16))
                    act.activation(stage[s][:, :], k.ps[s][:, :], ACT.Copy).then_inc(sem["ev"], 1)
                    act.wait_ge(sem["ev"], i * 2 + (3 * KT + KT * j + s + 3))
                    act.dma_start(scr[row, bass.ds(i * 2 + s, 1), :, :].rearrange("m p t -> (m p) t"),
                                  stage[s][:, :]).then_inc(stored[s], 16)
        for i in range(2):
            act.wait_ge(stored[i], 16 * 3 * KT + 16)

    def dve_part(dve):
        dve.memset(hn[:, :, 0:1], 0.0).then_inc(sem["zero"], 1)
        c = PCOL["b_mu"]
        dve.tensor_scalar(omu[:, :], k.pc[:, c:c + 48], -1.0, 1.0, ALU.mult, ALU.add).then_inc(sem["omu"], 1)
        for j in range(3):
            x_dve(dve, j)
        dve.wait_ge(sem["hid"], 4)
        dve.tensor_tensor(g_lo[:, :], t[0][:, :], g_hi[:, :].bitcast(F32), ALU.subtract).then_inc(sem["gh_lo"], 1)
        for j in range(3, 6):
            x_dve(dve, j)

    k.parts["pe"].append(pe_part)
    k.parts["act"].append(act_part)
    k.parts["dve"].append(dve_part)
    stage_end(k)


def rwkv_stage(k, a):
    nc = k.nc
    scr = nc.dram_tensor("rwkv_scratch", (6, PAIRS, P, S), F32, kind="Internal").ap()
    yscr = nc.dram_tensor("rwkv_y", (PAIRS, P, S), F32, kind="Internal").ap()
    begin = 3 * k.stages
    st = consts = ExitStack()
    sb = lambda name, shape, dt=F32: st.enter_context(nc.sbuf_tensor("rc_" + name, shape, dt))
    upper = sb("upper", [P, 2, P])
    diag = sb("diag", [P, P])
    level = sb("level", [P, 6, 2 * P], U8)
    carry = sb("carry", [P, S], mybir.dt.bfloat16)
    heads2 = sb("heads2", [P, 2])
    omka = sb("omka", [P, PAIRS])
    mask = sb("mask", [P, 2 * P])
    const, masks = k.sem("rc_const"), k.sem("rc_masks")

    def pool_const(pool):
        pool.wait_ge(k.stage_done, begin)
        n = [0]

        def done(ins):
            n[0] += 1
            ins.then_inc(const, 1)
            pool.wait_ge(const, n[0])
        done(pool.memset(upper[:, :, :], 1.0))
        for i in range(2):
            done(pool.affine_select(out=upper[:, i, :], in_=upper[:, i, :], compare_op=ALU.is_ge if i else ALU.is_gt, fill=0.0, base=0, pattern=[[1, P]], channel_multiplier=-1))
        done(pool.memset(upper[0:CHUNK, :, CHUNK:P], 0.0))
        done(pool.memset(diag[:, :], 0.0))
        done(pool.memset(heads2[:, :], 0.0))
        for h in range(2):
            half = slice(64 * h, 64 * h + 64)
            done(pool.memset(diag[half, half], 1.0))
            done(pool.memset(heads2[half, h:h + 1], 1.0))
        done(pool.memset(carry[:, :], 1.0))
        done(pool.memset(carry[:, :].rearrange("p (c t) -> p c t", t=CHUNK)[:, :, 0:1], 0.0))
        for lv in range(6):
            half, full = 1 << lv, 2 << lv
            nb = P // full
            f = mask[:, :]
            done(pool.memset(f, 0.0))
            for part in range(2):
                view = f[:, part * P:(part + 1) * P].rearrange("p (b s w) -> p b s w", s=2, w=half)[:, :, 1 - part, :]
                done(pool.memset(view, 1.0))
                lo = part * half
                done(pool.affine_select(out=view, in_=view, compare_op=ALU.is_ge, fill=0.0, base=-lo,
                                        pattern=[[-full, nb], [0, half]], channel_multiplier=1))
                done(pool.affine_select(out=view, in_=view, compare_op=ALU.is_ge, fill=0.0, base=lo + half - 1,
                                        pattern=[[full, nb], [0, half]], channel_multiplier=-1))
            done(pool.tensor_copy(level[:, lv, :], f))
        pool.sem_inc(masks, 1)

    k.parts["pool"].append(pool_const)
    rwkv_project(k, a, scr)
    before = 3 * k.stages
    st = ExitStack()
    BLK = S // P
    raw = sb("raw", [P, 4, S])
    r_in, k_in, w_in, a_in = (raw[:, i, :] for i in range(4))
    v_t = [sb(f"v_t{i}", [P, S]) for i in range(2)]
    ar = [sb(f"ar{i}", [P, BLK, 2, P]) for i in range(2)]
    b_t = [sb(f"b_t{i}", [P, S]) for i in range(2)]
    k_t = [sb(f"k_t{i}", [P, S]) for i in range(2)]
    b_e = [sb(f"b_e{i}", [P, S]) for i in range(2)]
    k_e = [sb(f"k_e{i}", [P, S]) for i in range(2)]
    p_end = [sb(f"p_end{i}", [P, 2 * BLK]) for i in range(2)]
    bonus = [sb(f"bonus{i}", [P, 2 * BLK]) for i in range(2)]
    gng = [sb(f"gng{i}", [P, P]) for i in range(2)]
    dec = sb("dec", [P, S])
    kk = sb("kk", [P, S])
    km = sb("km", [P, S])
    cum = sb("cum", [P, S])
    sm = sb("sm", [P, 8, 2 * BLK])
    rkw = sb("rkw", [P, 2])
    v_n = [sb(f"v_n{i}", [P, BLK, P]) for i in range(2)]
    y_n = [sb(f"y_n{i}", [P, BLK, P]) for i in range(2)]
    g_in = sb("g_in", [P, S])
    tmp = sb("tmp", [P, S])
    au = [sb(f"au{x}", [P, 2, P]) for x in range(2)]
    bk = [sb(f"bk{x}", [P, 2, P]) for x in range(2)]
    gm = [sb(f"gm{x}", [P, 2, 4, P]) for x in range(2)]
    n_t = [sb(f"n_t{x}", [P, 2, P]) for x in range(2)]
    xx = [sb(f"xx{x}", [P, 2, 2, P]) for x in range(2)]
    z = [sb(f"z{x}", [P, 2, P]) for x in range(2)]
    wu = [sb(f"wu{x}", [P, 2, P]) for x in range(2)]
    q_t = [sb(f"q_t{x}", [P, P]) for x in range(2)]
    mg = [[sb(f"mg{x}_{c}", [P, 2, P]) for c in range(2)] for x in range(2)]
    gp = sb("gp", [P, P])
    state = [sb(f"state{i}", [P, P]) for i in range(2)]
    st.close()
    y_t = st.enter_context(nc.sbuf_tensor("rc_y_t", [P, KT, S], F32))
    y_hi = st.enter_context(nc.sbuf_tensor("rc_y_hi", [P, KT, S], F32R))
    y_lo = st.enter_context(nc.sbuf_tensor("rc_y_lo", [P, KT, S], F32R))
    st.close()

    def bank(i):
        return k.ps[i // 2][:, (i % 2) * HALF:(i % 2 + 1) * HALF]

    sem = {n: k.sem("rc_" + n) for n in (
        "raw", "g", "store", "omka",
        "sq", "scan", "km1", "km", "cump", "sum", "nmax", "nrec", "nroot", "exp", "bc", "kk", "b", "pend", "out",
        "rkw", "bon_ps", "bon",
        "s1", "mean", "yc", "ysq", "s2", "var", "vroot", "vrec", "yn", "gn", "bv", "z", "tp", "y",
        "seen", "zero", "s_ps", "gp", "s_new")}
    for n in ("t_ps", "t_sb", "g_ps", "g_sb", "n_sb", "x_up", "z_ps", "z_sb", "x_ps", "up_ps", "up_sb",
              "wu_ps", "wu_sb", "q_ps", "q_sb", "mg_ps", "mg_sb", "y_ps", "y_sb"):
        sem[n] = [k.sem(f"rc_{n}{x}") for x in range(2)]
    v_ld = [k.sem(f"rc_v_ld{i}") for i in range(2)]
    gn_ld = [k.sem(f"rc_gn_ld{i}") for i in range(2)]

    def dve_const(dve):
        c = PCOL["b_k_a"]
        dve.tensor_scalar(omka[:, :], k.pc[:, c:c + PAIRS], -1.0, 1.0, ALU.mult, ALU.add).then_inc(sem["omka"], 1)

    def sp_part(sp):
        sp.wait_ge(k.stage_done, before)
        for p in range(PAIRS):
            if p:
                sp.wait_ge(sem["out"], 7 * p)
                sp.wait_ge(sem["bon_ps"], p)
            for i, row in enumerate((R_, K_, W_, A_)):
                sp.dma_start(raw[:, i, :], scr[row, p, :, :]).then_inc(sem["raw"], 16)
            if p >= 2:
                for x in range(2):
                    sp.wait_ge(sem["t_ps"][x], 4 * (p - 1))
                sp.wait_ge(sem["gn"], p - 1)
            sp.dma_start(v_t[p % 2][:, :], scr[V_, p, :, :]).then_inc(v_ld[p % 2], 16)
            sp.dma_start(gng[p % 2][:, :], a.b_gn_g[0:1, p * P:(p + 1) * P].to_broadcast([P, P])
                         ).then_inc(gn_ld[p % 2], 16)
            if p >= 2:
                store(sp, p - 2)
            if p >= 1:
                sp.dma_start(g_in[:, :], scr[G_, p - 1, :, :]).then_inc(sem["g"], 16)
        store(sp, PAIRS - 2)
        sp.dma_start(g_in[:, :], scr[G_, PAIRS - 1, :, :]).then_inc(sem["g"], 16)
        store(sp, PAIRS - 1)

    def store(sp, p):
        sp.wait_ge(sem["y"], p + 1)
        sp.dma_start(yscr[p, :, :], g_in[:, :]).then_inc(sem["store"], 16)
        sp.wait_ge(sem["store"], 16 * (p + 1))

    def first(q, n=1):
        return isinstance(q, int) and q < n

    def col(name, q):
        return k.pc[:, bass.ds(q + PCOL[name], 1)]

    def prep_act(act, q, u, piece):
        if piece == 0:
            act.wait_ge(sem["raw"], q * 64 + 64)
            if not first(q):
                act.wait_ge(sem["pend"], q)
            act.activation(dec[:, :], k_in, ACT.Square, scale=col("b_k_k", q)).then_inc(sem["sq"], 1)
        elif piece == 1:
            act.wait_ge(sem["nrec"], q + 1)
            act.activation(sm[:, 2, :], sm[:, 1, :], ACT.Sqrt).then_inc(sem["nroot"], 1)
            act.wait_ge(sem["sum"], q + 1)
            act.wait_ge(sem["cump"], q + 1)
            act.activation(dec[:, :], cum[:, :], ACT.Exp, scale=-DECAY_C).then_inc(sem["exp"], 1)
            act.activation(w_in, w_in, ACT.Exp, scale=-DECAY_C).then_inc(sem["exp"], 1)
        elif piece == 2:
            act.wait_ge(sem["exp"], q * 3 + 2)
            act.activation(cum[:, :], cum[:, :], ACT.Exp, scale=DECAY_C).then_inc(sem["exp"], 1)
            if not first(q, 2):
                act.wait_ge(sem["s_new"], q * 16 - 16)
            act.activation(p_end[u][:, :].unsqueeze(2),
                           dec[:, :].rearrange("p (c t) -> p c t", t=CHUNK)[:, :, CHUNK - 1:CHUNK], ACT.Copy
                           ).then_inc(sem["pend"], 1)

    def prep_dve(dve, q, u, piece):
        if piece == 0:
            dve.wait_ge(sem["raw"], q * 64 + 64)
            dve.tensor_tensor_scan(cum[:, :], carry[:, :], w_in, 0.0, ALU.mult, ALU.add).then_inc(sem["scan"], 1)
            dve.tensor_scalar(km[:, :], a_in, col("b_k_a", q), omka[:, bass.ds(q, 1)], ALU.mult, ALU.add
                              ).then_inc(sem["km1"], 1)
            dve.tensor_scalar(rkw[:, :], heads2[:, :], col("b_r_k", q), None, ALU.mult).then_inc(sem["rkw"], 1)
        elif piece == 1:
            dve.wait_ge(sem["sum"], q + 1)
            dve.tensor_scalar(sm[:, 0, :], k.ps[3][:, 0:2 * BLK], 1e-24, None, ALU.max).then_inc(sem["nmax"], 1)
            dve.wait_ge(sem["nmax"], q + 1)
            dve.reciprocal(sm[:, 1, :], sm[:, 0, :]).then_inc(sem["nrec"], 1)
        elif piece == 2:
            dve.wait_ge(sem["bc"], q + 1)
            dve.scalar_tensor_tensor(out=kk[:, :], in0=k_in, scalar=col("b_k_k", q), in1=k.ps[3][:, :],
                                     op0=ALU.mult, op1=ALU.mult).then_inc(sem["kk"], 1)
            dve.wait_ge(sem["kk"], q + 1)
            dve.scalar_tensor_tensor(out=a_in, in0=kk[:, :], scalar=-1.0, in1=a_in, op0=ALU.mult, op1=ALU.mult
                                     ).then_inc(sem["b"], 1)
        elif piece == 3:
            dve.wait_ge(sem["bon_ps"], q + 1)
            if not first(q, 2):
                dve.wait_ge(sem["bv"], q - 1)
            dve.tensor_copy(bonus[u][:, :], k.ps[3][:, 0:2 * BLK]).then_inc(sem["bon"], 1)

    def prep_pool(pool, q, u, piece):
        if piece == 0:
            pool.wait_ge(sem["km1"], q + 1)
            pool.tensor_tensor(km[:, :], km[:, :], k_in, ALU.mult).then_inc(sem["km"], 1)
            pool.wait_ge(sem["scan"], q + 1)
            pool.tensor_tensor(w_in, cum[:, :], w_in, ALU.subtract).then_inc(sem["cump"], 1)
        elif piece == 2:
            pool.wait_ge(sem["exp"], q * 3 + 3)
            pool.wait_ge(sem["km"], q + 1)
            blocks = lambda t: t.rearrange("p (b t) -> p b t", t=P)
            ops = [(ar[u][:, :, 1, :], blocks(r_in), blocks(dec[:, :])),
                   (k_t[u][:, :], km[:, :], cum[:, :]),
                   (r_in, r_in, km[:, :]),
                   (ar[u][:, :, 0, :], blocks(kk[:, :]), blocks(w_in)),
                   (b_t[u][:, :], a_in, cum[:, :])]
            chunks = lambda t: t.rearrange("p (c t) -> p c t", t=CHUNK)
            end = chunks(dec[:, :])[:, :, CHUNK - 1:CHUNK].to_broadcast([P, 2 * BLK, CHUNK])
            ops += [(chunks(b_e[u][:, :]), chunks(b_t[u][:, :]), end), (chunks(k_e[u][:, :]), chunks(k_t[u][:, :]), end)]
            for n, (out, x0, x1) in enumerate(ops):
                if n == 2:
                    pool.wait_ge(sem["out"], q * 7 + 1)
                if n == 3:
                    pool.wait_ge(sem["b"], q + 1)
                if n == 5:
                    pool.wait_ge(sem["out"], q * 7 + 5)
                pool.tensor_tensor(out, x0, x1, ALU.mult).then_inc(sem["out"], 1)

    def prep_pe(pe, q, u, piece):
        if piece == 1:
            pe.wait_ge(sem["sq"], q + 1)
            if not first(q):
                pe.wait_ge(sem["bon"], q)
            for tt in range(BLK):
                last = pe.matmul(k.ps[3][:, 2 * tt:2 * tt + 2], dec[:, tt * P:(tt + 1) * P], heads2[:, :],
                                 start=True, stop=True)
            last.then_inc(sem["sum"], 1)
        elif piece == 2:
            pe.wait_ge(masks, 1)
            pe.wait_ge(sem["nroot"], q + 1)
            for tt in range(BLK):
                for h in range(2):
                    last = pe.matmul(k.ps[3][hs(h), tt * P:(tt + 1) * P],
                                     sm[:, 2, 2 * tt + h:2 * tt + h + 1].to_broadcast([P, 64]), k.ident[:, :],
                                     start=True, stop=True)
            last.then_inc(sem["bc"], 1)
        elif piece == 3:
            pe.wait_ge(sem["out"], q * 7 + 3)
            pe.wait_ge(sem["rkw"], q + 1)
            pe.wait_ge(sem["kk"], q + 1)
            for tt in range(BLK):
                last = pe.matmul(k.ps[3][:, 2 * tt:2 * tt + 2], r_in[:, tt * P:(tt + 1) * P], rkw[:, :],
                                 start=True, stop=True)
            last.then_inc(sem["bon_ps"], 1)


    def heads(t):
        return t.rearrange("p (g n) -> p g n", n=64)

    def flat(t):
        return t[:, :, :].rearrange("p b c -> p (b c)")

    def post_dve(dve, q, u, piece):
        if piece == 0:
            for x in range(2):
                dve.wait_ge(sem["y_sb"][x], q * 4 + 4)
            dve.tensor_reduce(sm[:, 3, :], heads(flat(y_n[u])), AX_X, ALU.add).then_inc(sem["s1"], 1)
            dve.wait_ge(sem["s1"], q + 1)
            dve.tensor_scalar(sm[:, 4, :], sm[:, 3, :], 1.0 / 64, None, ALU.mult).then_inc(sem["mean"], 1)
        elif piece == 1:
            dve.wait_ge(sem["ysq"], q + 1)
            dve.tensor_reduce(sm[:, 5, :], heads(tmp[:, :]), AX_X, ALU.add).then_inc(sem["s2"], 1)
            dve.wait_ge(sem["s2"], q + 1)
            dve.tensor_scalar(sm[:, 6, :], sm[:, 5, :], 1.0 / 64, GN_EPS, ALU.mult, ALU.add).then_inc(sem["var"], 1)
        elif piece == 2:
            dve.wait_ge(sem["vroot"], q + 1)
            dve.reciprocal(sm[:, 5, :], sm[:, 7, :]).then_inc(sem["vrec"], 1)
        elif piece == 3:
            dve.wait_ge(sem["tp"], q + 2)
            dve.wait_ge(sem["g"], q * 16 + 16)
            dve.scalar_tensor_tensor(out=g_in[:, :], in0=k.ps[3][:, :], scalar=col("b_gn_b", q), in1=g_in[:, :],
                                     op0=ALU.add, op1=ALU.mult).then_inc(sem["y"], 1)

    def post_act(act, q, u, piece):
        if piece == 1:
            act.wait_ge(sem["var"], q + 1)
            act.activation(sm[:, 7, :], sm[:, 6, :], ACT.Sqrt).then_inc(sem["vroot"], 1)

    def post_pool(pool, q, u, piece):
        wide = [P, 2 * BLK, 64]
        if piece == 0:
            pool.wait_ge(sem["mean"], q + 1)
            pool.tensor_tensor(heads(flat(y_n[u])), heads(flat(y_n[u])), sm[:, 4, :].unsqueeze(2).to_broadcast(wide),
                               ALU.subtract).then_inc(sem["yc"], 1)
            pool.wait_ge(sem["yc"], q + 1)
            pool.tensor_tensor(tmp[:, :], flat(y_n[u]), flat(y_n[u]), ALU.mult).then_inc(sem["ysq"], 1)
        elif piece == 1:
            pool.wait_ge(sem["vrec"], q + 1)
            pool.tensor_tensor(heads(flat(y_n[u])), heads(flat(y_n[u])), sm[:, 5, :].unsqueeze(2).to_broadcast(wide),
                               ALU.mult).then_inc(sem["yn"], 1)
            pool.wait_ge(sem["bon"], q + 1)
            pool.tensor_tensor(heads(tmp[:, :]), heads(flat(v_n[u])), bonus[u][:, :].unsqueeze(2).to_broadcast(wide),
                               ALU.mult).then_inc(sem["bv"], 1)
            pool.wait_ge(sem["yn"], q + 1)
            pool.wait_ge(gn_ld[u], (q - u) * 8 + 16)
            pool.tensor_tensor(y_n[u][:, :, :], y_n[u][:, :, :], gng[u][:, :].unsqueeze(1).to_broadcast([P, BLK, P]),
                               ALU.mult).then_inc(sem["gn"], 1)
            pool.wait_ge(sem["gn"], q + 1)
            pool.wait_ge(sem["bv"], q + 1)
            pool.tensor_tensor(flat(y_n[u]), flat(y_n[u]), tmp[:, :], ALU.add).then_inc(sem["z"], 1)

    def post_pe(pe, q, u, piece):
        if piece == 3:
            pe.wait_ge(sem["z"], q + 1)
            pe.wait_ge(sem["bon"], min(q + 3, PAIRS) if isinstance(q, int) else q + 3)
            for tt in range(BLK):
                last = pe.transpose(k.ps[3][:, tt * P:(tt + 1) * P], y_n[u][:, tt, :], k.ident[:, :])
            last.then_inc(sem["tp"], 1)

    def hs(h):
        return slice(64 * h, 64 * h + 64)

    LV = range(1, 6)

    def transposes_pe(pe, p, u, g):
        if g == 0:
            pe.wait_ge(v_ld[u], (p - u) * 8 + 16)
            pe.wait_ge(sem["out"], p * 7 + 7)
        for x in range(2):
            blk = 2 * g + x
            toks = slice(blk * P, (blk + 1) * P)
            for i, src in enumerate((ar[u][:, blk, 0, :], b_e[u][:, toks], k_e[u][:, toks], v_t[u][:, toks])):
                last = pe.transpose(bank(x)[:, i * P:(i + 1) * P], src, k.ident[:, :])
            last.then_inc(sem["t_ps"][x], 1)

    def group_pe(pe, p, u, g, between, following):
        n = p * 4 + g
        if g or not first(p):
            pe.wait_ge(sem["y_sb"][0], n)
            pe.wait_ge(sem["s_new"], n * 4)
        for x in range(2):
            blk = 2 * g + x
            toks = slice(blk * P, (blk + 1) * P)
            if x == 1:
                pe.wait_ge(sem["n_sb"][0], n * 2 + 2)
            for h in range(2):
                pe.matmul(bank(2 + h)[:, 0:P], ar[u][hs(h), blk, 0, :], b_t[u][hs(h), toks],
                          start=True, stop=True).then_inc(sem["g_ps"][x], 1)
            if x == 1:
                pe.wait_ge(sem["g_sb"][0], n * 2 + 2)
            elif g or not first(p):
                pe.wait_ge(sem["y_sb"][1], n)
            for h in range(2):
                out = bank(4 + h)
                rhs = ar[u][hs(h), blk, :, :].rearrange("p a t -> p (a t)")
                pe.matmul(out[:, 0:2 * P], b_t[u][hs(h), toks], rhs, start=True, stop=True)
                pe.matmul(out[:, 2 * P:4 * P], k_t[u][hs(h), toks], rhs, start=True, stop=True
                          ).then_inc(sem["g_ps"][x], 1)
        between()
        for x in range(2):
            if x == 0:
                for y in range(2):
                    pe.wait_ge(sem["g_sb"][y], n * 2 + 2)
                    pe.wait_ge(sem["t_sb"][y], n * 3 + 3)
            for h in range(2):
                last = pe.matmul(bank(4 + x)[:, hs(h)], gm[x][:, h, 2, :], v_n[u][:, 2 * g + x, hs(h)],
                                 start=True, stop=True)
            last.then_inc(sem["up_ps"][x], 1)
        for lv in LV:
            for x in range(2):
                if lv == 1:
                    pe.wait_ge(sem["n_sb"][1], n * 2 + 2)
                pe.wait_ge(sem["x_up"][x], n * 12 + (3 if lv == 1 else 2 * lv))
                for h in range(2):
                    last = pe.matmul(bank(x)[:, h * P:(h + 1) * P], n_t[x][:, h, :], xx[x][:, h, 0, :],
                                     start=True, stop=True)
                last.then_inc(sem["z_ps"][x], 1)
            for x in range(2):
                pe.wait_ge(sem["z_sb"][x], n * 5 + lv)
                if lv > 1:
                    pe.wait_ge(sem["x_up"][x], n * 12 + (2 * lv + 1))
                for h in range(2):
                    out = bank(2 + x)[:, h * 2 * P:(h + 1) * 2 * P]
                    last = pe.matmul(out[:, 0:P], xx[x][:, h, 1, :], z[x][:, h, :], start=True, stop=True)
                    if lv < LV[-1]:
                        last = pe.matmul(out[:, P:2 * P], z[x][:, h, :], xx[x][:, h, 1, :], start=True, stop=True)
                last.then_inc(sem["x_ps"][x], 1)
        for x in range(2):
            pe.wait_ge(sem["up_sb"][x], n + 1)
            pe.wait_ge(sem["x_up"][x], n * 12 + 12)
            for h in range(2):
                last = pe.matmul(bank(4 + x)[:, h * P:(h + 1) * P], xx[x][:, h, 0, :], au[x][:, h, :],
                                 start=True, stop=True)
            last.then_inc(sem["wu_ps"][x], 1)
        for x in range(2):
            pe.wait_ge(sem["wu_sb"][x], n + 1)
            for h in range(2):
                last = pe.matmul(bank(4 + x)[hs(h), 0:P], wu[x][:, 0, hs(h)], gm[x][:, h, 1, :], start=True, stop=True)
            last.then_inc(sem["q_ps"][x], 1)
            for c in range(2):
                if x == 0:
                    out = bank(c)
                else:
                    out = bank(3 + c)
                    if c == 1:
                        pe.wait_ge(sem["q_sb"][0], n + 1)
                rows = hs(c)
                pe.matmul(out[:, 0:P], wu[x][rows, 0, :], bk[x][rows, 0, :], start=True, stop=True)
                pe.matmul(out[:, P:2 * P], bk[x][rows, 0, :], wu[x][rows, 1, :], start=True, stop=False,
                          skip_group_check=True)
                pe.matmul(out[:, P:2 * P], bk[x][rows, 1, :], v_n[u][rows, 2 * g + x, :], start=False, stop=True,
                          skip_group_check=True).then_inc(sem["mg_ps"][x], 1)
            if x == 1:
                pe.wait_ge(sem["q_sb"][1], n + 1)
            y = bank(2) if x == 0 else bank(5)
            for h in range(2):
                pe.matmul(y[:, hs(h)], gm[x][:, h, 1, :], wu[x][:, 1, hs(h)], start=h == 0, stop=False,
                          skip_group_check=True)
                pe.matmul(y[:, hs(h)], gm[x][:, h, 3, :], v_n[u][:, 2 * g + x, hs(h)], start=False, stop=False,
                          skip_group_check=True)
        for x in range(2):
            pe.wait_ge(sem["q_sb"][x], n + 1)
            y = bank(2) if x == 0 else bank(5)
            for c in range(2):
                if x == c == 0 and g == 0:
                    pe.wait_ge(sem["zero"], p + 1)
                else:
                    pe.wait_ge(sem["s_new"], n * 4 + (2 * x + c))
                pe.wait_ge(sem["mg_sb"][x], n * 2 + (c + 1))
                out = bank(c if x == 0 else 3 + c)
                pe.matmul(out[:, 0:P], mg[x][c][:, 0, :], state[c][:, :], start=True, stop=True
                          ).then_inc(sem["s_ps"], 1)
                last = pe.matmul(y[hs(c), 0:P], q_t[x][:, hs(c)], state[c][:, :], start=False, stop=c == 1,
                                 skip_group_check=True)
                if x == 1 and c == 0 and following:
                    transposes_pe(pe, *following)
            last.then_inc(sem["y_ps"][x], 1)

    def group_act(act, p, u, g, between):
        n = p * 4 + g
        for x in range(2):
            blk = 2 * g + x
            act.wait_ge(sem["t_ps"][x], n + 1)
            if g or not first(p):
                act.wait_ge(sem["s_ps"], n * 4)
            if g == 0 and not first(p, 2):
                act.wait_ge(sem["tp"], p)
            act.activation(au[x][:, :, 0:64], bank(x)[:, 0:P].rearrange("p (h n) -> p h n", n=64), ACT.Copy
                           ).then_inc(sem["t_sb"][x], 1)
            act.activation(bk[x][:, :, :].rearrange("p i c -> p (i c)"), bank(x)[:, P:3 * P], ACT.Copy
                           ).then_inc(sem["t_sb"][x], 1)
            act.activation(v_n[u][:, blk, :], bank(x)[:, 3 * P:4 * P], ACT.Copy).then_inc(sem["t_sb"][x], 1)
            for h in range(2):
                act.wait_ge(sem["g_ps"][x], n * 4 + (1 + h))
                act.activation(n_t[x][:, h, :], bank(2 + h)[:, 0:P], ACT.Copy).then_inc(sem["n_sb"][x], 1)
        for x in range(2):
            act.wait_ge(sem["up_ps"][x], n + 1)
            act.activation(au[x][:, :, 64:P], bank(4 + x)[:, 0:P].rearrange("p (h n) -> p h n", n=64), ACT.Copy
                           ).then_inc(sem["up_sb"][x], 1)
        for lv in LV:
            for x in range(2):
                act.wait_ge(sem["z_ps"][x], n * 5 + lv)
                act.activation(z[x][:, :, :].rearrange("p h c -> p (h c)"), bank(x)[:, 0:2 * P], ACT.Copy
                               ).then_inc(sem["z_sb"][x], 1)
        for x in range(2):
            act.wait_ge(sem["wu_ps"][x], n + 1)
            act.activation(wu[x][:, :, :].rearrange("p w (h n) -> p w h n", n=64),
                           bank(4 + x)[:, 0:2 * P].rearrange("p (h w n) -> p w h n", h=2, w=2), ACT.Copy
                           ).then_inc(sem["wu_sb"][x], 1)
        between()
        for x in range(2):
            act.wait_ge(sem["y_ps"][x], n + 1)
            act.activation(y_n[u][:, 2 * g + x, :], (bank(2) if x == 0 else bank(5))[:, 0:P], ACT.Copy
                           ).then_inc(sem["y_sb"][x], 1)

    def group_dve(dve, p, u, g, between):
        n = p * 4 + g
        ident4 = k.ident[:, :].unsqueeze(1).to_broadcast([P, 4, P])

        def lmask(lv, part):
            return level[:, lv, part * P:(part + 1) * P].unsqueeze(1).to_broadcast([P, 2, P])

        for x in range(2):
            if g or not first(p):
                dve.wait_ge(sem["s_ps"], n * 4)
            for h in range(2):
                dve.wait_ge(sem["g_ps"][x], n * 4 + (3 + h))
                dve.tensor_tensor(gm[x][:, h, :, :].rearrange("p (j i) c -> p j i c", i=2),
                                  bank(4 + h).rearrange("p (j i c) -> p j i c", i=2, c=P),
                                  upper[:, :, :].unsqueeze(1).to_broadcast([P, 2, 2, P]), ALU.mult).then_inc(sem["g_sb"][x], 1)
            dve.wait_ge(sem["g_sb"][x], n * 2 + 2)
            dve.wait_ge(sem["n_sb"][x], n * 2 + 2)
            dve.tensor_copy(xx[x][:, :, :, :].rearrange("p h i c -> p (h i) c"), ident4).then_inc(sem["x_up"][x], 1)
            dve.wait_ge(sem["x_up"][x], n * 12 + 1)
            dve.sem_inc(sem["seen"], 1)
            dve.copy_predicated(xx[x][:, :, 0, :], lmask(0, 0), gm[x][:, :, 0, :]).then_inc(sem["x_up"][x], 1)
            dve.copy_predicated(xx[x][:, :, 1, :], lmask(0, 1), n_t[x][:, :, :]).then_inc(sem["x_up"][x], 1)
        between()
        for lv in LV:
            for x in range(2):
                dve.wait_ge(sem["x_ps"][x], n * 5 + lv)
                dve.sem_inc(sem["seen"], 1)
                new = bank(2 + x).rearrange("p (h i c) -> p h i c", h=2, i=2)
                for part in range(1 if lv == LV[-1] else 2):
                    dve.copy_predicated(xx[x][:, :, part, :], lmask(lv, part), new[:, :, part, :]
                                        ).then_inc(sem["x_up"][x], 1)
        for x in range(2):
            dve.wait_ge(sem["q_ps"][x], n + 1)
            dve.tensor_tensor(q_t[x][:, :], bank(4 + x)[:, 0:P], ar[u][:, 2 * g + x, 1, :], ALU.add
                              ).then_inc(sem["q_sb"][x], 1)
            for c in range(2):
                dve.wait_ge(sem["mg_ps"][x], n * 2 + (c + 1))
                out = bank(c) if x == 0 else bank(3 + c)
                dve.tensor_tensor(mg[x][c][:, :, :], out[:, 0:2 * P].rearrange("p (i c) -> p i c", c=P),
                                  diag[:, :].unsqueeze(1).to_broadcast([P, 2, P]), ALU.mult).then_inc(sem["mg_sb"][x], 1)
        if g == 0:
            if not first(p):
                dve.wait_ge(sem["s_new"], n * 4)
            dve.memset(state[0][:, :], 0.0).then_inc(sem["zero"], 1)
            dve.wait_ge(sem["zero"], p + 1)
        for x in range(2):
            for c in range(2):
                e = n * 4 + (2 * x + c)
                if not (x == c == 0 and g == 0):
                    dve.wait_ge(sem["s_new"], e)
                dve.wait_ge(sem["mg_sb"][x], n * 2 + (c + 1))
                if x == c == g == 0:
                    dve.wait_ge(sem["pend"], p + 1)
                blk = 2 * g + x
                dve.scalar_tensor_tensor(out=gp[:, :], in0=state[c][:, :], scalar=p_end[u][:, 2 * blk + c:2 * blk + c + 1],
                                         in1=mg[x][c][:, 1, :], op0=ALU.mult, op1=ALU.add).then_inc(sem["gp"], 1)
                dve.wait_ge(sem["gp"], e + 1)
                dve.wait_ge(sem["s_ps"], e + 1)
                dve.tensor_tensor(state[1 - c][:, :], gp[:, :], bank(c if x == 0 else 3 + c)[:, 0:P], ALU.add
                                  ).then_inc(sem["s_new"], 1)

    def pair(eng, p, u, group, prep, post, do_post=True, do_prep=True):
        for g in range(4):
            def between():
                if do_post and post is post_act:
                    post(eng, p - 1, 1 - u, g)
                if do_prep and prep:
                    prep(eng, p + 1, 1 - u, g)
                if do_post and post and post is not post_act:
                    post(eng, p - 1, 1 - u, g)
            if group is group_pe:
                group(eng, p, u, g, between, (p, u, g + 1) if g < 3 else (p + 1, 1 - u, 0) if do_prep else None)
            elif group:
                group(eng, p, u, g, between)
            else:
                between()

    def whole(eng, group, prep, post):
        if prep:
            for piece in range(4):
                prep(eng, 0, 0, piece)
        if group is group_pe:
            transposes_pe(eng, 0, 0, 0)
        pair(eng, 0, 0, group, prep, post, do_post=False)
        with eng.Fori(0, 3) as i:
            pair(eng, i * 2 + 1, 1, group, prep, post)
            pair(eng, i * 2 + 2, 0, group, prep, post)
        pair(eng, PAIRS - 1, 1, group, prep, post, do_prep=False)
        if post:
            for piece in range(4):
                post(eng, PAIRS - 1, 1, piece)

    def pe_all(pe):
        pe.sem_inc(sem["tp"], 1)
        pe.wait_ge(masks, 1)
        whole(pe, group_pe, prep_pe, post_pe)

    def act_all(act):
        whole(act, group_act, prep_act, post_act)

    def dve_all(dve):
        dve.wait_ge(masks, 1)
        dve.wait_ge(sem["omka"], 1)
        whole(dve, group_dve, prep_dve, post_dve)

    def pool_all(pool):
        whole(pool, None, prep_pool, post_pool)

    k.parts["sp"].append(sp_part)
    k.parts["pool"].append(pool_all)
    k.parts["dve"].append(dve_const)
    k.parts["pe"].append(pe_all)
    k.parts["act"].append(act_all)
    k.parts["dve"].append(dve_all)
    stage_end(k)
    y_back = [k.sem(f"rc_y_back{kt}") for kt in range(KT)]

    def act_back(act):
        act.wait_ge(sem["store"], 16 * PAIRS)
        for kt in range(KT):
            act.dma_start(y_t[:, kt, :], yscr[kt, :, :]).then_inc(y_back[kt], 16)

    k.parts["act"].append(act_back)
    lo_done = split_tiles(k, "rc_y", y_t, y_hi, y_lo, y_back)
    project_residual(k, "rc", a.b_w_o[0].rearrange("(k p) n -> p k n", p=P), y_hi, y_lo, lo_done, mod_col(1, 2))
    stage_end(k)
    consts.close()


def out_stage(k, a):
    nc = k.nc
    with ExitStack() as st:
        y = st.enter_context(nc.sbuf_tensor("y", [P, KT, S], F32))
        row = [st.enter_context(nc.sbuf_tensor(f"out_row{i}", [P, D], F32)) for i in range(2)]
        norm_stage(k, PCOL["norm_final"], plain=lambda kt: y[:, kt, :])
    n = k.norms - 1
    o_t = k.sem("o_t")
    o_copied = k.sem("o_copied")
    o_stored = [k.sem(f"o_stored{i}") for i in range(2)]

    def pe_part(pe):
        pe.wait_ge(k.nm["t"], KT * (n + 1))
        for tt in range(TT):
            if tt >= 2:
                pe.wait_ge(o_copied, tt - 1)
            for kt in range(KT):
                last = pe.transpose(k.ps[2 + tt % 2][:, kt * P:(kt + 1) * P], y[:, kt, tt * P:(tt + 1) * P],
                                    k.ident[:, :])
            last.then_inc(o_t, 1)

    def act_part(act):
        for tt in range(TT):
            act.wait_ge(o_t, tt + 1)
            if tt >= 2:
                act.wait_ge(o_stored[tt % 2], 16 * (tt // 2))
            act.activation(row[tt % 2][:, :], k.ps[2 + tt % 2][:, :], ACT.Copy).then_inc(o_copied, 1)

    def sp_part(sp):
        for tt in range(TT):
            sp.wait_ge(o_copied, tt + 1)
            sp.dma_start(a.out[0, tt * P:(tt + 1) * P, :], row[tt % 2][:, :]).then_inc(o_stored[tt % 2], 16)
        for i in range(2):
            sp.wait_ge(o_stored[i], 16 * (TT // 2))

    for name, part in (("pe", pe_part), ("act", act_part), ("sp", sp_part)):
        k.parts[name].append(part)


def build(nc, a, stages=("dsa", "ffn0", "rwkv", "ffn1")):
    k = Kern()
    k.nc = nc
    with ExitStack() as stack:
        alloc(k, stack)
        setup_stage(k, a)
        if "dsa" in stages:
            dsa_stage(k, a)
        if "ffn0" in stages:
            ffn_stage(k, a, 0)
        if "rwkv" in stages:
            rwkv_stage(k, a)
        if "ffn1" in stages:
            ffn_stage(k, a, 1)
        out_stage(k, a)
        block = stack.enter_context(nc.Block())

        @block.sync
        def _(eng):
            for part in k.parts["sp"]:
                part(eng)

        @block.gpsimd
        def _(eng):
            for part in k.parts["pool"]:
                part(eng)

        @block.tensor
        def _(eng):
            for part in k.parts["pe"]:
                part(eng)

        @block.scalar
        def _(eng):
            for part in k.parts["act"]:
                part(eng)

        @block.vector
        def _(eng):
            for part in k.parts["dve"]:
                part(eng)


_INS = ['x', 'c', 'ada_w', 'ada_b', 'norm_mix', 'norm_ffn', 'norm_final',
        'a_w_in', 'a_q_norm', 'a_kv_norm', 'a_kidx_g', 'a_kidx_b', 'a_w_uq', 'a_w_qi', 'a_w_uk', 'a_w_uv', 'a_w_o',
        'b_mu', 'b_w_r', 'b_w_k', 'b_w_v', 'b_w_o', 'b_w0', 'b_w1', 'b_w2', 'b_a0', 'b_a1', 'b_a2', 'b_g1', 'b_g2',
        'b_k_k', 'b_k_a', 'b_r_k', 'b_gn_g', 'b_gn_b', 'f_w_up', 'f_conv_w', 'f_conv_b', 'f_w_down']


Args = namedtuple("Args", _INS + ["out"])


def kernel(**inputs):
    import numpy as _np
    import concourse.bacc as _bacc
    from concourse import mybir as _mybir
    from concourse.bass_utils import run_bass_kernel_spmd as _run

    nc = _bacc.Bacc("TRN2", target_bir_lowering=False, num_devices=1)
    arrays, views = {}, {}
    for name in _INS:
        v = _np.ascontiguousarray(inputs[name])
        arrays[f"in_{name}_dram"] = v
        views[name] = nc.dram_tensor(f"in_{name}_dram", v.shape, _mybir.dt.from_np(v.dtype), kind="ExternalInput").ap()
    views["out"] = nc.dram_tensor("out_0_dram", (1, S, D), F32, kind="ExternalOutput").ap()
    build(nc, Args(**views))
    r = _run(nc, [arrays], core_ids=[0])
    return r.results[0]["out_0_dram"]
```
